# Optimizing a Trainium2 kernel written in Bass

```python
import jax, jax.numpy as jnp
from jax import lax
import numpy as np
import math

D_MODEL = 1024
BATCH = 1
SEQ = 512
DEPTH = 1

CHUNK = 64
LEFT_CHUNKS = 8
BAND = (LEFT_CHUNKS + 1) * CHUNK
ATT_HEADS = 8
ATT_HEAD_DIM = 64
ATT_WIDTH = ATT_HEADS * ATT_HEAD_DIM
MAX_REL = 128
LRU_WIDTH = D_MODEL
LRU_BLOCKS = 16
LRU_BLOCK = LRU_WIDTH // LRU_BLOCKS
CONV_WIDTH = 4
LRU_C = 8.0
D_FF = 2816
N_SUB = 3
EPS = 1e-6
PROJ_SIZES = (ATT_WIDTH, ATT_WIDTH, ATT_WIDTH, LRU_WIDTH, LRU_WIDTH, D_MODEL, D_MODEL)
PROJ_WIDTH = sum(PROJ_SIZES)


def rmsnorm(x, g):
    xf = x.astype(jnp.float32)
    y = xf * lax.rsqrt(jnp.mean(xf * xf, axis=-1, keepdims=True) + EPS)
    return (y * g.astype(jnp.float32)).astype(x.dtype)

def modulate(h, shift, scale):
    return h * (1 + scale[:, None, :]) + shift[:, None, :]

def swiglu(h, w_gu, w_down):
    g, u = jnp.split(h @ w_gu, 2, axis=-1)
    return (jax.nn.silu(g) * u) @ w_down

def chunked_attention(q, k, v, rel_bias):
    b, s, _ = q.shape
    nc = s // CHUNK
    q = q.reshape(b, nc, CHUNK, ATT_HEADS, ATT_HEAD_DIM)
    k = k.reshape(b, nc, CHUNK, ATT_HEADS, ATT_HEAD_DIM)
    v = v.reshape(b, nc, CHUNK, ATT_HEADS, ATT_HEAD_DIM)
    pad = ((0, 0), (LEFT_CHUNKS, 0), (0, 0), (0, 0), (0, 0))
    kp, vp = jnp.pad(k, pad), jnp.pad(v, pad)
    kb = jnp.concatenate([kp[:, j:j + nc] for j in range(LEFT_CHUNKS + 1)], axis=2)
    vb = jnp.concatenate([vp[:, j:j + nc] for j in range(LEFT_CHUNKS + 1)], axis=2)
    scores = jnp.einsum('bnqhd,bnkhd->bhnqk', q, kb).astype(jnp.float32) * (ATT_HEAD_DIM ** -0.5)
    qi = jnp.arange(CHUNK)[:, None]
    kj = jnp.arange(BAND)[None, :]
    rel = jnp.clip(qi - kj + LEFT_CHUNKS * CHUNK, -MAX_REL, MAX_REL) + MAX_REL
    bias = rel_bias.astype(jnp.float32)[:, rel]
    scores = scores + bias[None, :, None, :, :]
    valid = (jnp.arange(nc)[:, None] - LEFT_CHUNKS + jnp.arange(BAND)[None, :] // CHUNK) >= 0
    scores = jnp.where(valid[None, None, :, None, :], scores, jnp.finfo(jnp.float32).min)
    p = jax.nn.softmax(scores, axis=-1).astype(v.dtype)
    out = jnp.einsum('bhnqk,bnkhd->bnqhd', p, vb)
    return out.reshape(b, s, ATT_WIDTH)

def causal_depthwise_conv(x, w, bias):
    rhs = w[:, None, :]
    y = lax.conv_general_dilated(x, rhs, window_strides=(1,), padding=[(CONV_WIDTH - 1, 0)],
                                 dimension_numbers=('NWC', 'WIO', 'NWC'),
                                 feature_group_count=x.shape[-1])
    return y + bias

def block_diag_linear(x, w, bias):
    b, s, _ = x.shape
    xb = x.reshape(b, s, LRU_BLOCKS, LRU_BLOCK)
    return jnp.einsum('bsnk,nkj->bsnj', xb, w).reshape(b, s, LRU_WIDTH) + bias

def rg_lru(x, w_a, b_a, w_x, b_x, lam):
    r = jax.nn.sigmoid(block_diag_linear(x, w_a, b_a).astype(jnp.float32))
    i = jax.nn.sigmoid(block_diag_linear(x, w_x, b_x).astype(jnp.float32))
    log_a = -LRU_C * r * jax.nn.softplus(-lam.astype(jnp.float32))
    a = jnp.exp(log_a)
    mult = jnp.sqrt(-jnp.expm1(2.0 * log_a))
    u = mult * (i * x.astype(jnp.float32))

    def combine(left, right):
        a1, b1 = left
        a2, b2 = right
        return a1 * a2, a2 * b1 + b2

    _, h = lax.associative_scan(combine, (a, u), axis=1)
    return h.astype(x.dtype)

def mixer(h, w_in, rel_bias, conv_w, conv_b, lru_wa, lru_ba, lru_wx, lru_bx, lru_lambda,
          w_att_o, w_rec_o, w_out):
    proj = h @ w_in
    idx = [int(v) for v in np.cumsum(PROJ_SIZES)[:-1]]
    q, k, v, xr, yr, g_att, g_rec = jnp.split(proj, idx, axis=-1)
    att = chunked_attention(q, k, v, rel_bias) @ w_att_o
    xr = causal_depthwise_conv(xr, conv_w, conv_b)
    rec = (rg_lru(xr, lru_wa, lru_ba, lru_wx, lru_bx, lru_lambda) * jax.nn.gelu(yr)) @ w_rec_o
    merged = jax.nn.sigmoid(g_att) * att + jax.nn.sigmoid(g_rec) * rec
    return merged @ w_out

def sandwich(x, fn, g_pre, g_post, shift, scale, gate, res_w):
    h = modulate(rmsnorm(x, g_pre), shift, scale)
    y = rmsnorm(fn(h), g_post)
    return x + res_w * gate[:, None, :] * y

def first_inputs(seed: int = 0) -> dict:
    key = jax.random.key(seed)
    ks = jax.random.split(key, 24)
    L, D, F, W = DEPTH, D_MODEL, D_FF, LRU_WIDTH
    nrm = lambda k, shape, fan_in: jax.random.normal(k, shape, jnp.float32) * (fan_in ** -0.5)
    u = jax.random.uniform(ks[20], (L, W), jnp.float32, 0.9, 0.999)
    p = u ** (1.0 / LRU_C)
    lam = jnp.log(p) - jnp.log1p(-p)
    return {
        "x": jax.random.normal(ks[0], (BATCH, SEQ, D), jnp.float32),
        "c": jax.random.normal(ks[1], (BATCH, D), jnp.float32),
        "w_ada": nrm(ks[2], (L, D, N_SUB * 3 * D), D) * 0.5,
        "b_ada": 0.02 * jax.random.normal(ks[3], (L, N_SUB * 3 * D), jnp.float32),
        "norm_pre": 1.0 + 0.05 * jax.random.normal(ks[4], (L, N_SUB, D), jnp.float32),
        "norm_post": 1.0 + 0.05 * jax.random.normal(ks[5], (L, N_SUB, D), jnp.float32),
        "ffn1_w_gu": nrm(ks[6], (L, D, 2 * F), D),
        "ffn1_w_down": nrm(ks[7], (L, F, D), F),
        "w_in": nrm(ks[8], (L, D, PROJ_WIDTH), D),
        "rel_bias": 0.5 * jax.random.normal(ks[9], (L, ATT_HEADS, 2 * MAX_REL + 1), jnp.float32),
        "conv_w": nrm(ks[10], (L, CONV_WIDTH, W), CONV_WIDTH),
        "conv_b": 0.02 * jax.random.normal(ks[11], (L, W), jnp.float32),
        "lru_wa": nrm(ks[12], (L, LRU_BLOCKS, LRU_BLOCK, LRU_BLOCK), LRU_BLOCK),
        "lru_ba": 0.02 * jax.random.normal(ks[13], (L, W), jnp.float32),
        "lru_wx": nrm(ks[14], (L, LRU_BLOCKS, LRU_BLOCK, LRU_BLOCK), LRU_BLOCK),
        "lru_bx": 0.02 * jax.random.normal(ks[15], (L, W), jnp.float32),
        "lru_lambda": lam,
        "w_att_o": nrm(ks[16], (L, ATT_WIDTH, D), ATT_WIDTH),
        "w_rec_o": nrm(ks[17], (L, W, D), W),
        "w_out": nrm(ks[18], (L, D, D), D),
        "ffn2_w_gu": nrm(ks[19], (L, D, 2 * F), D),
        "ffn2_w_down": nrm(ks[21], (L, F, D), F),
    }

def first_block(x, c, w_ada, b_ada, norm_pre, norm_post, ffn1_w_gu, ffn1_w_down, w_in, rel_bias,
              conv_w, conv_b, lru_wa, lru_ba, lru_wx, lru_bx, lru_lambda, w_att_o, w_rec_o,
              w_out, ffn2_w_gu, ffn2_w_down):
    b = x.shape[0]
    c_act = jax.nn.silu(c)
    for l in range(DEPTH):
        mod = (c_act @ w_ada[l] + b_ada[l]).reshape(b, N_SUB, 3, D_MODEL)
        ffn1 = lambda h: swiglu(h, ffn1_w_gu[l], ffn1_w_down[l])
        mix = lambda h: mixer(h, w_in[l], rel_bias[l], conv_w[l], conv_b[l], lru_wa[l], lru_ba[l],
                              lru_wx[l], lru_bx[l], lru_lambda[l], w_att_o[l], w_rec_o[l], w_out[l])
        ffn2 = lambda h: swiglu(h, ffn2_w_gu[l], ffn2_w_down[l])
        x = sandwich(x, ffn1, norm_pre[l, 0], norm_post[l, 0], mod[:, 0, 0], mod[:, 0, 1], mod[:, 0, 2], 0.5)
        x = sandwich(x, mix, norm_pre[l, 1], norm_post[l, 1], mod[:, 1, 0], mod[:, 1, 1], mod[:, 1, 2], 1.0)
        x = sandwich(x, ffn2, norm_pre[l, 2], norm_post[l, 2], mod[:, 2, 0], mod[:, 2, 1], mod[:, 2, 2], 0.5)
    return x


DEPTH_2 = 2

GRID_W = 64
CTX_LEN = 256
HEAD_DIM = 64
ROPE_FREQS = HEAD_DIM // 4
ROPE_THETA = 10000.0
Q_BLOCK = 128
ATTN_SCALE = HEAD_DIM ** -0.5

FOURIER_GROUP_DIM = 64
FOURIER_GROUPS = (3 * D_MODEL // 8) // FOURIER_GROUP_DIM
FOURIER_WIDTH = FOURIER_GROUPS * FOURIER_GROUP_DIM
DIFF_HEADS = D_MODEL // 256
DIFF_QK_WIDTH = DIFF_HEADS * 2 * HEAD_DIM
DIFF_V_DIM = 2 * HEAD_DIM
DIFF_V_WIDTH = DIFF_HEADS * DIFF_V_DIM
GQA_Q_HEADS = D_MODEL // 128
GQA_GROUP = 4
GQA_KV_HEADS = GQA_Q_HEADS // GQA_GROUP
GQA_Q_WIDTH = GQA_Q_HEADS * HEAD_DIM
GQA_KV_WIDTH = GQA_KV_HEADS * HEAD_DIM
CONV_WIDTH_2 = 3 * D_MODEL // 8
CONV_KERNEL = 31
N_BRANCHES = 4
D_FF_2 = 4 * D_MODEL
N_MOD = 6

KV_SIZES = (DIFF_QK_WIDTH, DIFF_V_WIDTH, GQA_KV_WIDTH, GQA_KV_WIDTH)
REST_SIZES = (FOURIER_WIDTH, DIFF_QK_WIDTH, GQA_Q_WIDTH, 2 * CONV_WIDTH_2, N_BRANCHES * D_MODEL)
KV_COLS = sum(KV_SIZES)
IN_COLS = KV_COLS + sum(REST_SIZES)


def _split(t, sizes):
    idx = np.cumsum(sizes)[:-1].tolist()
    return jnp.split(t, idx, axis=-1)

def _rms_norm(x, g):
    xf = x.astype(jnp.float32)
    y = xf * lax.rsqrt(jnp.mean(xf * xf, axis=-1, keepdims=True) + EPS)
    return (y * g.astype(jnp.float32)).astype(x.dtype)

def _layer_norm(x, g, b):
    xf = x.astype(jnp.float32)
    mu = jnp.mean(xf, axis=-1, keepdims=True)
    var = jnp.mean(jnp.square(xf - mu), axis=-1, keepdims=True)
    y = (xf - mu) * lax.rsqrt(var + EPS) * g.astype(jnp.float32) + b.astype(jnp.float32)
    return y.astype(x.dtype)

def _modulate(x, g, shift, scale):
    return _rms_norm(x, g) * (1 + scale) + shift

def _axial_rope_tables(seq_len):
    rows = seq_len // GRID_W
    row = jnp.repeat(jnp.arange(rows, dtype=jnp.float32), GRID_W)
    col = jnp.tile(jnp.arange(GRID_W, dtype=jnp.float32), rows)
    inv_freq = ROPE_THETA ** (-jnp.arange(ROPE_FREQS, dtype=jnp.float32) / ROPE_FREQS)
    ang = jnp.stack([row[:, None] * inv_freq, col[:, None] * inv_freq], axis=1)
    return jnp.cos(ang), jnp.sin(ang)

def _apply_rope(x, cos, sin):
    xf = x.astype(jnp.float32).reshape(x.shape[:-1] + (2, 2, ROPE_FREQS))
    bshape = (cos.shape[0],) + (1,) * (x.ndim - 3) + cos.shape[1:]
    cs, sn = cos.reshape(bshape), sin.reshape(bshape)
    re, im = xf[..., 0, :], xf[..., 1, :]
    out = jnp.stack([re * cs - im * sn, im * cs + re * sn], axis=-2)
    return out.reshape(x.shape).astype(x.dtype)

def _kv_heads(kv, k_norm):
    b, l = kv.shape[:2]
    dk, dv, gk, gv = _split(kv, KV_SIZES)
    dk = dk.reshape(b, l, DIFF_HEADS, 2, HEAD_DIM)
    dv = dv.reshape(b, l, DIFF_HEADS, DIFF_V_DIM)
    gk = _rms_norm(gk.reshape(b, l, GQA_KV_HEADS, HEAD_DIM), k_norm)
    gv = gv.reshape(b, l, GQA_KV_HEADS, HEAD_DIM)
    return dk, dv, gk, gv

def _diff_attention(dq, dk, dv, lam):
    s = jnp.einsum('bqhjd,bkhjd->bhjqk', dq, dk).astype(jnp.float32) * ATTN_SCALE
    p = jax.nn.softmax(s, axis=-1)
    a = (p[:, :, 0] - lam * p[:, :, 1]).astype(dv.dtype)
    return jnp.einsum('bhqk,bkhe->bqhe', a, dv)

def _gqa_attention(gq, gk, gv):
    s = jnp.einsum('bqhgd,bkhd->bhgqk', gq, gk).astype(jnp.float32) * ATTN_SCALE
    p = jax.nn.softmax(s, axis=-1).astype(gv.dtype)
    return jnp.einsum('bhgqk,bkhd->bqhgd', p, gv)

def _sweep_query_blocks(fn, qs):
    b, l = qs[0].shape[:2]
    n = l // Q_BLOCK
    def to_blocks(q):
        return jnp.moveaxis(q.reshape((b, n, Q_BLOCK) + q.shape[2:]), 1, 0)
    out = lax.map(lambda qb: fn(*qb), tuple(to_blocks(q) for q in qs))
    def from_blocks(o):
        return jnp.moveaxis(o, 0, 1).reshape((b, l) + o.shape[3:])
    return jax.tree_util.tree_map(from_blocks, out)

def _fourier_mix(u):
    b, l = u.shape[:2]
    ug = u.astype(jnp.float32).reshape(b, l, FOURIER_GROUPS, FOURIER_GROUP_DIM)
    y = jnp.fft.fft2(ug, axes=(1, 3), norm='ortho').real
    return y.reshape(b, l, FOURIER_WIDTH).astype(u.dtype)

def _conformer_conv(u, dw, dw_bias, ln_g, ln_b):
    a, g = jnp.split(u, 2, axis=-1)
    v = a * jax.nn.sigmoid(g)
    y = lax.conv_general_dilated(
        v, dw[:, None, :], window_strides=(1,),
        padding=[(CONV_KERNEL // 2, CONV_KERNEL // 2)],
        dimension_numbers=('NWC', 'WIO', 'NWC'),
        feature_group_count=CONV_WIDTH_2) + dw_bias
    return jax.nn.silu(_layer_norm(y, ln_g, ln_b))

def _token_mixer(h, kv_ctx, rope, lp, lam, lam_init):
    b, l = h.shape[:2]
    w_in = lp['w_in']
    if rope is None:
        rest = h @ w_in[:, KV_COLS:]
        dk, dv, gk, gv = kv_ctx
    else:
        proj = h @ w_in
        dk, dv, gk, gv = _kv_heads(proj[..., :KV_COLS], lp['k_norm'])
        rest = proj[..., KV_COLS:]
    u_f, dq, gq, u_c, gate_logits = _split(rest, REST_SIZES)
    dq = dq.reshape(b, l, DIFF_HEADS, 2, HEAD_DIM)
    gq = _rms_norm(gq.reshape(b, l, GQA_KV_HEADS, GQA_GROUP, HEAD_DIM), lp['q_norm'])
    if rope is None:
        o_d = _diff_attention(dq, dk, dv, lam)
        o_g = _gqa_attention(gq, gk, gv)
    else:
        cos, sin = rope
        dq, dk = _apply_rope(dq, cos, sin), _apply_rope(dk, cos, sin)
        gq, gk = _apply_rope(gq, cos, sin), _apply_rope(gk, cos, sin)
        cdk, cdv, cgk, cgv = kv_ctx
        dk_all = jnp.concatenate([dk, cdk], axis=1)
        dv_all = jnp.concatenate([dv, cdv], axis=1)
        gk_all = jnp.concatenate([gk, cgk], axis=1)
        gv_all = jnp.concatenate([gv, cgv], axis=1)
        o_d, o_g = _sweep_query_blocks(
            lambda qd, qg: (_diff_attention(qd, dk_all, dv_all, lam), _gqa_attention(qg, gk_all, gv_all)),
            (dq, gq))
    o_d = (_rms_norm(o_d, lp['subln']) * (1.0 - lam_init)).reshape(b, l, DIFF_V_WIDTH)
    o_g = o_g.reshape(b, l, GQA_Q_WIDTH)
    y_f = _fourier_mix(u_f)
    y_c = _conformer_conv(u_c, lp['conv_dw'], lp['conv_dw_bias'], lp['conv_ln_g'], lp['conv_ln_b'])
    g_f, g_d, g_g, g_c = jnp.split(jax.nn.sigmoid(gate_logits), N_BRANCHES, axis=-1)
    merged = (g_f * (y_f @ lp['w_br_fourier']) + g_d * (o_d @ lp['w_br_diff'])
              + g_g * (o_g @ lp['w_br_gqa']) + g_c * (y_c @ lp['w_br_conv']))
    return merged @ lp['w_out']

def _sq_relu_mlp(h, w1, w2):
    return jnp.square(jax.nn.relu(h @ w1)) @ w2

def second_inputs(seed: int = 0) -> dict:
    key = jax.random.key(seed)
    ks = jax.random.split(key, 32)
    f32 = jnp.float32
    def nrm(k, shape, scale):
        return jax.random.normal(k, shape, f32) * scale
    def gain(k, shape):
        return 1.0 + 0.02 * jax.random.normal(k, shape, f32)
    D = D_MODEL
    return {
        "x": nrm(ks[0], (BATCH, SEQ, D), 1.0),
        "c": nrm(ks[1], (BATCH, D), 1.0),
        "ctx": nrm(ks[2], (BATCH, CTX_LEN, D), 1.0),
        "c_ctx": nrm(ks[3], (D,), 1.0),
        "w_mod": nrm(ks[4], (DEPTH_2, D, N_MOD * D), 0.5 * D ** -0.5),
        "b_mod": nrm(ks[5], (DEPTH_2, N_MOD * D), 0.01),
        "g_pre_mix": gain(ks[6], (DEPTH_2, D)),
        "g_post_mix": gain(ks[7], (DEPTH_2, D)),
        "g_pre_mlp": gain(ks[8], (DEPTH_2, D)),
        "g_post_mlp": gain(ks[9], (DEPTH_2, D)),
        "w_in": nrm(ks[10], (DEPTH_2, D, IN_COLS), D ** -0.5),
        "q_norm": gain(ks[11], (DEPTH_2, HEAD_DIM)),
        "k_norm": gain(ks[12], (DEPTH_2, HEAD_DIM)),
        "diff_lambda": nrm(ks[13], (DEPTH_2, 4, HEAD_DIM), 0.1),
        "diff_subln": gain(ks[14], (DEPTH_2, DIFF_V_DIM)),
        "conv_dw": nrm(ks[15], (DEPTH_2, CONV_KERNEL, CONV_WIDTH_2), CONV_KERNEL ** -0.5),
        "conv_dw_bias": nrm(ks[16], (DEPTH_2, CONV_WIDTH_2), 0.01),
        "conv_ln_g": gain(ks[17], (DEPTH_2, CONV_WIDTH_2)),
        "conv_ln_b": nrm(ks[18], (DEPTH_2, CONV_WIDTH_2), 0.01),
        "w_br_fourier": nrm(ks[19], (DEPTH_2, FOURIER_WIDTH, D), FOURIER_WIDTH ** -0.5),
        "w_br_diff": nrm(ks[20], (DEPTH_2, DIFF_V_WIDTH, D), DIFF_V_WIDTH ** -0.5),
        "w_br_gqa": nrm(ks[21], (DEPTH_2, GQA_Q_WIDTH, D), GQA_Q_WIDTH ** -0.5),
        "w_br_conv": nrm(ks[22], (DEPTH_2, CONV_WIDTH_2, D), CONV_WIDTH_2 ** -0.5),
        "w_out": nrm(ks[23], (DEPTH_2, D, D), D ** -0.5),
        "w_ff1": nrm(ks[24], (DEPTH_2, D, D_FF_2), D ** -0.5),
        "w_ff2": nrm(ks[25], (DEPTH_2, D_FF_2, D), D_FF_2 ** -0.5),
    }

def second_block(x, c, ctx, c_ctx, w_mod, b_mod, g_pre_mix, g_post_mix, g_pre_mlp, g_post_mlp,
              w_in, q_norm, k_norm, diff_lambda, diff_subln, conv_dw, conv_dw_bias, conv_ln_g, conv_ln_b,
              w_br_fourier, w_br_diff, w_br_gqa, w_br_conv, w_out, w_ff1, w_ff2):
    rope = _axial_rope_tables(x.shape[1])
    xc = ctx
    for l in range(DEPTH_2):
        lp = {
            'w_in': w_in[l], 'q_norm': q_norm[l], 'k_norm': k_norm[l], 'subln': diff_subln[l],
            'conv_dw': conv_dw[l], 'conv_dw_bias': conv_dw_bias[l],
            'conv_ln_g': conv_ln_g[l], 'conv_ln_b': conv_ln_b[l],
            'w_br_fourier': w_br_fourier[l], 'w_br_diff': w_br_diff[l],
            'w_br_gqa': w_br_gqa[l], 'w_br_conv': w_br_conv[l], 'w_out': w_out[l],
        }
        lam_init = 0.8 - 0.6 * math.exp(-0.3 * l)
        lv = diff_lambda[l].astype(jnp.float32)
        lam = jnp.exp(jnp.sum(lv[0] * lv[1])) - jnp.exp(jnp.sum(lv[2] * lv[3])) + lam_init

        mod_x = (jax.nn.silu(c) @ w_mod[l] + b_mod[l])[:, None, :]
        mod_c = (jax.nn.silu(c_ctx) @ w_mod[l] + b_mod[l])[None, None, :]
        sx1, cx1, gx1, sx2, cx2, gx2 = jnp.split(mod_x, N_MOD, axis=-1)
        sc1, cc1, gc1, sc2, cc2, gc2 = jnp.split(mod_c, N_MOD, axis=-1)

        hc = _modulate(xc, g_pre_mix[l], sc1, cc1)
        kv_ctx = _kv_heads(hc @ w_in[l][:, :KV_COLS], k_norm[l])

        h = _modulate(x, g_pre_mix[l], sx1, cx1)
        x = x + gx1 * _rms_norm(_token_mixer(h, kv_ctx, rope, lp, lam, lam_init), g_post_mix[l])
        hm = _modulate(x, g_pre_mlp[l], sx2, cx2)
        x = x + gx2 * _rms_norm(_sq_relu_mlp(hm, w_ff1[l], w_ff2[l]), g_post_mlp[l])

        if l < DEPTH_2 - 1:
            xc = xc + gc1 * _rms_norm(_token_mixer(hc, kv_ctx, None, lp, lam, lam_init), g_post_mix[l])
            hcm = _modulate(xc, g_pre_mlp[l], sc2, cc2)
            xc = xc + gc2 * _rms_norm(_sq_relu_mlp(hcm, w_ff1[l], w_ff2[l]), g_post_mlp[l])
    return x


def setup_inputs(seed=0):
    out = dict(first_inputs(seed))
    for name, value in second_inputs(seed + 1).items():
        if name != "x":
            out[name + "_2"] = value
    return out


def reference(
    x, c, w_ada, b_ada, norm_pre, norm_post, ffn1_w_gu, ffn1_w_down, w_in, rel_bias, conv_w,
    conv_b, lru_wa, lru_ba, lru_wx, lru_bx, lru_lambda, w_att_o, w_rec_o, w_out, ffn2_w_gu,
    ffn2_w_down, c_2, ctx_2, c_ctx_2, w_mod_2, b_mod_2, g_pre_mix_2, g_post_mix_2, g_pre_mlp_2,
    g_post_mlp_2, w_in_2, q_norm_2, k_norm_2, diff_lambda_2, diff_subln_2, conv_dw_2,
    conv_dw_bias_2, conv_ln_g_2, conv_ln_b_2, w_br_fourier_2, w_br_diff_2, w_br_gqa_2,
    w_br_conv_2, w_out_2, w_ff1_2, w_ff2_2,
):
    x = first_block(
        x, c, w_ada, b_ada, norm_pre, norm_post, ffn1_w_gu, ffn1_w_down, w_in, rel_bias, conv_w,
        conv_b, lru_wa, lru_ba, lru_wx, lru_bx, lru_lambda, w_att_o, w_rec_o, w_out, ffn2_w_gu,
        ffn2_w_down,
    )
    return second_block(
        x, c_2, ctx_2, c_ctx_2, w_mod_2, b_mod_2, g_pre_mix_2, g_post_mix_2, g_pre_mlp_2,
        g_post_mlp_2, w_in_2, q_norm_2, k_norm_2, diff_lambda_2, diff_subln_2, conv_dw_2,
        conv_dw_bias_2, conv_ln_g_2, conv_ln_b_2, w_br_fourier_2, w_br_diff_2, w_br_gqa_2,
        w_br_conv_2, w_out_2, w_ff1_2, w_ff2_2,
    )


_drawn_inputs = setup_inputs


def setup_inputs(seed=0):
    import zlib

    import numpy as np

    out = dict(_drawn_inputs(seed))
    spreads = {}
    factors = {'norm_post': 3.062,
     'conv_b': 3.051,
     'lru_ba': 8.0,
     'lru_bx': 8.0,
     'b_mod_2': 2.752,
     'g_pre_mix_2': 7.346,
     'g_post_mix_2': 7.45,
     'g_pre_mlp_2': 6.726,
     'g_post_mlp_2': 7.8,
     'q_norm_2': 8.0,
     'k_norm_2': 8.0,
     'diff_lambda_2': 3.195,
     'diff_subln_2': 8.0,
     'conv_dw_bias_2': 8.0,
     'conv_ln_g_2': 8.0,
     'conv_ln_b_2': 25.245}
    for name, (base, spread) in spreads.items():
        noise = np.random.default_rng([zlib.crc32(name.encode()), seed]).standard_normal(out[name].shape)
        drawn = base * np.exp(spread * noise) if base else spread * noise
        out[name] = __import__('jax').numpy.asarray(drawn.astype(out[name].dtype))
    for name, factor in factors.items():
        out[name] = (out[name] * factor).astype(out[name].dtype)
    return out
```

```python
from contextlib import ExitStack, contextmanager
import math

import numpy as np
import concourse.bass as bass
from concourse import mybir

F32 = mybir.dt.float32
F32R = mybir.dt.float32r
ACT = mybir.ActivationFunctionType
ALU = mybir.AluOpType
AX = mybir.AxisListType

P = 128
D = 1024
KD = D // P
L = 512
LC = 256
TT = L + LC
FF1 = 2816
FF2 = 4096
CW = 256
EPS = 1e-6
PANEL = 2048
NM1 = 36
NM2 = 24
HEADS = 8
SCALE = 64 ** -0.5
GELU_C = math.sqrt(2.0 / math.pi)


def tiles_of(w, rows, cols):
    part = w[rows, :][:, cols] if not isinstance(cols, slice) else w[rows, cols]
    kt = part.shape[0] // P
    return part.reshape(kt, P, part.shape[1]).transpose(1, 0, 2).reshape(P, -1)


def full(flat):
    if flat.shape[1] == PANEL:
        return flat
    out = np.zeros((P, PANEL), np.float32)
    out[:, :flat.shape[1]] = flat
    return out


def up_gu(w, c, n):
    g = slice(c * CW + n * P, c * CW + (n + 1) * P)
    u = slice(FF1 + c * CW + n * P, FF1 + c * CW + (n + 1) * P)
    a = tiles_of(w, slice(0, D), g).reshape(P, KD, P)
    b = tiles_of(w, slice(0, D), u).reshape(P, KD, P)
    return np.concatenate([a, b], axis=2).reshape(P, PANEL)


def cols_panels(w, c0, c1):
    return [full(tiles_of(w, slice(0, D), slice(c, min(c + CW, c1)))) for c in range(c0, c1, CW)]


def rows_panels(w, c0, c1):
    return [full(tiles_of(w, slice(0, w.shape[0]), slice(c, c + 512))) for c in range(c0, c1, 512)]


def ffn_panels(wgu, wd):
    n = FF1 // CW
    up = [[up_gu(wgu, c, 0), up_gu(wgu, c, 1)] for c in range(n)]
    down = [tiles_of(wd, slice(c * CW, (c + 1) * CW), slice(0, D)) for c in range(n)]
    out = list(up[0])
    for c in range(1, n):
        out += up[c] + [down[c - 1]]
    return out + [down[n - 1]]


def mlp_panels(w1, w2):
    n = FF2 // CW
    out = cols_panels(w1, 0, CW)
    for c in range(1, n):
        out += cols_panels(w1, c * CW, (c + 1) * CW) + [tiles_of(w2, slice((c - 1) * CW, c * CW), slice(0, D))]
    return out + [tiles_of(w2, slice(FF2 - CW, FF2), slice(0, D))]


def dft_panels(n):
    a = 2 * np.pi * (np.outer(np.arange(n), np.arange(n)) % n) / n
    m = (np.concatenate([np.cos(a), -np.sin(a)], axis=1) / math.sqrt(64 * n)).astype(np.float32)
    return [full(tiles_of(m, slice(r, r + 2 * P), slice(0, 2 * n))) for r in range(0, n, 2 * P)]


PAIRED = np.concatenate([np.arange(64) + 64 * (4 * kv + g) for g in range(4) for kv in range(2)])


def mix2_panels(v, l):
    w = v["w_in_2"][l]

    def merge(gate0, wb):
        out = []
        for j in range(2):
            out += cols_panels(w, gate0 + 512 * j, gate0 + 512 * (j + 1)) + rows_panels(wb, 512 * j, 512 * (j + 1))
        return out

    ps = cols_panels(w, 0, 1024) + cols_panels(w, 1664, 2176) + merge(4480, v["w_br_diff_2"][l])
    ps += cols_panels(w, 1024, 1280) + cols_panels(w[:, 2176:2688][:, PAIRED], 0, 512)
    ps += merge(5504, v["w_br_gqa_2"][l][PAIRED, :])
    ps += cols_panels(w, 1280, 1664) + dft_panels(L) + (dft_panels(LC) if l == 0 else [])
    ps += merge(3456, v["w_br_fourier_2"][l])
    for n in range(3):
        ps += cols_panels(np.concatenate([w[:, 2688 + n * P:2688 + (n + 1) * P], w[:, 3072 + n * P:3072 + (n + 1) * P]], axis=1), 0, CW)
    return ps + merge(6528, v["w_br_conv_2"][l]) + cols_panels(v["w_out_2"][l], 0, D)


BAND = np.minimum(2 * P + np.arange(P)[:, None] - np.arange(2 * P)[None, :], 2 * P)


def rope_tables():
    t = np.arange(L)
    inv = (np.float32(10000.0) ** (-np.arange(16, dtype=np.float32) / np.float32(16))).astype(np.float32)
    ang = [np.outer(inv, p.astype(np.float32)) for p in (t // 64, t % 64)]
    cos = np.concatenate([np.cos(a) for a in ang for _ in range(2)])
    sin = np.concatenate([s * np.sin(a) for a in ang for s in (-1, 1)])
    return np.stack([np.tile(cos, (2, 1)), np.tile(sin, (2, 1))], axis=1)


def block_diagonal(w):
    out = np.zeros((P, KD, P), np.float32)
    for b in range(16):
        out[64 * (b % 2):64 * (b % 2) + 64, b // 2, 64 * (b % 2):64 * (b % 2) + 64] = w[b]
    return out


def columns(v):
    return np.asarray(v).reshape(-1, P).T


class Counts:

    def __init__(self, nc, ctx, known):
        self.nc, self.ctx, self.known = nc, ctx, known
        self.sems, self.count, self.labels, self.inside = {}, {}, {}, None

    def sem(self, kind):
        if kind not in self.sems:
            self.sems[kind] = self.ctx.enter_context(self.nc.semaphore("sm_" + kind))
            self.count[kind] = 0
        return self.sems[kind]

    def up(self, kind, key=None, by=1):
        s = self.sem(kind)
        self.count[kind] += by
        if key is not None:
            self.name(kind, key, kind, self.count[kind])
        return s, by

    def name(self, kind, key, sem_kind, value):
        assert (kind, key) not in self.labels, (kind, key)
        self.labels[(kind, key)] = (sem_kind, value)

    def start(self, kind, stage):
        self.sem(kind)
        self.name(kind, ("start", stage), kind, self.count[kind])

    def at(self, kind, key, plus=0):
        if self.known is None:
            return self.sem(kind), 1
        sem_kind, v = self.known[(kind, key)]
        out = v + plus
        assert not isinstance(out, int) or out > 0, (kind, key, plus)
        return self.sem(sem_kind), out

    @contextmanager
    def loop(self, eng, n):
        before = dict(self.count)
        with eng.Fori(0, n) as i:
            yield i
        for k, v in self.count.items():
            self.count[k] = v + (v - before.get(k, 0)) * (n - 1)


PAR_SIZES = [("b_ada", 72), ("b_mod", 96), ("norm_pre", 24), ("norm_post", 24), ("conv_w", 32), ("conv_b", 8),
             ("lru_ba", 8), ("lru_bx", 8), ("lru_lambda", 8), ("g_pre_mix", 16), ("g_post_mix", 16),
             ("g_pre_mlp", 16), ("g_post_mlp", 16), ("q_norm", 2), ("k_norm", 2), ("subln", 2), ("conv_dw", 186),
             ("conv_dw_b", 6), ("ln_g", 6), ("ln_b", 6), ("rb_far", 8), ("cond", 24)]
PAR = {n: sum(m for _, m in PAR_SIZES[:i]) for i, (n, _) in enumerate(PAR_SIZES)}
NPAR = sum(m for _, m in PAR_SIZES)
CST_SIZES = [("ident", 128), ("block", 128), ("dft64", 256)]
CST = {n: sum(m for _, m in CST_SIZES[:i]) for i, (n, _) in enumerate(CST_SIZES)}
NCST = sum(m for _, m in CST_SIZES)

N_FFN = 3 * (FF1 // CW)
N_MLP = 2 * (FF2 // CW)


class Mlp:

    def __init__(self, name, gated, T, first, mod0, mods):
        self.name, self.gated, self.T, self.p0, self.mod0 = name, gated, T, first, mod0
        self.C = (FF1 if gated else FF2) // CW
        self.UP = 2 if gated else 1
        self.H = 1 if T <= 512 else 2
        self.O = KD * self.H
        self.trips = (self.C - 1) // 2
        self.rest = self.C - 1 - 2 * self.trips
        self.before, self.within, self.after = mods
        self.mod_end = mod0 + self.before + self.within * self.trips + self.after
        self.per_trip = 2 * (self.UP + 1)


class Rows:

    def __init__(self, tag, T):
        self.tag, self.rows, self.units = tag, [], []
        for t in range(4):
            for half in ((None,) if tag == "d" else (0, 1)):
                for g in range(1 if T <= L else 2):
                    self.units.append((t, half, g))
                    for i in (range(4) if g == 0 else range(4, 6)):
                        js = (0, 1) if half is None else (half,)
                        self.rows.append((len(self.units) - 1, i, js, 0 if g == 0 else L, TT))

    def __len__(self):
        return len(self.rows)

    def __getitem__(self, r):
        n, i, js, k0, k1 = self.rows[r]
        return self.units[n], i, js, k0, k1

    def unit(self, n):
        return self.units[n]

    def unit_no(self, r):
        return self.rows[r][0]

    def unit_start(self, r):
        return r == 0 or self.rows[r - 1][0] != self.rows[r][0]

    def unit_end(self, r):
        return r == len(self.rows) - 1 or self.rows[r + 1][0] != self.rows[r][0]

    def slot(self, j):
        return j if self.tag == "d" else 0

    def bank(self, r, j):
        return 2 * (j if self.tag == "d" else r % 2)

    def last_row_with(self, n, j):
        found = [r for r in range(len(self.rows)) if self.rows[r][0] < n and j in self.rows[r][2]]
        return found[-1] if found else None

    def last_unit_of(self, t):
        return max(n for n, u in enumerate(self.units) if u[0] == t)

    def query_event(self, X, t, g):
        q = "dq" if self.tag == "d" else "gq"
        if g == 1 and self.tag == "d":
            return "ctx_kept", X(q, t)
        return "roped", X(q, t)


def program(nc, ctx, io, C, first, n_panels, stop):
    sem, up, at, known = C.sem, C.up, C.at, C.known

    def sb(name, shape, dt=F32, stack=ctx):
        return stack.enter_context(nc.sbuf_tensor("b_" + name, [P] + shape, dt))

    raw = sb("raw", [2, PANEL])
    whi = sb("whi", [2, PANEL], F32R)
    wlo = sb("wlo", [2, PANEL], F32R)
    x = sb("x", [KD, TT])
    hhi = sb("hhi", [KD, TT], F32R)
    hlo = sb("hlo", [KD, TT], F32R)
    par = sb("par", [NPAR])
    cst = sb("cst", [NCST])
    ones = sb("ones", [P])
    mods = sb("mods", [2 * (NM1 + 2 * NM2), 2])
    csil = sb("csil", [3, KD])
    vec = sb("vec", [2, 4, KD])
    rstd = sb("rstd", [TT])
    small = sb("small", [96])
    arena = ExitStack()
    with arena as s:
        y = sb("y", [KD, TT], F32, s)
        with ExitStack() as s2:
            tmp = sb("tmp", [2, TT], F32, s2)
            dhi = sb("dhi", [2, 2, TT], F32R, s2)
            dlo = sb("dlo", [2, 2, TT], F32R, s2)
            mraw = sb("mraw", [2, PANEL], F32, s2)
            macc = sb("macc", [2, 2, CW], F32, s2)
        with ExitStack() as s2:
            sq = sb("sq", [2, TT], F32, s2)
            tn = sb("tn", [2, TT], F32, s2)
            hf = sb("hf", [2, TT], F32, s2)
        with ExitStack() as s2:
            xpad = sb("xpad", [2, L + 4], F32, s2)
            xc = sb("xc", [2, L], F32, s2)
            ga = sb("ga", [2, L], F32, s2)
            gx = sb("gx", [2, L], F32, s2)
            gm = sb("gm", [2, L], F32, s2)
            gy = sb("gy", [2, L], F32, s2)
            hs = sb("hs", [2, L], F32, s2)
            wbd = sb("wbd", [2, KD, P], F32, s2)
        with ExitStack() as s2:
            qf = sb("qf", [4, L], F32, s2)
            kf = sb("kf", [4, L], F32, s2)
            pr = sb("pr", [2, 4, L], F32, s2)
            pt = sb("pt", [4, L], F32, s2)
            qm = sb("qm", [2, L], F32, s2)
            bias = sb("bias", [2, 2 * P], F32, s2)
        with ExitStack() as s2:
            bhi = sb("bhi", [KD, L], F32R, s2)
            blo = sb("blo", [KD, L], F32R, s2)
            gate = sb("gate", [4, L], F32, s2)
    with ExitStack() as s:
        dk = sb("dk", [4, TT], F32, s)
        dv = sb("dv", [6, 512], F32, s)
        with ExitStack() as s2:
            qm2 = sb("qm2", [2, L], F32, s2)
            pr2 = sb("pr2", [2, 2, TT], F32, s2)
            gv = sb("gv", [6, P], F32, s2)
            rope = sb("rope", [2, L], F32, s2)
        with ExitStack() as s2:
            ch = sb("ch", [4, TT], F32R, s2)
            cl = sb("cl", [4, TT], F32R, s2)
            with ExitStack() as s3:
                aq = sb("aq", [4, TT], F32, s3)
                pt2 = sb("pt2", [6, L], F32, s3)
                gk = sb("gk", [1, TT], F32, s3)
            with ExitStack() as s3:
                sb("under_gate2", [4, TT], F32, s3)
                gate2 = sb("gate2", [4, TT], F32, s3)
            with ExitStack() as s3:
                uf = sb("uf", [3, TT], F32, s3)
                fh = sb("fh", [2, TT], F32R, s3)
                fl = sb("fl", [2, TT], F32R, s3)
            with ExitStack() as s3:
                vp = sb("vp", [3, TT + 60], F32, s3)
                cv = sb("cv", [3, TT], F32, s3)
                sg = sb("sg", [2, TT], F32, s3)
                mean = sb("mean", [TT], F32, s3)
        with ExitStack() as s2:
            mh = sb("mh", [KD, TT], F32R, s2)
            ml = sb("ml", [KD, TT], F32R, s2)

    ps = ctx.enter_context(nc.psum_tensor("ps", [P, 8, 512], F32))

    def const(name):
        return cst[:, CST[name]:CST[name] + dict(CST_SIZES)[name]]

    def pcol(name, j, n=1):
        return par[:, PAR[name] + j:PAR[name] + j + n]

    def spans(T):
        return [(0, L), (L, TT)][:1 if T <= L else 2]

    def wide(bank, T):
        return ps[:, bank:bank + len(spans(T)), :].rearrange("p a n -> p (a n)")[:, 0:T]

    def lin(a, b, i):
        return a if i is None else i * b + a

    raw_loaded = [sem("raw_loaded0"), sem("raw_loaded1")]
    mod_loaded = [sem("mod_loaded0"), sem("mod_loaded1")]
    hi_ready, lo_ready, panel_used = sem("hi_ready"), sem("lo_ready"), sem("panel_used")
    mod_read, mod_used = sem("mod_read"), sem("mod_used")
    setup = sem("setup")
    N_SETUP = 5

    first = {**{n: 10 ** 6 for n in ("mix1", "ffn2", "mix2", "mlp1", "mix3", "mlp2")}, **first}
    MLPS = {"ffn1": Mlp("ffn1", True, L, first["ffn1"], 8, (4, 4, 4)),
            "ffn2": Mlp("ffn2", True, L, first["ffn2"], 36, (2, 4, 2)),
            "mlp1": Mlp("mlp1", False, TT, first["mlp1"], 60, (4, 2, 6)),
            "mlp2": Mlp("mlp2", False, L, first["mlp2"], 84, (0, 0, 0))}

    LAYER, TOKENS = {"mix2": 0, "mix3": 1}, {"mix2": TT, "mix3": L}
    BRANCHES = ("d", "g", "f", "c")
    DFT_PANELS = [(0, 1, 2), (0, 1)]
    DV_BANK, GV_BANK = [4, 5, 6, 7, 4, 5], [2, 3, 4, 5, 2, 3]
    GQ_BANK = [2, 4, 0, 2]
    ROWS = lambda st, tag: Rows(tag, TOKENS[st])
    LAST_UNIT = {(st, tag): len(ROWS(st, tag).units) - 1 for st in LAYER for tag in "dg"}
    ROW_COL = lambda r, j: 72 + 8 * (r % 2) + j

    l0, l1 = 2 * NM1, 2 * (NM1 + NM2)
    NORMS = {
        "n0": (None, (L, 0, 8, ("norm_pre", 0))),
        "n1": ((L, 16, 0.5, ("norm_post", 0)), (L, 24, 32, ("norm_pre", 8))),
        "n2": ((L, 40, 1.0, ("norm_post", 8)), (L, 48, 56, ("norm_pre", 16))),
        "n3": ((L, 64, 0.5, ("norm_post", 16)), (TT, l0, l0 + 8, ("g_pre_mix", 0))),
        "n4": ((TT, l0 + 16, 1.0, ("g_post_mix", 0)), (TT, l0 + 24, l0 + 32, ("g_pre_mlp", 0))),
        "n5": ((TT, l0 + 40, 1.0, ("g_post_mlp", 0)), (TT, l1, l1 + 8, ("g_pre_mix", 8))),
        "n6": ((L, l1 + 16, 1.0, ("g_post_mix", 8)), (L, l1 + 24, l1 + 32, ("g_pre_mlp", 8))),
        "n7": ((L, l1 + 40, 1.0, ("g_post_mlp", 8)), None),
    }
    SUM_BANK = {"post": 0, "pre": 2}
    MOD_NEED = {"n0": (0, 16, 8), "n1": (16, 72, 36), "n3": (72, 120, 60), "n5": (120, 168, 84)}
    GROUPS = [(0, L), (L, TT)]

    def groups(T):
        return [g for g in enumerate(GROUPS) if g[1][1] <= T]

    ORDER = ["n0", "ffn1", "n1", "mix1", "n2", "ffn2", "n3", "mix2", "n4", "mlp1", "n5", "mix3", "n6", "mlp2", "n7"][:stop]
    LAST_NORM = [s for s in ORDER if s in NORMS][-1]

    block = ctx.enter_context(nc.Block())

    @block.sync
    def _(sp):
        sp.dma_start(par[:, :], io["par"]).then_inc(setup, 16)
        sp.dma_start(raw[:, 0, :], io["panels"][0]).then_inc(raw_loaded[0], 16)
        sp.dma_start(x[:, :, 0:L], io["xT"].rearrange("(k p) t -> p k t", p=P)).then_inc(setup, 16)
        sp.dma_start(raw[:, 1, :], io["panels"][1]).then_inc(raw_loaded[1], 16)
        sp.dma_start(cst[:, :], io["cst"]).then_inc(setup, 16)
        with sp.Fori(1, n_panels // 2) as i:
            for s in range(2):
                sp.wait_ge(lo_ready, i * 2 + (s - 1))
                sp.dma_start(raw[:, s, :], io["panels"][i * 2 + s]).then_inc(raw_loaded[s], 16)
        for k in range(KD):
            sp.wait_ge(*at("x_new", (LAST_NORM, k)))
            sp.dma_start(io["outT"][k * P:(k + 1) * P, :], x[:, k, 0:L]).then_inc(sem("stored"), 16)
        sp.wait_ge(sem("stored"), 16 * KD)

    @block.gpsimd
    def _(pool):
        with pool.Fori(0, n_panels // 2) as i:
            for s in range(2):
                pool.wait_ge(hi_ready, i * 2 + (s + 1))
                pool.tensor_tensor(wlo[:, s, :], raw[:, s, :], whi[:, s, :].bitcast(F32), ALU.subtract).then_inc(lo_ready, 1)

    @block.scalar
    def _(act):
        def split(p, i=None, by=0):
            if p >= n_panels:
                return
            act.wait_ge(raw_loaded[p % 2], lin(16 * (p // 2 + 1), 8 * by, i))
            if p >= 2:
                act.wait_ge(panel_used, lin(p - 1, by, i))
            act.activation(whi[:, p % 2, :], raw[:, p % 2, :], ACT.Copy).then_inc(hi_ready, 1)

        def mod_load(k, i=None, by=0):
            if k >= 2:
                act.wait_ge(mod_read, lin(k - 1, by, i))
            act.dma_start(mraw[:, k % 2, :], io["mod_panels"][lin(k, by, i)]).then_inc(mod_loaded[k % 2], 16)

        def squares(st, what, src, T):
            for k in range(KD):
                act.wait_ge(*at("src", (st, what, k)))
                if (st, what, k) == ("n3", "pre", 0):
                    act.wait_ge(*at("ctx_loaded", "all"))
                if k >= 2:
                    act.wait_ge(*at("sq_used", (st, what, k - 2)))
                act.activation(sq[:, k % 2, 0:T], src[:, k, 0:T], ACT.Square).then_inc(*up("sq", (st, what, k)))

        def root(st, what, T):
            act.wait_ge(*at("ms", (st, what)))
            act.activation(rstd[:, 0:T], rstd[:, 0:T], ACT.Sqrt).then_inc(*up("root", (st, what)))

        def norm(st):
            post, pre = NORMS[st]
            if post:
                squares(st, "post", y, post[0])
                root(st, "post", post[0])
            if pre:
                T = pre[0]
                squares(st, "pre", x, T)
                root(st, "pre", T)
                v = vec[:, int(st[1]) % 2, :, :]
                for k in range(KD + 1):
                    if k < KD:
                        act.wait_ge(*at("normed", (st, k)))
                        if k >= 2:
                            act.wait_ge(*at("h_lo", (st, k - 2)))
                        for g, (a, b) in groups(T):
                            act.activation(hf[:, k % 2, a:b], tn[:, k % 2, a:b], ACT.Identity,
                                           bias=mods[:, pre[1] + k, g:g + 1],
                                           scale=v[:, 2 + g, k:k + 1]).then_inc(*up("hf", (st, k, g)))
                    if k >= 1:
                        act.wait_ge(*at("hf", (st, k - 1, groups(T)[-1][0])))
                        act.activation(hhi[:, k - 1, 0:T], hf[:, (k - 1) % 2, 0:T], ACT.Copy)\
                           .then_inc(*up("h_hi", (st, k - 1)))

        def mlp(m):
            st, T = m.name, m.T
            for kind in ("acted", "hid_hi"):
                C.start(kind, st)

            def units(c, p, i=None):
                for n in range(2):
                    if m.gated or n == 0:
                        split(p + n + 1, i, m.per_trip)
                    if m.gated or n == 1:
                        act.wait_ge(panel_used, lin(p + (n if m.gated else 0) + 1, m.per_trip, i))
                    else:
                        act.wait_ge(*at("up_first", ("start", st), lin(c + 1, 2, i)))
                    if c >= 1:
                        act.wait_ge(*at("hid_lo", ("start", st), lin(2 * (c - 1) + n + 1, 4, i)))
                    if m.gated:
                        act.activation(tmp[:, n, 0:T], ps[:, 2 * n, 0:T], ACT.Silu).then_inc(*up("acted"))
                    else:
                        act.activation(tmp[:, n, 0:T], wide(2 * n, T), ACT.Relu).then_inc(*up("acted"))
                    act.wait_ge(*at("hid", ("start", st), lin(2 * c + n + 1, 4, i)))
                    if c >= 2:
                        act.wait_ge(panel_used, lin(down_panel(m, c - 2) + 1, m.per_trip, i))
                    elif i is not None:
                        act.wait_ge(panel_used, lin(p, m.per_trip, i))
                    act.activation(dhi[:, c % 2, n, 0:T], tmp[:, n, 0:T], ACT.Copy).then_inc(*up("hid_hi"))

            k = m.mod0
            if m.before:
                mod_load(k)
                mod_load(k + 1)
            units(0, m.p0)
            for u in range(m.before):
                mod_load(k + u + 2)
            k += m.before
            with C.loop(act, m.trips) as i:
                for u in range(2):
                    p = m.p0 + m.UP + u * (m.UP + 1)
                    units(1 + u, p, i)
                    split(p + m.UP + 1, i, m.per_trip)
                    for v in range(m.within // 2):
                        mod_load(k + u * (m.within // 2) + v + 2, i, m.within)
            k += m.within * m.trips
            for u in range(m.rest):
                p = m.p0 + m.UP + m.trips * m.per_trip
                units(2 * m.trips + 1, p)
                split(p + m.UP + 1)
            for u in range(m.after):
                if k + u + 2 < m.mod_end:
                    mod_load(k + u + 2)
            split(m.p0 + m.UP * m.C + m.C)

        mod_load(0)
        mod_load(1)
        split(0)
        act.wait_ge(setup, 16 * 3)
        act.activation(csil[:, :, :].rearrange("p a k -> p (a k)"), pcol("cond", 0, 24), ACT.Silu).then_inc(*up("csil", "all"))
        for k in range(2, 8):
            mod_load(k)

        def mix1():
            p0 = first["mix1"]
            act.wait_ge(*at("h_lo", ("n1", KD - 1)))
            act.dma_start(wbd[:, :, :, :].rearrange("p a k n -> p (a k n)"),
                          io["wbd"].rearrange("p a k n -> p (a k n)")).then_inc(*up("wbd", "all", 16))
            act.wait_ge(*at("lam", "abs"))
            act.activation(small[:, 24:32], small[:, 16:24], ACT.Exp, scale=-1.0).then_inc(*up("lam_exp", "all"))
            for r in range(4):
                p = p0 + 2 * r
                split(p + 1)
                for n in range(2):
                    act.wait_ge(*at("out", (p, n)))
                    if r == 0:
                        act.wait_ge(*at("xpad", n))
                    else:
                        act.wait_ge(*at("xc", (r - 1, n)))
                    act.activation(xpad[:, n, 3:3 + L], ps[:, n, :], ACT.Copy).then_inc(*up("xcopy", (r, n)))
                split(p + 2)
                for n in range(2):
                    act.wait_ge(*at("out", (p + 1, n)))
                    if r >= 1:
                        act.wait_ge(*at("rec", (r - 1, n)))
                    act.activation(gy[:, n, :], ps[:, 2 + n, :], ACT.Gelu_apprx_tanh).then_inc(*up("gelu", (r, n)))
                for n in range(2):
                    j = 2 * r + n
                    act.wait_ge(*at("gates", (r, n)))
                    act.activation(ga[:, n, :], ps[:, 4 + n, :], ACT.Sigmoid, bias=pcol("lru_ba", j)).then_inc(*up("ga", (r, n)))
                    act.activation(gx[:, n, :], ps[:, 6 + n, :], ACT.Sigmoid, bias=pcol("lru_bx", j)).then_inc(*up("gx", (r, n)))
                for n in range(2):
                    act.wait_ge(*at("exponent", (r, n)))
                    act.activation(gm[:, n, :], ga[:, n, :], ACT.Tanh).then_inc(*up("tanh", (r, n)))
                    act.wait_ge(*at("tanh", (r, n)))
                    act.activation(ga[:, n, :], ga[:, n, :], ACT.Exp, scale=-1.0).then_inc(*up("decay", (r, n)))
                for n in range(2):
                    act.wait_ge(*at("one_less_a2", (r, n)))
                    act.activation(gm[:, n, :], gm[:, n, :], ACT.Sqrt).then_inc(*up("mult", (r, n)))
            p = p0 + 8
            act.wait_ge(*at("rec", (3, 1)))
            for a in range(2):
                split(p + a + 1)
                for n in range(2):
                    act.wait_ge(*at("out", (p + a, n)))
                    act.activation(qf[:, 2 * a + n, :], ps[:, 2 * a + n, :], ACT.Copy).then_inc(*up("q", 2 * a + n))
            split(p + 3)
            split(p + 4)
            for a in range(2):
                split(p + 5 + a)
                for t in range(4):
                    act.wait_ge(*at("out", (p + 4 + a, t)))
                    act.activation(x[:, 2 * t + a, L:TT], ps[:, t + 4 * a, 0:CW], ACT.Copy).then_inc(*up("v", (a, t)))

            def load_bias(h):
                if h >= 2:
                    act.wait_ge(*at("biased", (h - 2, 3)))
                act.dma_start(bias[:, h % 2, :], io["bias_band"][h]).then_inc(*up(f"bias{h % 2}", h, 16))

            def exps(u):
                for i in range(4):
                    act.wait_ge(*at("max", (u, i)))
                    s = pr[:, u % 2, i, 0:(i + 1) * P]
                    act.activation(s, s, ACT.Exp, bias=small[:, 32 + 4 * (u % 2) + i:33 + 4 * (u % 2) + i],
                                   accum_out=small[:, 40 + 4 * (u % 2) + i:41 + 4 * (u % 2) + i]).then_inc(*up("exp", (u, i)))

            def keep_transposed(u):
                for j in range(4):
                    act.wait_ge(*at("tr", (u, j)))
                    if u >= 1:
                        act.wait_ge(*at("pv", u - 1))
                    act.activation(pt[:, j, j * P:L], ps[:, 4 * (u % 2) + j, j * P:L], ACT.Copy).then_inc(*up("pt", (u, j)))

            load_bias(0)
            load_bias(1)
            exps(0)
            exps(1)
            for u in range(HEADS):
                if u + 2 < HEADS:
                    load_bias(u + 2)
                keep_transposed(u)
                if u + 2 < HEADS:
                    exps(u + 2)
            act.wait_ge(*at("pv", HEADS - 1))
            act.dma_start(x[:, :, L:TT], io["ctxT"].rearrange("(k p) t -> p k t", p=P)).then_inc(*up("ctx_loaded", "all", 16))
            for k in range(KD):
                act.activation(bhi[:, k, :], y[:, k, 0:L], ACT.Copy).then_inc(*up("bhi", ("rec", k)))
            for j in range(2):
                p = p0 + 14 + 7 * j
                for b, q in (("a", p), ("r", p + 3)):
                    for a in range(2):
                        split(q + a + 1)
                        for n in range(2):
                            t = 2 * a + n
                            act.wait_ge(*at("out", (q + a, n)))
                            prev = ("a" if b == "r" else "r", j if b == "r" else j - 1)
                            if prev[1] >= 0:
                                act.wait_ge(*at("merged", (prev[1], prev[0], t)))
                            act.activation(gate[:, t, :], ps[:, t, :], ACT.Sigmoid).then_inc(*up("gate", (j, b, t)))
                    split(q + 3)
                    if b == "r":
                        split(q + 4)
            p = p0 + 28
            act.wait_ge(panel_used, p)
            for k in range(KD):
                act.wait_ge(*at("merged", (k // 4, "r", k % 4)))
                act.activation(bhi[:, k, :], y[:, k, 0:L], ACT.Copy).then_inc(*up("bhi", ("out", k)))
            for a in range(4):
                split(p + a + 1)
                for n in range(2):
                    k = 2 * a + n
                    act.wait_ge(*at("out", (p + a, n)))
                    act.activation(y[:, k, 0:L], ps[:, k % 4, :], ACT.Copy).then_inc(*up("src", ("n2", "post", k)))

        def mix2(st):
            X = lambda *k: (st,) + k
            l, T, p0 = LAYER[st], TOKENS[st], first[st]
            norm_before = "n3" if l == 0 else "n5"
            panel = [p0]

            def next_split():
                panel[0] += 1
                split(panel[0])

            def keep_hi(tag, nt, dst, src):
                for k in range(nt):
                    act.wait_ge(*at("ready", X(tag, k)))
                    act.activation(dst[:, k, 0:T], src(k), ACT.Copy).then_inc(*up("c_hi", X(tag, k)))

            def gates(tag):
                for j in range(2):
                    for a in range(2):
                        next_split()
                        for n in range(2):
                            t = 2 * a + n
                            act.wait_ge(*at("out", (panel[0] - 1, n)))
                            if (tag, j) != ("d", 0):
                                act.wait_ge(*at("gated", X(*((tag, 0) if j else (BRANCHES[BRANCHES.index(tag) - 1], 1)), t)))
                            if (tag, j, t) == ("c", 0, 0):
                                act.wait_ge(*at("c_lo", X("c", 2)))
                            act.activation(gate2[:, t, 0:T], wide(2 * t % 4, T), ACT.Sigmoid).then_inc(*up("gate", X(tag, j, t)))
                    next_split()

            def row_exps(rows, r):
                u, i, js, k0, k1 = rows[r]
                for j in js:
                    c = ROW_COL(r, j)
                    act.wait_ge(*at("nmax", X(rows.tag, r)))
                    act.wait_ge(*at("scores", X(rows.tag, r, j)))
                    if r >= 2:
                        act.wait_ge(*at("tr", X(rows.tag, r - 2)))
                    b = rows.bank(r, j)
                    s = ps[:, b:b + 2, :].rearrange("p a n -> p (a n)")[:, k0:k1] if k0 == 0 else ps[:, b, 0:k1 - k0]
                    act.activation(pr2[:, r % 2, rows.slot(j), 0:k1 - k0], s, ACT.Exp, bias=small[:, c:c + 1], scale=SCALE,
                                   accum_out=small[:, c + 4:c + 5]).then_inc(*up("exp", X(rows.tag, r, j)))

            def attention(rows):
                row_exps(rows, 0)
                for r in range(len(rows)):
                    if r + 1 < len(rows):
                        row_exps(rows, r + 1)
                    u, i, js, k0, k1 = rows[r]
                    act.wait_ge(*at("tr", X(rows.tag, r)))
                    if rows.unit_start(r) and rows.unit_no(r) >= 1:
                        act.wait_ge(*at("pv", X(rows.tag, rows.unit_no(r) - 1)))
                    n = (k1 - k0) // P
                    q0 = (i % 4) * P
                    src = ps[:, 4:6, :].rearrange("p a n -> p (a n)")[:, 0:k1 - k0].rearrange("p (k q) -> p k q", q=P)
                    act.activation(pt2[:, 0:n, q0:q0 + P], src, ACT.Copy).then_inc(*up("pt", X(rows.tag, r)))
                    if rows.unit_end(r):
                        uno = rows.unit_no(r)
                        t, half, g = u
                        o = slice(0, P) if half is None else slice(64 * half, 64 * half + 64)
                        a, b = GROUPS[g]
                        act.wait_ge(*at("pv", X(rows.tag, uno)))
                        act.wait_ge(*at("qm", X(rows.tag, uno)))
                        act.activation(aq[o, t, a:b], ps[o, 6 + uno % 2, 0:b - a], ACT.Copy).then_inc(*up("kept", X(rows.tag, uno)))

            def head_norm(tag, src, T, source, free):
                head_squares(tag, src, T, source, free)
                head_root(tag, T)

            def head_squares(tag, src, T, source, free):
                act.wait_ge(*at(*source))
                act.wait_ge(*at(*free))
                act.activation(pr2[:, 0, 0, 0:T], src, ACT.Square).then_inc(*up("hsq", X(tag)))

            def head_root(tag, T):
                act.wait_ge(*at("hms", X(tag)))
                act.activation(rstd[:, 0:T], rstd[:, 0:T], ACT.Sqrt).then_inc(*up("hroot", X(tag)))

            act.wait_ge(*at("h_lo", (norm_before, KD - 1)))
            act.dma_start(rope[:, :, :], io["rope"]).then_inc(*up("rope", st, 16))
            act.dma_start(pr2[:, 0, 0, 0:256], io["lv"][:, l, :]).then_inc(*up("lv", st, 16))
            act.wait_ge(*at("lv_sums", st))
            act.activation(small[:, 66:68], small[:, 64:66], ACT.Exp).then_inc(*up("lv_exp", st))
            for a in range(2):
                next_split()
                for n in range(2):
                    act.wait_ge(*at("out", (panel[0] - 1, n)))
                    act.wait_ge(*at("roped", X("dk", 2 * a + n)))
                    act.activation(dk[:, 2 * a + n, L:TT], ps[:, 2 * (2 * a + n) % 4 + 1, 0:LC], ACT.Copy)\
                       .then_inc(*up("ctx_kept", X("dk", 2 * a + n)))
            for a in range(2):
                next_split()
                for t in range(6):
                    act.wait_ge(*at("out", (panel[0] - 1, t)))
                    act.activation(dv[:, t, a * CW:(a + 1) * CW], ps[:, DV_BANK[t], 0:CW], ACT.Copy).then_inc(*up("dv", X(a, t)))
            for a in range(2):
                next_split()
                for n in range(2 if T > L else 0):
                    act.wait_ge(*at("roped", X("dq", 2 * a + n)))
                    act.activation(aq[:, 2 * a + n, L:TT], ps[:, 2 * (2 * a + n) % 4 + 1, 0:LC], ACT.Copy)\
                       .then_inc(*up("ctx_kept", X("dq", 2 * a + n)))
            rows = ROWS(st, "d")
            attention(rows)
            for t in range(4):
                head_norm(("sub", t), aq[:, t, 0:T], T, ("kept", X("d", rows.last_unit_of(t))),
                          ("hsum", X(("sub", t - 1))) if t else ("tr", X("d", len(rows) - 1)))
            keep_hi("d", 4, ch, lambda k: aq[:, k, 0:T])
            gates("d")
            act.wait_ge(*at("out", (p0 + 11, 3)))
            act.dma_start(rope[:, :, :], io["rope"]).then_inc(*up("rope2", st, 16))
            next_split()
            head_squares(("gk", 0), wide(0, TT), TT, ("out", (panel[0] - 1, 0)), ("out", (p0 + 11, 3)))
            for t in range(6):
                act.wait_ge(*at("out", (panel[0] - 1, 1 + t)))
                act.activation(gv[:, t, :], ps[:, GV_BANK[t], 0:P], ACT.Copy).then_inc(*up("gv", X(t)))
            head_root(("gk", 0), TT)
            for a in range(2):
                next_split()
                for n in range(2):
                    t = 2 * a + n
                    head_norm(("gq", t), wide(GQ_BANK[t], T), T, ("out", (panel[0] - 1, n)),
                              ("hsum", X(("gq", t - 1) if t else ("gk", 0))))
            rows = ROWS(st, "g")
            attention(rows)
            for t in range(4):
                C.name("ready", X("g", t), *C.labels[("kept", X("g", rows.last_unit_of(t)))])
            keep_hi("g", 4, ch, lambda k: aq[:, k, 0:T])
            gates("g")
            for a in range(2):
                next_split()
                for n in range(2 - a):
                    t = 2 * a + n
                    act.wait_ge(*at("out", (panel[0] - 1, n)))
                    if t == 0:
                        act.wait_ge(*at("gated", X("g", 1, 3)))
                    act.activation(uf[:, t, 0:T], wide(2 * t % 4, T), ACT.Copy).then_inc(*up("uf", X(t)))
            for g, (a, b) in groups(T):
                for t in range(a // P, b // P):
                    if (t - a // P) % 2 == 1:
                        next_split()
                    act.wait_ge(*at("grouped", X(t)))
                    if t >= 2:
                        act.wait_ge(*at("slot_read", X(t - 2)))
                    act.activation(fh[:, t % 2, :], wide(2 * (t % 2), TT), ACT.Copy).then_inc(*up("fh", X(t)))
                for f in range(3):
                    act.wait_ge(*at("mixed", X(g, f)))
                    act.activation(ch[:, f, a:b], ps[:, 4 + f, 0:b - a], ACT.Copy).then_inc(*up("yf_hi", X(g, f)))
            gates("f")
            for n in range(3):
                next_split()
                act.wait_ge(*at("out", (panel[0] - 1, 1)))
                if n == 0:
                    act.wait_ge(*at("gated", X("f", 1, 3)))
                if n == 2:
                    act.wait_ge(*at("vp", X(0)))
                act.activation(sg[:, n % 2, 0:T], wide(4 * (n % 2) + 2, T), ACT.Sigmoid).then_inc(*up("sg", X(n)))
            for n in range(3):
                act.wait_ge(*at("centred", X(n)))
                if n == 0:
                    act.wait_ge(*at("vp", X(2)))
                else:
                    act.wait_ge(*at("var_sum", X(n - 1)))
                act.activation(sg[:, 0, 0:T], cv[:, n, 0:T], ACT.Square).then_inc(*up("csq", X(n)))
            act.wait_ge(*at("cvar", X()))
            act.activation(rstd[:, 0:T], rstd[:, 0:T], ACT.Sqrt).then_inc(*up("croot", X()))
            for n in range(3):
                act.wait_ge(*at("cnormed", X(n)))
                act.activation(cv[:, n, 0:T], cv[:, n, 0:T], ACT.Silu, bias=pcol("ln_b", 3 * l + n),
                               scale=pcol("ln_g", 3 * l + n)).then_inc(*up("ready", X("c", n)))
            keep_hi("c", 3, ch, lambda k: cv[:, k, 0:T])
            gates("c")
            act.wait_ge(panel_used, panel[0])
            for k in range(KD):
                act.wait_ge(*at("gated", X("c", k // 4, k % 4)))
                act.activation(mh[:, k, 0:T], y[:, k, 0:T], ACT.Copy).then_inc(*up("c_hi", X("out", k)))
            nxt = "n4" if l == 0 else "n6"
            for a in range(4):
                next_split()
                for n in range(2):
                    k = 2 * a + n
                    act.wait_ge(*at("out", (panel[0] - 1, n)))
                    act.activation(y[:, k, 0:T], wide(2 * k % 4, T), ACT.Copy).then_inc(*up("src", (nxt, "post", k)))

        def mix_act(st):
            if st == "mix1":
                mix1()
            else:
                mix2(st)

        for st in ORDER:
            if st in NORMS:
                norm(st)
            elif st in MLPS:
                mlp(MLPS[st])
            else:
                mix_act(st)

    @block.vector
    def _(dve):
        def chain(ins):
            ins.then_inc(*up("chain", ("n", C.count.get("chain", 0))))
            dve.wait_ge(sem("chain"), C.count["chain"])

        def mean_square(st, what, T):
            dve.wait_ge(*at("sq_used", (st, what, KD - 1)))
            dve.tensor_scalar(rstd[:, 0:T], wide(SUM_BANK[what], T), 1.0 / D, EPS, ALU.mult, ALU.add)\
               .then_inc(*up("ms", (st, what)))
            dve.wait_ge(*at("root", (st, what)))
            dve.reciprocal(rstd[:, 0:T], rstd[:, 0:T]).then_inc(*up("rstd", (st, what)))
            dve.wait_ge(*at("rstd", (st, what)))

        def mod(k, i=None, by=0):
            dve.wait_ge(mod_loaded[k % 2], lin(16 * (k // 2 + 1), 8 * by, i))
            if k >= 2:
                dve.wait_ge(mod_used, lin(k - 1, by, i))
            conds = (0,) if k < NM1 else (1, 2)
            C.start("mod_part", (k,))
            n = 0
            for j in range(KD):
                for c, cond in enumerate(conds):
                    w, s = mraw[:, k % 2, j * CW:(j + 1) * CW], csil[:, cond, j:j + 1]
                    acc = macc[:, k % 2, c, :]
                    if j == 0:
                        ins = dve.tensor_scalar(acc, w, s, None, ALU.mult)
                    else:
                        dve.wait_ge(*at("mod_part", ("start", (k,)), lin(n - len(conds) + 1, by * (KD * len(conds) - 1), i)))
                        ins = dve.scalar_tensor_tensor(acc, w, s, acc, ALU.mult, ALU.add)
                    n += 1
                    if n < KD * len(conds):
                        ins.then_inc(*up("mod_part"))
            ins.then_inc(mod_read, 1)

        def norm(st):
            post, pre = NORMS[st]
            v = vec[:, int(st[1]) % 2, :, :]
            if st in MOD_NEED:
                t0, t1, n = MOD_NEED[st]
                dve.wait_ge(mod_used, n)
                name, b0 = ("b_ada", t0) if t0 < 72 else ("b_mod", t0 - 72)
                for c in range(1 if t0 < 72 else 2):
                    chain(dve.tensor_tensor(mods[:, t0:t1, c], ps[:, 7, 2 * t0 + c:2 * t1 + c:2],
                                            pcol(name, b0, t1 - t0), ALU.add))
            if post:
                T, tg, factor, (gain, j) = post
                for g, _ in groups(T):
                    chain(dve.scalar_tensor_tensor(v[:, g, :], mods[:, tg:tg + KD, g], factor,
                                                   pcol(gain, j, KD), ALU.mult, ALU.mult))
            if pre:
                T, _, tsc, (gain, j) = pre
                for g, _ in groups(T):
                    chain(dve.scalar_tensor_tensor(v[:, 2 + g, :], mods[:, tsc:tsc + KD, g], 1.0,
                                                   pcol(gain, j, KD), ALU.add, ALU.mult))
            if post:
                T = post[0]
                mean_square(st, "post", T)
                for k in range(KD + 1):
                    if k < KD:
                        dve.tensor_tensor(y[:, k, 0:T], y[:, k, 0:T], rstd[:, 0:T], ALU.mult)\
                           .then_inc(*up("ynormed", (st, k)))
                    if k >= 1:
                        dve.wait_ge(*at("ynormed", (st, k - 1)))
                        gs = groups(T)
                        for g, (a, b) in gs:
                            ins = dve.scalar_tensor_tensor(x[:, k - 1, a:b], y[:, k - 1, a:b],
                                                           v[:, g, k - 1:k], x[:, k - 1, a:b], ALU.mult, ALU.add)
                            ins.then_inc(*up("x_new", (st, k - 1, g)))
                        C.name("x_new", (st, k - 1), *C.labels[("x_new", (st, k - 1, gs[-1][0]))])
                        C.name("src", (st, "pre", k - 1), *C.labels[("x_new", (st, k - 1))])
            else:
                for k in range(KD):
                    C.name("src", (st, "pre", k), "setup", 16 * 3)
            if pre:
                T = pre[0]
                mean_square(st, "pre", T)
                for k in range(KD + 1):
                    if k < KD:
                        if k >= 2:
                            dve.wait_ge(*at("hf", (st, k - 2, groups(T)[-1][0])))
                        dve.tensor_tensor(tn[:, k % 2, 0:T], x[:, k, 0:T], rstd[:, 0:T], ALU.mult)\
                           .then_inc(*up("normed", (st, k)))
                    if k >= 1:
                        dve.wait_ge(*at("h_hi", (st, k - 1)))
                        dve.tensor_tensor(hlo[:, k - 1, 0:T], hf[:, (k - 1) % 2, 0:T],
                                          hhi[:, k - 1, 0:T].bitcast(F32), ALU.subtract).then_inc(*up("h_lo", (st, k - 1)))

        def mlp(m):
            st, T, O = m.name, m.T, m.O
            for kind in ("hid", "hid_lo", "added"):
                C.start(kind, st)
            for k in range(KD):
                for a, b in spans(T):
                    dve.memset(y[:, k, a:b], 0.0).then_inc(*up("added"))

            def units(c, i=None):
                for n in range(2):
                    e = lin(2 * c + n + 1, 4, i)
                    dve.wait_ge(*at("acted", ("start", st), e))
                    if m.gated:
                        dve.tensor_tensor(tmp[:, n, 0:T], tmp[:, n, 0:T], ps[:, 2 * n + 1, 0:T], ALU.mult)\
                           .then_inc(*up("hid"))
                    else:
                        dve.tensor_tensor(tmp[:, n, 0:T], tmp[:, n, 0:T], wide(2 * n, T), ALU.mult)\
                           .then_inc(*up("hid"))
                    dve.wait_ge(*at("hid_hi", ("start", st), e))
                    dve.tensor_tensor(dlo[:, c % 2, n, 0:T], tmp[:, n, 0:T],
                                      dhi[:, c % 2, n, 0:T].bitcast(F32), ALU.subtract).then_inc(*up("hid_lo"))

            def add(c, i=None):
                for o in range(O):
                    if o < O - 1:
                        dve.wait_ge(*at("down", ("start", st), lin((O - 1) * c + o + 1, 2 * (O - 1), i)))
                    else:
                        dve.wait_ge(panel_used, lin(down_panel(m, c) + 1, m.per_trip, i))
                    dve.wait_ge(*at("added", ("start", st), lin(O * c + o + 1, 2 * O, i)))
                    a, b = spans(T)[o % m.H]
                    dst = y[:, o // m.H, a:b]
                    dve.tensor_tensor(dst, ps[:, 4 + o % 3, 0:b - a], dst, ALU.add).then_inc(*up("added"))

            k = m.mod0
            units(0)
            for u in range(m.before):
                mod(k + u)
            k += m.before
            with C.loop(dve, m.trips) as i:
                for u in range(2):
                    for v in range(m.within // 2):
                        mod(k + u * (m.within // 2) + v, i, m.within)
                    units(1 + u, i)
                    add(u, i)
            k += m.within * m.trips
            if m.rest:
                units(m.C - 1)
                add(m.C - 2)
            for u in range(m.after):
                mod(k + u)
            add(m.C - 1)
            nxt = ORDER[ORDER.index(st) + 1] if ORDER.index(st) + 1 < len(ORDER) else None
            for k in range(KD):
                C.name("src", (nxt, "post", k), "added", C.count["added"] - O + (k + 1) * m.H)

        dve.memset(ones[:, :], 1.0).then_inc(*up("ones", "all"))
        dve.wait_ge(*at("csil", "all"))
        for k in range(8):
            mod(k)

        def softplus_of_minus_lambda():
            lam = pcol("lru_lambda", 0, KD)
            s8, neg, ab, e, s, s2, q = [small[:, KD * i:KD * (i + 1)] for i in range(7)]
            chain(dve.tensor_scalar(neg, lam, -1.0, None, ALU.mult))
            dve.tensor_tensor(ab, lam, neg, ALU.max).then_inc(*up("lam", "abs"))
            dve.wait_ge(*at("lam_exp", "all"))
            chain(dve.tensor_scalar(s, e, 2.0, None, ALU.add))
            chain(dve.reciprocal(s, s))
            chain(dve.tensor_tensor(s, s, e, ALU.mult))
            chain(dve.tensor_tensor(s2, s, s, ALU.mult))
            chain(dve.tensor_scalar(q, s2, 1.0 / 17, None, ALU.mult))
            for n in (15, 13, 11, 9, 7, 5, 3):
                chain(dve.scalar_tensor_tensor(q, q, 1.0 / n, s2, ALU.add, ALU.mult))
            chain(dve.scalar_tensor_tensor(q, q, 1.0, s, ALU.add, ALU.mult))
            chain(dve.tensor_scalar(neg, neg, 0.0, 8.0, ALU.max, ALU.mult))
            chain(dve.scalar_tensor_tensor(s8, q, 16.0, neg, ALU.mult, ALU.add))

        def mix1():
            softplus_of_minus_lambda()
            for n in range(2):
                dve.memset(xpad[:, n, 0:4], 0.0).then_inc(*up("xpad", n))
            for r in range(4):
                for n in range(2):
                    j = 2 * r + n
                    dve.wait_ge(*at("xcopy", (r, n)))
                    if r >= 1:
                        dve.wait_ge(*at("gates", (r - 1, n)))
                        dve.wait_ge(*at("gated_in", (r - 1, n)))
                    chain(dve.tensor_scalar(xc[:, n, :], xpad[:, n, 0:L], pcol("conv_w", j), pcol("conv_b", j),
                                            ALU.mult, ALU.add))
                    for t in range(1, 4):
                        ins = dve.scalar_tensor_tensor(xc[:, n, :], xpad[:, n, t:t + L], pcol("conv_w", KD * t + j),
                                                       xc[:, n, :], ALU.mult, ALU.add)
                        if t < 3:
                            chain(ins)
                    ins.then_inc(*up("xc", (r, n)))
                for n in range(2):
                    j = 2 * r + n
                    dve.wait_ge(*at("ga", (r, n)))
                    dve.tensor_scalar(ga[:, n, :], ga[:, n, :], small[:, j:j + 1], None, ALU.mult)\
                       .then_inc(*up("exponent", (r, n)))
                    dve.wait_ge(*at("gx", (r, n)))
                    dve.wait_ge(*at("xc", (r, n)))
                    dve.tensor_tensor(gx[:, n, :], gx[:, n, :], xc[:, n, :], ALU.mult).then_inc(*up("gated_in", (r, n)))
                for n in range(2):
                    dve.wait_ge(*at("decay", (r, n)))
                    chain(dve.tensor_tensor(hs[:, n, :], ga[:, n, :], ga[:, n, :], ALU.mult))
                    dve.scalar_tensor_tensor(gm[:, n, :], hs[:, n, :], 1.0, gm[:, n, :], ALU.add, ALU.mult)\
                       .then_inc(*up("one_less_a2", (r, n)))
                for n in range(2):
                    j = 2 * r + n
                    dve.wait_ge(*at("mult", (r, n)))
                    dve.wait_ge(*at("gated_in", (r, n)))
                    chain(dve.tensor_tensor(gm[:, n, :], gm[:, n, :], gx[:, n, :], ALU.mult))
                    chain(dve.tensor_tensor_scan(hs[:, n, :], ga[:, n, :], gm[:, n, :], 0.0, ALU.mult, ALU.add))
                    dve.wait_ge(*at("gelu", (r, n)))
                    dve.tensor_tensor(y[:, j, 0:L], hs[:, n, :], gy[:, n, :], ALU.mult).then_inc(*up("rec", (r, n)))
            p = first["mix1"] + 8
            dve.wait_ge(*at("rec", (3, 1)))
            for half in range(2):
                o = 64 * (1 - half)
                chain(dve.memset(qm[o:o + 64, half, :], 0.0))
            for t in range(4):
                dve.wait_ge(*at("out", (p + 2 + t // 2, t % 2)))
                dve.tensor_copy(kf[:, t, :], ps[:, 4 + t, :]).then_inc(*up("k", t))

            def one_head(u):
                if u >= 2:
                    dve.wait_ge(*at("scores", (u - 2, 3)))
                dve.wait_ge(*at("q", u // 2))
                o = 64 * (u % 2)
                dve.tensor_copy(qm[o:o + 64, u % 2, :], qf[o:o + 64, u // 2, :]).then_inc(*up("qm", u))

            def biased_max(u):
                dve.wait_ge(*at(f"bias{u % 2}", u))
                chain(dve.memset(bias[0:64, u % 2, 192:256], float(np.finfo(np.float32).min)))
                for i in range(4):
                    dve.wait_ge(*at("scores", (u, i)))
                    if u >= 2:
                        dve.wait_ge(*at("tr", (u - 2, 3)))
                    near = max(0, i - 1) * P
                    end = (i + 1) * P
                    b = 4 * (u % 2) + i
                    ins = dve.scalar_tensor_tensor(pr[:, u % 2, i, near:end], ps[:, b, near:end], SCALE,
                                                   bias[:, u % 2, 2 * P - (end - near):2 * P], ALU.mult, ALU.add)
                    if near:
                        chain(ins)
                        ins = dve.tensor_scalar(pr[:, u % 2, i, 0:near], ps[:, b, 0:near], SCALE, pcol("rb_far", u),
                                                ALU.mult, ALU.add)
                    ins.then_inc(*up("biased", (u, i)))
                    dve.wait_ge(*at("biased", (u, i)))
                    dve.tensor_reduce(small[:, 32 + 4 * (u % 2) + i:33 + 4 * (u % 2) + i], pr[:, u % 2, i, 0:end],
                                      AX.X, ALU.max, negate=True).then_inc(*up("max", (u, i)))

            def normalise(u):
                s = slice(40 + 4 * (u % 2), 44 + 4 * (u % 2))
                dve.wait_ge(*at("exp", (u, 3)))
                chain(dve.reciprocal(small[:, s], small[:, s]))
                for i in range(4):
                    a = pr[:, u % 2, i, 0:(i + 1) * P]
                    dve.tensor_scalar(a, a, small[:, s.start + i:s.start + i + 1], None, ALU.mult).then_inc(*up("probs", (u, i)))

            def keep(u):
                o, t = 64 * (u % 2), u // 2
                dve.wait_ge(*at("pv", u))
                src = ps[o:o + 64, 4 * (u % 2), :].rearrange("p (a n) -> p a n", a=2)
                hi, lo = hhi[o:o + 64, 2 * t:2 * t + 2, L:TT], hlo[o:o + 64, 2 * t:2 * t + 2, L:TT]
                chain(dve.tensor_copy(hi, src))
                dve.tensor_tensor(lo, src, hi.bitcast(F32), ALU.subtract).then_inc(*up("att", u))

            for u in range(2):
                one_head(u)
                biased_max(u)
            normalise(0)
            normalise(1)
            for u in range(HEADS):
                if u + 2 < HEADS:
                    one_head(u + 2)
                keep(u)
                if u + 2 < HEADS:
                    biased_max(u + 2)
                    normalise(u + 2)
            for k in range(KD):
                dve.wait_ge(*at("bhi", ("rec", k)))
                dve.tensor_tensor(blo[:, k, :], y[:, k, 0:L], bhi[:, k, :].bitcast(F32), ALU.subtract).then_inc(*up("blo", ("rec", k)))
            for j in range(2):
                p = first["mix1"] + 14 + 7 * j
                for t in range(4):
                    dve.wait_ge(*at("out", (p + 2, t)))
                    dve.wait_ge(*at("gate", (j, "a", t)))
                    dve.wait_ge(*at("blo", ("rec", 4 * j + t)))
                    dve.tensor_tensor(y[:, 4 * j + t, 0:L], ps[:, 4 + t, :], gate[:, t, :], ALU.mult).then_inc(*up("merged", (j, "a", t)))
                for t in range(4):
                    dve.wait_ge(*at("out", (p + 5 + t // 2, t % 2)))
                    dve.wait_ge(*at("gate", (j, "r", t)))
                    dve.tensor_tensor(gate[:, t, :], ps[:, 4 + t, :], gate[:, t, :], ALU.mult).then_inc(*up("rgated", (j, t)))
                    dve.wait_ge(*at("rgated", (j, t)))
                    dve.tensor_tensor(y[:, 4 * j + t, 0:L], y[:, 4 * j + t, 0:L], gate[:, t, :], ALU.add).then_inc(*up("merged", (j, "r", t)))
            for k in range(KD):
                dve.wait_ge(*at("bhi", ("out", k)))
                dve.tensor_tensor(blo[:, k, :], y[:, k, 0:L], bhi[:, k, :].bitcast(F32), ALU.subtract).then_inc(*up("blo", ("out", k)))

        def mix2(st):
            X = lambda *k: (st,) + k
            l, T, p0 = LAYER[st], TOKENS[st], first[st]
            lam_init = 0.8 - 0.6 * math.exp(-0.3 * l)
            swap = [(i + 16) % 32 for i in range(32)]

            def turn(tag, t, src, dst, scratch, rope_event):
                dve.wait_ge(*at(rope_event, st))
                chain(dve.stream_shuffle(scratch, src, swap))
                chain(dve.tensor_tensor(scratch, scratch, rope[:, 1, :], ALU.mult))
                chain(dve.tensor_tensor(dst, src, rope[:, 0, :], ALU.mult))
                dve.tensor_tensor(dst, dst, scratch, ALU.add).then_inc(*up("roped", X(tag, t)))

            def head_norm(tag, T, size, src, gain, dst, bank, out_event, before):
                if before:
                    dve.wait_ge(*at(out_event, X(before)))
                dve.wait_ge(*at("hsum", X(tag)))
                dve.tensor_scalar(rstd[:, 0:T], wide(bank, T), 1.0 / size, EPS, ALU.mult, ALU.add)\
                   .then_inc(*up("hms", X(tag)))
                dve.wait_ge(*at("hroot", X(tag)))
                chain(dve.reciprocal(rstd[:, 0:T], rstd[:, 0:T]))
                dve.scalar_tensor_tensor(dst, src, gain, rstd[:, 0:T], ALU.mult, ALU.mult).then_inc(*up(out_event, X(tag)))

            def keep_lo(tag, nt, dst, hi, src):
                for k in range(nt):
                    dve.wait_ge(*at("c_hi", X(tag, k)))
                    dve.tensor_tensor(dst[:, k, 0:T], src(k), hi[:, k, 0:T].bitcast(F32), ALU.subtract)\
                       .then_inc(*up("c_lo", X(tag, k)))

            def merge(tag, p):
                for j in range(2):
                    for t in range(4):
                        k = 4 * j + t
                        dve.wait_ge(*at("out", (p + 3 * j, t)))
                        dve.wait_ge(*at("gate", X(tag, j, t)))
                        b = 4 + 2 * (t % 2)
                        if tag == BRANCHES[0]:
                            if k == 0:
                                dve.wait_ge(*at("pv", X("d", LAST_UNIT[st, "d"])))
                            dve.tensor_tensor(y[:, k, 0:T], wide(b, T), gate2[:, t, 0:T], ALU.mult).then_inc(*up("gated", X(tag, j, t)))
                        else:
                            dve.tensor_tensor(gate2[:, t, 0:T], wide(b, T), gate2[:, t, 0:T], ALU.mult).then_inc(*up("bank_read", X(tag, j, t)))
                            dve.wait_ge(*at("bank_read", X(tag, j, t)))
                            dve.tensor_tensor(y[:, k, 0:T], y[:, k, 0:T], gate2[:, t, 0:T], ALU.add).then_inc(*up("gated", X(tag, j, t)))

            def masked_query(rows, uno):
                u = rows.unit(uno)
                t, half, g = u
                a, b = GROUPS[g]
                for j in ((0, 1) if half is None else (half,)):
                    prev = rows.last_row_with(uno, j)
                    if prev is not None:
                        dve.wait_ge(*at("scores", X(rows.tag, prev, j)))
                    dve.wait_ge(*at(*rows.query_event(X, t, g)))
                    o = slice(64 * j, 64 * j + 64)
                    ins = dve.tensor_copy(qm2[o, j, 0:b - a], aq[o, t, a:b])
                    if half is None and j == 0:
                        chain(ins)
                ins.then_inc(*up("qm", X(rows.tag, uno)))

            def row_max(rows, r):
                u, i, js, k0, k1 = rows[r]
                for j in js:
                    c = ROW_COL(r, j)
                    dve.wait_ge(*at("scores", X(rows.tag, r, j)))
                    if r >= 2:
                        dve.wait_ge(*at("exp", X(rows.tag, r - 2, rows[r - 2][2][-1])))
                    b = rows.bank(r, j)
                    s = ps[:, b:b + 2, :].rearrange("p a n -> p (a n)")[:, k0:k1] if k0 == 0 else ps[:, b, 0:k1 - k0]
                    chain(dve.tensor_reduce(small[:, c:c + 1], s, AX.X, ALU.max, negate=True))
                c0, c1 = ROW_COL(r, js[0]), ROW_COL(r, js[-1]) + 1
                dve.tensor_scalar(small[:, c0:c1], small[:, c0:c1], SCALE, None, ALU.mult).then_inc(*up("nmax", X(rows.tag, r)))

            def row_probs(rows, r):
                u, i, js, k0, k1 = rows[r]
                n = k1 - k0
                c = ROW_COL(r, js[0]) + 4
                dve.wait_ge(*at("exp", X(rows.tag, r, js[-1])))
                chain(dve.reciprocal(small[:, c:c + len(js)], small[:, c:c + len(js)]))
                if len(js) == 2:
                    chain(dve.tensor_scalar(pr2[:, r % 2, 1, 0:n], pr2[:, r % 2, 1, 0:n], small[:, c + 1:c + 2],
                                            small[:, 48:49], ALU.mult, ALU.mult))
                    dve.scalar_tensor_tensor(pr2[:, r % 2, 0, 0:n], pr2[:, r % 2, 0, 0:n], small[:, c:c + 1],
                                             pr2[:, r % 2, 1, 0:n], ALU.mult, ALU.add).then_inc(*up("probs", X(rows.tag, r)))
                else:
                    dve.tensor_scalar(pr2[:, r % 2, 0, 0:n], pr2[:, r % 2, 0, 0:n], small[:, c:c + 1], None, ALU.mult)\
                       .then_inc(*up("probs", X(rows.tag, r)))

            def attention(rows):
                for half in range(2):
                    o = 64 * (1 - half)
                    chain(dve.memset(qm2[o:o + 64, half, :], 0.0))
                masked_query(rows, 0)
                row_max(rows, 0)
                for r in range(len(rows)):
                    if r + 1 < len(rows):
                        if rows.unit_start(r + 1):
                            masked_query(rows, rows.unit_no(r + 1))
                        row_max(rows, r + 1)
                    row_probs(rows, r)

            dve.wait_ge(*at("lv", st))
            v = pr2[:, 0, 0, 0:256].rearrange("p (a b d) -> p a b d", a=2, b=2)
            chain(dve.tensor_tensor(v[:, :, 0, :], v[:, :, 0, :], v[:, :, 1, :], ALU.mult))
            dve.tensor_reduce(small[:, 64:66], v[:, :, 0, :], AX.X, ALU.add).then_inc(*up("lv_sums", st))
            dve.wait_ge(*at("lv_exp", st))
            chain(dve.tensor_tensor(small[:, 48:49], small[:, 67:68], small[:, 66:67], ALU.subtract))
            chain(dve.tensor_scalar(small[:, 48:49], small[:, 48:49], -lam_init, None, ALU.add))
            chain(dve.tensor_scalar(small[:, 49:50], pcol("subln", l), 1.0 - lam_init, None, ALU.mult))
            for t in range(4):
                dve.wait_ge(*at("out", (p0 + t // 2, t % 2)))
                turn("dk", t, ps[:, 2 * t % 4, :], dk[:, t, 0:L], pr2[:, 1, t % 2, 0:L], "rope")
            for t in range(4):
                dve.wait_ge(*at("out", (p0 + 4 + t // 2, t % 2)))
                turn("dq", t, ps[:, 2 * t % 4, :], aq[:, t, 0:L], pr2[:, 1, t % 2, 0:L], "rope")
            for t in range(4):
                dve.wait_ge(*at("roped", X("dq", t)))
            attention(ROWS(st, "d"))
            for t in range(4):
                head_norm(("sub", t), T, P, aq[:, t, 0:T], small[:, 49:50], aq[:, t, 0:T], 2 * (t % 2), "subbed",
                          ("sub", t - 1) if t else None)
                C.name("ready", X("d", t), *C.labels[("subbed", X(("sub", t)))])
            keep_lo("d", 4, cl, ch, lambda k: aq[:, k, 0:T])
            merge("d", p0 + 8)
            pg = p0 + 12

            def normed_and_turned(tag, t, bank, sum_bank, T, gain, dst):
                dve.wait_ge(*at("out", (pg if tag == "gk" else pg + 1 + t // 2, t % 2 if tag == "gq" else 0)))
                before = {("gk", 0): None, ("gq", 0): ("gk", 0)}.get((tag, t), ("gq", t - 1))
                head_norm((tag, t), T, 64, wide(bank, T), gain, dst, sum_bank, "hnormed", before)
                dve.wait_ge(*at("hnormed", X((tag, t))))
                turn(tag, t, dst[:, 0:L], dst[:, 0:L], pr2[:, 1, t % 2, 0:L], "rope2")

            normed_and_turned("gk", 0, 0, 6, TT, pcol("k_norm", l), gk[:, 0, :])
            for t in range(4):
                normed_and_turned("gq", t, GQ_BANK[t], 6, T, pcol("q_norm", l), aq[:, t, 0:T])
            for t in range(4):
                dve.wait_ge(*at("roped", X("gq", t)))
            attention(ROWS(st, "g"))
            keep_lo("g", 4, cl, ch, lambda k: aq[:, k, 0:T])
            merge("g", pg + 5)
            pf = pg + 9
            for g, (a, b) in groups(T):
                for t in range(a // P, b // P):
                    dve.wait_ge(*at("fh", X(t)))
                    dve.tensor_tensor(fl[:, t % 2, :], wide(2 * (t % 2), TT), fh[:, t % 2, :].bitcast(F32), ALU.subtract)\
                       .then_inc(*up("fl", X(t)))
                for f in range(3):
                    dve.wait_ge(*at("yf_hi", X(g, f)))
                    dve.tensor_tensor(cl[:, f, a:b], ps[:, 4 + f, 0:b - a], ch[:, f, a:b].bitcast(F32), ALU.subtract)\
                       .then_inc(*up("yf_lo", X(g, f)))
            for f in range(3):
                C.name("c_lo", X("f", f), *C.labels[("yf_lo", X(groups(T)[-1][0], f))])
            pm = pf + 2 + len(DFT_PANELS[l])
            merge("f", pm + 2)
            pc = pm + 6
            dve.wait_ge(*at("gated", X("f", 1, 3)))
            dve.wait_ge(*at("out", (pc - 1, 3)))
            segs = [(a, b, a + 15 + 30 * g) for g, (a, b) in groups(T)]
            for n in range(3):
                chain(dve.memset(vp[:, n, :], 0.0))
            for n in range(3):
                dve.wait_ge(*at("sg", X(n)))
                for g, (a, b, s) in enumerate(segs):
                    ins = dve.tensor_tensor(vp[:, n, s:s + b - a], ps[:, 4 * (n % 2) + g, 0:b - a], sg[:, n % 2, a:b], ALU.mult)
                    if g + 1 < len(segs):
                        chain(ins)
                ins.then_inc(*up("vp", X(n)))
                dve.wait_ge(*at("vp", X(n)))
                for t in range(31):
                    w = pcol("conv_dw", 93 * l + 3 * t + n)
                    for a, b, s in segs:
                        tap = vp[:, n, s - 15 + t:s - 15 + t + b - a]
                        if t == 0:
                            ins = dve.tensor_scalar(cv[:, n, a:b], tap, w, pcol("conv_dw_b", 3 * l + n), ALU.mult, ALU.add)
                        else:
                            ins = dve.scalar_tensor_tensor(cv[:, n, a:b], tap, w, cv[:, n, a:b], ALU.mult, ALU.add)
                        if (t, b) != (30, segs[-1][1]):
                            ins.then_inc(*up("tap", X(n, t, a)))
                        else:
                            ins.then_inc(*up("conv", X(n)))
                    if t < 30:
                        dve.wait_ge(*at("tap", X(n, t, segs[-1][0])))
            dve.wait_ge(*at("mean_sum", X(2)))
            chain(dve.tensor_scalar(mean[:, 0:T], wide(0, T), 1.0 / 384, None, ALU.mult))
            for n in range(3):
                dve.tensor_tensor(cv[:, n, 0:T], cv[:, n, 0:T], mean[:, 0:T], ALU.subtract).then_inc(*up("centred", X(n)))
            dve.wait_ge(*at("var_sum", X(2)))
            dve.tensor_scalar(rstd[:, 0:T], wide(2, T), 1.0 / 384, EPS, ALU.mult, ALU.add).then_inc(*up("cvar", X()))
            dve.wait_ge(*at("croot", X()))
            chain(dve.reciprocal(rstd[:, 0:T], rstd[:, 0:T]))
            for n in range(3):
                dve.tensor_tensor(cv[:, n, 0:T], cv[:, n, 0:T], rstd[:, 0:T], ALU.mult).then_inc(*up("cnormed", X(n)))
            keep_lo("c", 3, cl, ch, lambda k: cv[:, k, 0:T])
            merge("c", pc + 5)
            for k in range(KD):
                dve.wait_ge(*at("c_hi", X("out", k)))
                dve.tensor_tensor(ml[:, k, 0:T], y[:, k, 0:T], mh[:, k, 0:T].bitcast(F32), ALU.subtract)\
                   .then_inc(*up("c_lo", X("out", k)))

        def mix_dve(st):
            if st == "mix1":
                mix1()
            else:
                mix2(st)

        for st in ORDER:
            if st in NORMS:
                norm(st)
            elif st in MLPS:
                mlp(MLPS[st])
            else:
                mix_dve(st)

    @block.tensor
    def _(pe):
        def tri(out, a, b, first, last):
            pe.matmul(out, a[0], b[0], start=first, stop=False)
            pe.matmul(out, a[0], b[1], start=False, stop=False)
            return pe.matmul(out, a[1], b[0], start=False, stop=last)

        def wtile(p, kt, cw, k, c0, n=P):
            s = k * cw + c0
            return whi[:, p % 2, s:s + n], wlo[:, p % 2, s:s + n]

        def mod(k, i=None, by=0):
            pe.wait_ge(mod_read, lin(k + 1, by, i))
            for n in range(2):
                for c in range(1 if k < NM1 else 2):
                    ins = pe.matmul(ps[:, 7, bass.ds(lin(4 * k + 2 * n + c, 4 * by, i), 1)],
                                    macc[:, k % 2, c, n * P:(n + 1) * P], ones[:, 0:1], start=True, stop=True)
            ins.then_inc(mod_used, 1)

        def sums(st, what, T):
            for k in range(KD):
                pe.wait_ge(*at("sq", (st, what, k)))
                for h, (a, b) in enumerate(spans(T)):
                    ins = pe.matmul(ps[:, SUM_BANK[what] + h, 0:b - a], ones[:, :], sq[:, k % 2, a:b],
                                    start=(k == 0), stop=(k == KD - 1))
                ins.then_inc(*up("sq_used", (st, what, k)))

        def norm(st):
            post, pre = NORMS[st]
            if post:
                sums(st, "post", post[0])
            if pre:
                sums(st, "pre", pre[0])

        def mlp(m):
            st, T, H, O = m.name, m.T, m.H, m.O
            for kind in ("up_first", "down"):
                C.start(kind, st)
            pre = ORDER[ORDER.index(st) - 1]

            def ups(c, p, i=None):
                for n in range(2):
                    pn = p + n if m.gated else p
                    if m.gated or n == 0:
                        pe.wait_ge(lo_ready, lin(pn + 1, m.per_trip, i))
                    if c >= 1:
                        pe.wait_ge(*at("hid", ("start", st), lin(2 * (c - 1) + n + 1, 4, i)))
                    for h in range(2 if m.gated else H):
                        mv = slice(*spans(T)[0 if m.gated else h])
                        out = ps[:, 2 * n + h, 0:mv.stop - mv.start]
                        c0 = h * P if m.gated else n * P
                        for k in range(KD):
                            if c == 0 and n == 0 and h == 0:
                                pe.wait_ge(*at("h_lo", (pre, k)))
                            ins = tri(out, wtile(pn, KD, CW, k, c0), (hhi[:, k, mv], hlo[:, k, mv]),
                                      k == 0, k == KD - 1)
                    if m.gated or n == 1:
                        ins.then_inc(panel_used, 1)
                    else:
                        ins.then_inc(*up("up_first"))

            def down(c, p, i=None):
                pe.wait_ge(lo_ready, lin(p + 1, m.per_trip, i))
                pe.wait_ge(*at("hid_lo", ("start", st), lin(2 * c + 2, 4, i)))
                for o in range(O):
                    j, h = o // H, o % H
                    prior = O * (c + 1) + o - 3 if o >= 3 else O * c + max(q for q in range(O) if q % 3 == o)
                    pe.wait_ge(*at("added", ("start", st), lin(prior + 1, 2 * O, i)))
                    for k in range(2):
                        mv = slice(*spans(T)[h])
                        ins = tri(ps[:, 4 + o % 3, 0:mv.stop - mv.start], wtile(p, 2, D, k, j * P),
                                  (dhi[:, c % 2, k, mv], dlo[:, c % 2, k, mv]), k == 0, k == 1)
                    if o < O - 1:
                        ins.then_inc(*up("down"))
                ins.then_inc(panel_used, 1)

            ups(0, m.p0)
            k = m.mod0
            for u in range(m.before):
                mod(k + u)
            k += m.before
            with C.loop(pe, m.trips) as i:
                for u in range(2):
                    p = m.p0 + m.UP + u * (m.UP + 1)
                    ups(1 + u, p, i)
                    for v in range(m.within // 2):
                        mod(k + u * (m.within // 2) + v, i, m.within)
                    down(u, p + m.UP, i)
            k += m.within * m.trips
            if m.rest:
                p = m.p0 + m.UP + m.trips * m.per_trip
                ups(m.C - 1, p)
                down(m.C - 2, p + m.UP)
            for u in range(m.after):
                mod(k + u)
            down(m.C - 1, m.p0 + (m.UP + 1) * m.C - 1)

        pe.wait_ge(*at("ones", "all"))
        for k in range(8):
            mod(k)

        free = {}

        def claim(banks, event):
            for b in banks:
                if b in free:
                    pe.wait_ge(*at(*free[b]))
                free[b] = event

        def ended(ins, p, n, last):
            if last:
                ins.then_inc(panel_used, 1)
                C.name("out", (p, n), "panel_used", p + 1)
            else:
                ins.then_inc(*up("out", (p, n)))

        def project(p, kt, cw, src, T, banks, events, ready=None, whole=True):
            pe.wait_ge(lo_ready, p + 1)
            for n in range(cw // P):
                if n >= len(banks):
                    break
                claim(range(banks[n], banks[n] + len(spans(T))), events[n])
                for h, (a, b) in enumerate(spans(T)):
                    for k in range(kt):
                        if ready and n == 0 and h == 0:
                            pe.wait_ge(*at(*ready(k)))
                        hi, lo = src(k, a, b)
                        ins = tri(ps[:, banks[n] + h, 0:b - a], wtile(p, kt, cw, k, n * P), (hi, lo), k == 0, k == kt - 1)
                ended(ins, p, n, whole and n == len(banks) - 1)

        def by_token(p, cw, c0, c1, T, banks, events, n0=0):
            pe.wait_ge(lo_ready, p + 1)
            for t in range(T // P):
                claim([banks[t]], events[t])
                for k in range(KD):
                    a = (hhi[:, k, t * P:(t + 1) * P], hlo[:, k, t * P:(t + 1) * P])
                    b = wtile(p, KD, cw, k, c0, c1 - c0)
                    ins = tri(ps[:, banks[t], 0:c1 - c0], a, b, k == 0, k == KD - 1)
                ended(ins, p, n0 + t, t == T // P - 1)

        def from_h(k, a, b):
            return hhi[:, k, a:b], hlo[:, k, a:b]

        def mix1():
            p0 = first["mix1"]
            free.clear()
            for r in range(4):
                p = p0 + 2 * r
                project(p, KD, CW, from_h, L, (0, 1), [("xcopy", (r, n)) for n in range(2)],
                        (lambda k: ("h_lo", ("n1", k))) if r == 0 else None)
                project(p + 1, KD, CW, from_h, L, (2, 3), [("gelu", (r, n)) for n in range(2)])
                if r == 0:
                    pe.wait_ge(*at("wbd", "all"))
                for n in range(2):
                    pe.wait_ge(*at("xc", (r, n)))
                    claim([4 + n], ("ga", (r, n)))
                    claim([6 + n], ("gx", (r, n)))
                    pe.matmul(ps[:, 4 + n, :], wbd[:, 0, 2 * r + n, :], xc[:, n, :], start=True, stop=True)
                    pe.matmul(ps[:, 6 + n, :], wbd[:, 1, 2 * r + n, :], xc[:, n, :], start=True, stop=True)\
                      .then_inc(*up("gates", (r, n)))
            p = p0 + 8
            for a in range(2):
                project(p + a, KD, CW, from_h, L, (2 * a, 2 * a + 1), [("q", 2 * a + n) for n in range(2)])
            for a in range(2):
                project(p + 2 + a, KD, CW, from_h, L, (4 + 2 * a, 5 + 2 * a), [("k", 2 * a + n) for n in range(2)])
            for a in range(2):
                by_token(p + 4 + a, CW, 0, CW, L, [4 * a + t for t in range(4)], [("v", (a, t)) for t in range(4)])

            def scores(u):
                pe.wait_ge(*at("qm", u))
                pe.wait_ge(*at("k", u // 2))
                for i in range(4):
                    b = 4 * (u % 2) + i
                    claim([b], ("biased", (u, i)))
                    pe.matmul(ps[:, b, 0:(i + 1) * P], qm[:, u % 2, i * P:(i + 1) * P], kf[:, u // 2, 0:(i + 1) * P],
                              start=True, stop=True).then_inc(*up("scores", (u, i)))

            def turn(u):
                pe.wait_ge(*at("probs", (u, 3)))
                for j in range(4):
                    b = 4 * (u % 2) + j
                    claim([b], ("pt", (u, j)))
                    for i in range(j, 4):
                        ins = pe.transpose(ps[:, b, i * P:(i + 1) * P], pr[:, u % 2, i, j * P:(j + 1) * P], const("ident"))
                    ins.then_inc(*up("tr", (u, j)))

            def weigh(u):
                b, t = 4 * (u % 2), u // 2
                claim([b], ("att", u))
                for j in range(4):
                    pe.wait_ge(*at("pt", (u, j)))
                    v = x[:, 2 * j + t // 2, L + (t % 2) * P:L + (t % 2 + 1) * P]
                    ins = pe.matmul(ps[:, b, j * P:L], v, pt[:, j, j * P:L], start=(j == 0), stop=(j == 3))
                ins.then_inc(*up("pv", u))

            scores(0)
            scores(1)
            for u in range(HEADS):
                turn(u)
                weigh(u)
                if u + 2 < HEADS:
                    scores(u + 2)

            def from_att(k, a, b):
                return hhi[:, 2 * k:2 * k + 2, L:TT], hlo[:, 2 * k:2 * k + 2, L:TT]

            def from_b(k, a, b):
                return bhi[:, k, a:b], blo[:, k, a:b]

            for j in range(2):
                p = p0 + 14 + 7 * j
                for a in range(2):
                    project(p + a, KD, CW, from_h, L, (2 * a, 2 * a + 1), [("gate", (j, "a", 2 * a + n)) for n in range(2)])
                pe.wait_ge(*at("att", HEADS - 1))
                project(p + 2, 4, 512, from_att, L, (4, 5, 6, 7), [("merged", (j, "a", t)) for t in range(4)])
                for a in range(2):
                    project(p + 3 + a, KD, CW, from_h, L, (2 * a, 2 * a + 1), [("gate", (j, "r", 2 * a + n)) for n in range(2)])
                for a in range(2):
                    project(p + 5 + a, KD, CW, from_b, L, (4 + 2 * a, 5 + 2 * a), [("rgated", (j, 2 * a + n)) for n in range(2)],
                            (lambda k: ("blo", ("rec", k))) if j == 0 and a == 0 else None)
            p = p0 + 28
            for a in range(4):
                b = 2 * (a % 2)
                project(p + a, KD, CW, from_b, L, (b, b + 1), [("src", ("n2", "post", 2 * a + n)) for n in range(2)],
                        (lambda k: ("blo", ("out", k))) if a == 0 else None)

        def mix2(st):
            X = lambda *k: (st,) + k
            l, T, p = LAYER[st], TOKENS[st], first[st]
            norm_before = "n3" if l == 0 else "n5"
            free.clear()

            def from_c(k, a, b):
                return ch[:, k, a:b], cl[:, k, a:b]

            def merge(tag, kt, p):
                for j in range(2):
                    for a in range(2):
                        project(p, KD, CW, from_h, T, (0, 2), [("gate", X(tag, j, 2 * a + n)) for n in range(2)])
                        p += 1
                    kind = "gated" if tag == BRANCHES[0] else "bank_read"
                    project(p, kt, 512, from_c, T, (4, 6, 4, 6), [(kind, X(tag, j, t)) for t in range(4)],
                            (lambda k: ("c_lo", X(tag, k))) if j == 0 else None)
                    p += 1
                return p

            def head_sum(tag, T, bank, weights):
                pe.wait_ge(*at("hsq", X(tag)))
                claim(range(bank, bank + len(spans(T))), ("hms", X(tag)))
                for h, (a, b) in enumerate(spans(T)):
                    ins = pe.matmul(ps[:, bank + h, 0:b - a], weights, pr2[:, 0, 0, a:b], start=True, stop=True)
                ins.then_inc(*up("hsum", X(tag)))

            def row_scores(rows, r, keys):
                u, i, js, k0, k1 = rows[r]
                if rows.unit_start(r):
                    pe.wait_ge(*at("qm", X(rows.tag, rows.unit_no(r))))
                for j in js:
                    b = rows.bank(r, j)
                    claim([b, b + 1] if k1 - k0 > L else [b], ("exp", X(rows.tag, r, j)))
                    q = qm2[:, j, (i % 4) * P:(i % 4 + 1) * P]
                    if k0 == 0:
                        pe.matmul(ps[:, b, :], q, keys(u)[:, 0:L], start=True, stop=True)
                        ins = pe.matmul(ps[:, b + 1, 0:LC], q, keys(u)[:, L:TT], start=True, stop=True)
                    else:
                        ins = pe.matmul(ps[:, b, 0:LC], q, keys(u)[:, L:TT], start=True, stop=True)
                    ins.then_inc(*up("scores", X(rows.tag, r, j)))

            def attention(rows, keys, values):
                row_scores(rows, 0, keys)
                for r in range(len(rows)):
                    if r + 1 < len(rows):
                        row_scores(rows, r + 1, keys)
                    u, i, js, k0, k1 = rows[r]
                    pe.wait_ge(*at("probs", X(rows.tag, r)))
                    claim([4, 5], ("pt", X(rows.tag, r)))
                    for k in range((k1 - k0) // P):
                        ins = pe.transpose(ps[:, 4 + k // 4, (k % 4) * P:(k % 4 + 1) * P],
                                           pr2[:, r % 2, 0, k * P:(k + 1) * P], const("ident"))
                    ins.then_inc(*up("tr", X(rows.tag, r)))
                    if rows.unit_end(r):
                        uno = rows.unit_no(r)
                        a, b = GROUPS[u[2]]
                        pe.wait_ge(*at("pt", X(rows.tag, r)))
                        claim([6 + uno % 2], ("kept", X(rows.tag, uno)))
                        n = (k1 - k0) // P
                        for k in range(n):
                            ins = pe.matmul(ps[:, 6 + uno % 2, 0:b - a], values(u, k0 // P + k), pt2[:, k, 0:b - a],
                                            start=(k == 0), stop=(k == n - 1))
                        ins.then_inc(*up("pv", X(rows.tag, uno)))

            for a in range(2):
                project(p + a, KD, CW, from_h, TT, (0, 2), [("ctx_kept", X("dk", 2 * a + n)) for n in range(2)],
                        (lambda k: ("h_lo", (norm_before, k))) if a == 0 else None)
            for a in range(2):
                by_token(p + 2 + a, CW, 0, CW, TT, DV_BANK, [("dv", X(a, t)) for t in range(6)])
            for a in range(2):
                kind = "ctx_kept" if T > L else "roped"
                project(p + 4 + a, KD, CW, from_h, T, (0, 2), [(kind, X("dq", 2 * a + n)) for n in range(2)])
            pe.wait_ge(*at("ctx_kept", X("dk", 3)))
            pe.wait_ge(*at("roped", X("dk", 3)))
            pe.wait_ge(*at("dv", X(1, 5)))
            attention(ROWS(st, "d"), lambda u: dk[:, u[0], :], lambda u, k: dv[:, k, u[0] * P:(u[0] + 1) * P])
            for t in range(4):
                head_sum(("sub", t), T, 2 * (t % 2), ones[:, :])
            p = merge("d", 4, p + 6)
            project(p, KD, CW, from_h, TT, (0,), [("hnormed", X(("gk", 0)))], whole=False)
            by_token(p, CW, P, CW, TT, GV_BANK, [("gv", X(t)) for t in range(6)], n0=1)
            head_sum(("gk", 0), TT, 6, const("block"))
            for a in range(2):
                project(p + 1 + a, KD, CW, from_h, T, tuple(GQ_BANK[2 * a:2 * a + 2]),
                        [("hnormed", X(("gq", 2 * a + n))) for n in range(2)])
                for n in range(2):
                    head_sum(("gq", 2 * a + n), T, 6, const("block"))
            pe.wait_ge(*at("roped", X("gk", 0)))
            pe.wait_ge(*at("gv", X(5)))
            attention(ROWS(st, "g"), lambda u: gk[:, 0, :], lambda u, k: gv[:, k, :])
            p = merge("g", 4, p + 3)
            project(p, KD, CW, from_h, T, (0, 2), [("uf", X(n)) for n in range(2)])
            project(p + 1, KD, P, from_h, T, (0,), [("uf", X(2))])
            p += 2
            pe.wait_ge(*at("uf", X(2)))

            def over_group(t):
                b = 2 * (t % 2)
                claim([b, b + 1], ("fl", X(t)))
                for f in range(3):
                    ins = pe.matmul(ps[:, b + f // 2, (f % 2) * CW:(f % 2 + 1) * CW], uf[:, f, t * P:(t + 1) * P],
                                    const("dft64"), start=True, stop=True)
                ins.then_inc(*up("grouped", X(t)))

            for g, (a, b) in groups(T):
                t0, t1, n = a // P, b // P, b - a
                over_group(t0)
                for t in range(t0, t1):
                    if t + 1 < t1:
                        over_group(t + 1)
                    if (t - t0) % 2 == 0:
                        pe.wait_ge(lo_ready, p + 1)
                    pe.wait_ge(*at("fl", X(t)))
                    for f in range(3):
                        if t == t0:
                            claim([4 + f], ("yf_lo", X(g, f)))
                        for part in range(2):
                            c = f * CW + part * P
                            ins = tri(ps[:, 4 + f, 0:n], (fh[:, t % 2, c:c + P], fl[:, t % 2, c:c + P]),
                                      wtile(p, 2, 2 * n, (t - t0) % 2, part * n, n), t == t0 and part == 0, t == t1 - 1 and part == 1)
                        if t == t1 - 1 and f < 2:
                            ins.then_inc(*up("mixed", X(g, f)))
                    if (t - t0) % 2 == 1:
                        ins.then_inc(panel_used, 1)
                        p += 1
                        C.name("slot_read", X(t), "panel_used", p)
                        if t == t1 - 1:
                            C.name("mixed", X(g, 2), "panel_used", p)
                    else:
                        ins.then_inc(*up("slot_read", X(t)))
            p = merge("f", 3, p)
            for n in range(3):
                b = 4 * (n % 2)
                project(p, KD, CW, from_h, T, (b, b + 2), [("vp", X(n)), ("sg", X(n))])
                p += 1
            for n in range(3):
                pe.wait_ge(*at("conv", X(n)))
                if n == 0:
                    claim(range(0, len(spans(T))), ("centred", X(2)))
                for h, (a, b) in enumerate(spans(T)):
                    ins = pe.matmul(ps[:, h, 0:b - a], ones[:, :], cv[:, n, a:b], start=(n == 0), stop=(n == 2))
                ins.then_inc(*up("mean_sum", X(n)))
            for n in range(3):
                pe.wait_ge(*at("csq", X(n)))
                if n == 0:
                    claim(range(2, 2 + len(spans(T))), ("cvar", X()))
                for h, (a, b) in enumerate(spans(T)):
                    ins = pe.matmul(ps[:, 2 + h, 0:b - a], ones[:, :], sg[:, 0, a:b], start=(n == 0), stop=(n == 2))
                ins.then_inc(*up("var_sum", X(n)))
            p = merge("c", 3, p)
            nxt = "n4" if l == 0 else "n6"
            for a in range(4):
                project(p + a, KD, CW, lambda k, a, b: (mh[:, k, a:b], ml[:, k, a:b]), T, (0, 2),
                        [("src", (nxt, "post", 2 * a + n)) for n in range(2)],
                        (lambda k: ("c_lo", X("out", k))) if a == 0 else None)

        def mix_pe(st):
            if st == "mix1":
                mix1()
            else:
                mix2(st)

        for st in ORDER:
            if st in NORMS:
                norm(st)
            elif st in MLPS:
                mlp(MLPS[st])
            else:
                mix_pe(st)


def down_panel(m, c):
    return m.p0 + m.UP * min(c + 2, m.C) + c


def lay_out(v):
    v = {k: np.asarray(a) for k, a in v.items()}
    first, panels = {}, []

    def stage(name, ps):
        first[name] = len(panels)
        panels.extend(ps)

    stage("ffn1", ffn_panels(v["ffn1_w_gu"][0], v["ffn1_w_down"][0]))
    w = v["w_in"][0]
    ps = []
    for r in range(4):
        ps += cols_panels(w, 1536 + r * CW, 1536 + (r + 1) * CW) + cols_panels(w, 2560 + r * CW, 2560 + (r + 1) * CW)
    ps += cols_panels(w, 0, 1536)
    for j in range(2):
        ps += cols_panels(w, 3584 + 512 * j, 4096 + 512 * j)
        ps += rows_panels(v["w_att_o"][0], 512 * j, 512 * (j + 1))
        ps += cols_panels(w, 4608 + 512 * j, 5120 + 512 * j)
        ps += cols_panels(v["w_rec_o"][0], 512 * j, 512 * (j + 1))
    stage("mix1", ps + cols_panels(v["w_out"][0], 0, D))

    stage("ffn2", ffn_panels(v["ffn2_w_gu"][0], v["ffn2_w_down"][0]))
    stage("mix2", mix2_panels(v, 0))

    stage("mlp1", mlp_panels(v["w_ff1_2"][0], v["w_ff2_2"][0]))
    stage("mix3", mix2_panels(v, 1))

    stage("mlp2", mlp_panels(v["w_ff1_2"][1], v["w_ff2_2"][1]))
    if len(panels) % 2:
        panels.append(np.zeros((P, PANEL), np.float32))

    mod_panels = []
    for w in (v["w_ada"][0], v["w_mod_2"][0], v["w_mod_2"][1]):
        mod_panels += cols_panels(w, 0, w.shape[1])

    par = {
        "b_ada": columns(v["b_ada"]), "b_mod": columns(v["b_mod_2"]), "norm_pre": columns(v["norm_pre"]),
        "norm_post": columns(v["norm_post"]), "conv_w": columns(v["conv_w"]), "conv_b": columns(v["conv_b"]),
        "lru_ba": columns(v["lru_ba"]), "lru_bx": columns(v["lru_bx"]), "lru_lambda": columns(v["lru_lambda"]),
        "g_pre_mix": columns(v["g_pre_mix_2"]), "g_post_mix": columns(v["g_post_mix_2"]),
        "g_pre_mlp": columns(v["g_pre_mlp_2"]), "g_post_mlp": columns(v["g_post_mlp_2"]),
        "q_norm": np.tile(v["q_norm_2"], (1, 2)).T, "k_norm": np.tile(v["k_norm_2"], (1, 2)).T,
        "subln": v["diff_subln_2"].T, "conv_dw": columns(v["conv_dw_2"]), "conv_dw_b": columns(v["conv_dw_bias_2"]),
        "ln_g": columns(v["conv_ln_g_2"]), "ln_b": columns(v["conv_ln_b_2"]),
        "rb_far": np.tile(v["rel_bias"][0][:, -1], (P, 1)),
        "cond": columns(np.concatenate([v["c"][0], v["c_2"][0], v["c_ctx_2"]])),
    }
    par = np.concatenate([par[n] for n, _ in PAR_SIZES], axis=1)

    half = np.kron(np.eye(2), np.ones((64, 64)))
    w64 = 2 * np.pi * np.outer(np.arange(64), np.arange(64)) / 64
    dft = np.concatenate([np.kron(np.eye(2), np.cos(w64)), np.kron(np.eye(2), np.sin(w64))], axis=1)
    cst = np.concatenate([np.eye(P), half, dft], axis=1)
    arrays = {
        "panels": np.stack(panels), "mod_panels": np.stack(mod_panels), "par": par, "cst": cst,
        "xT": v["x"][0].T,
        "wbd": np.stack([block_diagonal(v["lru_wa"][0]), block_diagonal(v["lru_wx"][0])], axis=1),
        "bias_band": v["rel_bias"][0][:, BAND],
        "ctxT": v["ctx_2"][0].T,
        "rope": rope_tables(),
        "lv": np.tile(v["diff_lambda_2"].reshape(1, 2, 256), (P, 1, 1)),

    }
    return {k: np.ascontiguousarray(a, dtype=np.float32) for k, a in arrays.items()}, first


def build(nc, shapes, first, stop=99, known=None):
    io = {k: nc.dram_tensor(k, shape, F32, kind="ExternalInput").ap() for k, shape in shapes.items()}
    io["outT"] = nc.dram_tensor("outT", (D, L), F32, kind="ExternalOutput").ap()
    with ExitStack() as ctx:
        C = Counts(nc, ctx, known)
        program(nc, ctx, io, C, first, shapes["panels"][0], stop)
    return C.labels


def kernel(**inputs):
    import concourse.bacc as bacc
    from concourse.bass_utils import run_bass_kernel_spmd

    arrays, first = lay_out(inputs)
    shapes = {k: a.shape for k, a in arrays.items()}
    counts = build(bacc.Bacc("TRN2", target_bir_lowering=False, num_devices=1), shapes, first)
    nc = bacc.Bacc("TRN2", target_bir_lowering=False, num_devices=1)
    build(nc, shapes, first, known=counts)
    r = run_bass_kernel_spmd(nc, [arrays], core_ids=[0])
    return np.ascontiguousarray(r.results[0]["outT"].T)[None]
```

```python
from contextlib import ExitStack, contextmanager
import math

import numpy as np
import concourse.bass as bass
from concourse import mybir

F32 = mybir.dt.float32
F32R = mybir.dt.float32r
ACT = mybir.ActivationFunctionType
ALU = mybir.AluOpType
AX = mybir.AxisListType

P = 128
D = 1024
KD = D // P
L = 512
LC = 256
TT = L + LC
FF1 = 2816
FF2 = 4096
CW = 256
EPS = 1e-6
PANEL = 2048
NM1 = 36
NM2 = 24
HEADS = 8
SCALE = 64 ** -0.5
GELU_C = math.sqrt(2.0 / math.pi)


def tiles_of(w, rows, cols):
    part = w[rows, :][:, cols] if not isinstance(cols, slice) else w[rows, cols]
    kt = part.shape[0] // P
    return part.reshape(kt, P, part.shape[1]).transpose(1, 0, 2).reshape(P, -1)


def full(flat):
    if flat.shape[1] == PANEL:
        return flat
    out = np.zeros((P, PANEL), np.float32)
    out[:, :flat.shape[1]] = flat
    return out


def up_gu(w, c, n):
    g = slice(c * CW + n * P, c * CW + (n + 1) * P)
    u = slice(FF1 + c * CW + n * P, FF1 + c * CW + (n + 1) * P)
    a = tiles_of(w, slice(0, D), g).reshape(P, KD, P)
    b = tiles_of(w, slice(0, D), u).reshape(P, KD, P)
    return np.concatenate([a, b], axis=2).reshape(P, PANEL)


def cols_panels(w, c0, c1):
    return [full(tiles_of(w, slice(0, D), slice(c, min(c + CW, c1)))) for c in range(c0, c1, CW)]


def rows_panels(w, c0, c1):
    return [full(tiles_of(w, slice(0, w.shape[0]), slice(c, c + 512))) for c in range(c0, c1, 512)]


def ffn_panels(wgu, wd):
    n = FF1 // CW
    up = [[up_gu(wgu, c, 0), up_gu(wgu, c, 1)] for c in range(n)]
    down = [tiles_of(wd, slice(c * CW, (c + 1) * CW), slice(0, D)) for c in range(n)]
    out = list(up[0])
    for c in range(1, n):
        out += up[c] + [down[c - 1]]
    return out + [down[n - 1]]


def mlp_panels(w1, w2):
    n = FF2 // CW
    out = cols_panels(w1, 0, CW)
    for c in range(1, n):
        out += cols_panels(w1, c * CW, (c + 1) * CW) + [tiles_of(w2, slice((c - 1) * CW, c * CW), slice(0, D))]
    return out + [tiles_of(w2, slice(FF2 - CW, FF2), slice(0, D))]


def dft_panels(n):
    a = 2 * np.pi * (np.outer(np.arange(n), np.arange(n)) % n) / n
    m = (np.concatenate([np.cos(a), -np.sin(a)], axis=1) / math.sqrt(64 * n)).astype(np.float32)
    return [full(tiles_of(m, slice(r, r + 2 * P), slice(0, 2 * n))) for r in range(0, n, 2 * P)]


PAIRED = np.concatenate([np.arange(64) + 64 * (4 * kv + g) for g in range(4) for kv in range(2)])


def mix2_panels(v, l):
    w = v["w_in_2"][l]

    def merge(gate0, wb):
        out = []
        for j in range(2):
            out += cols_panels(w, gate0 + 512 * j, gate0 + 512 * (j + 1)) + rows_panels(wb, 512 * j, 512 * (j + 1))
        return out

    ps = cols_panels(w, 0, 1024) + cols_panels(w, 1664, 2176) + merge(4480, v["w_br_diff_2"][l])
    ps += cols_panels(w, 1024, 1280) + cols_panels(w[:, 2176:2688][:, PAIRED], 0, 512)
    ps += merge(5504, v["w_br_gqa_2"][l][PAIRED, :])
    for n in range(3):
        ps += cols_panels(np.concatenate([w[:, 2688 + n * P:2688 + (n + 1) * P], w[:, 3072 + n * P:3072 + (n + 1) * P]], axis=1), 0, CW)
    ps += cols_panels(w, 1280, 1664) + dft_panels(L) + (dft_panels(LC) if l == 0 else [])
    ps += merge(3456, v["w_br_fourier_2"][l])
    return ps + merge(6528, v["w_br_conv_2"][l]) + cols_panels(v["w_out_2"][l], 0, D)


BAND = np.minimum(2 * P + np.arange(P)[:, None] - np.arange(2 * P)[None, :], 2 * P)


def rope_tables():
    t = np.arange(L)
    inv = (np.float32(10000.0) ** (-np.arange(16, dtype=np.float32) / np.float32(16))).astype(np.float32)
    ang = [np.outer(inv, p.astype(np.float32)) for p in (t // 64, t % 64)]
    cos = np.concatenate([np.cos(a) for a in ang for _ in range(2)])
    sin = np.concatenate([s * np.sin(a) for a in ang for s in (-1, 1)])
    return np.stack([np.tile(cos, (2, 1)), np.tile(sin, (2, 1))], axis=1)


def block_diagonal(w):
    out = np.zeros((P, KD, P), np.float32)
    for b in range(16):
        out[64 * (b % 2):64 * (b % 2) + 64, b // 2, 64 * (b % 2):64 * (b % 2) + 64] = w[b]
    return out


def columns(v):
    return np.asarray(v).reshape(-1, P).T


class Counts:

    def __init__(self, nc, ctx, known):
        self.nc, self.ctx, self.known = nc, ctx, known
        self.sems, self.count, self.labels, self.inside = {}, {}, {}, None

    def sem(self, kind):
        if kind not in self.sems:
            self.sems[kind] = self.ctx.enter_context(self.nc.semaphore("sm_" + kind))
            self.count[kind] = 0
        return self.sems[kind]

    def up(self, kind, key=None, by=1):
        s = self.sem(kind)
        self.count[kind] += by
        if key is not None:
            self.name(kind, key, kind, self.count[kind])
        return s, by

    def name(self, kind, key, sem_kind, value):
        assert (kind, key) not in self.labels, (kind, key)
        self.labels[(kind, key)] = (sem_kind, value)

    def start(self, kind, stage):
        self.sem(kind)
        self.name(kind, ("start", stage), kind, self.count[kind])

    def at(self, kind, key, plus=0):
        if self.known is None:
            return self.sem(kind), 1
        sem_kind, v = self.known[(kind, key)]
        out = v + plus
        assert not isinstance(out, int) or out > 0, (kind, key, plus)
        return self.sem(sem_kind), out

    @contextmanager
    def loop(self, eng, n):
        before = dict(self.count)
        with eng.Fori(0, n) as i:
            yield i
        for k, v in self.count.items():
            self.count[k] = v + (v - before.get(k, 0)) * (n - 1)


PAR_SIZES = [("b_ada", 72), ("b_mod", 96), ("norm_pre", 24), ("norm_post", 24), ("conv_w", 32), ("conv_b", 8),
             ("lru_ba", 8), ("lru_bx", 8), ("lru_lambda", 8), ("g_pre_mix", 16), ("g_post_mix", 16),
             ("g_pre_mlp", 16), ("g_post_mlp", 16), ("q_norm", 2), ("k_norm", 2), ("subln", 2), ("conv_dw", 186),
             ("conv_dw_b", 6), ("ln_g", 6), ("ln_b", 6), ("rb_far", 8), ("cond", 24)]
PAR = {n: sum(m for _, m in PAR_SIZES[:i]) for i, (n, _) in enumerate(PAR_SIZES)}
NPAR = sum(m for _, m in PAR_SIZES)
CST_SIZES = [("ident", 128), ("block", 128), ("dft64", 256)]
CST = {n: sum(m for _, m in CST_SIZES[:i]) for i, (n, _) in enumerate(CST_SIZES)}
NCST = sum(m for _, m in CST_SIZES)

N_FFN = 3 * (FF1 // CW)
N_MLP = 2 * (FF2 // CW)


class Mlp:

    def __init__(self, name, gated, T, first, mod0, mods):
        self.name, self.gated, self.T, self.p0, self.mod0 = name, gated, T, first, mod0
        self.C = (FF1 if gated else FF2) // CW
        self.UP = 2 if gated else 1
        self.H = 1 if T <= 512 else 2
        self.O = KD * self.H
        self.before, self.half, self.trips = mods
        self.rest = range(2 * self.trips + 1, self.C)
        self.per_trip = 2 * (self.UP + 1)


class Rows:

    def __init__(self, tag, T):
        self.tag, self.rows, self.units = tag, [], []
        self.ahead = 1 if tag == "d" else 2
        for t in range(4):
            for half in ((None,) if tag == "d" else (0, 1)):
                for g in range(1 if T <= L else 2):
                    self.units.append((t, half, g))
                    for i in (range(4) if g == 0 else range(4, 6)):
                        js = (0, 1) if half is None else (half,)
                        self.rows.append((len(self.units) - 1, i, js, 0 if g == 0 else L, TT))

    def __len__(self):
        return len(self.rows)

    def __getitem__(self, r):
        n, i, js, k0, k1 = self.rows[r]
        return self.units[n], i, js, k0, k1

    def unit(self, n):
        return self.units[n]

    def unit_no(self, r):
        return self.rows[r][0]

    def unit_start(self, r):
        return r == 0 or self.rows[r - 1][0] != self.rows[r][0]

    def unit_end(self, r):
        return r == len(self.rows) - 1 or self.rows[r + 1][0] != self.rows[r][0]

    def slot(self, j):
        return j if self.tag == "d" else 0

    def bank(self, r, j):
        return 2 * (j if self.tag == "d" else r % 2)

    def last_row_with(self, n, j):
        found = [r for r in range(len(self.rows)) if self.rows[r][0] < n and j in self.rows[r][2]]
        return found[-1] if found else None

    def last_unit_of(self, t):
        return max(n for n, u in enumerate(self.units) if u[0] == t)

    def query_event(self, X, t, g):
        q = "dq" if self.tag == "d" else "gq"
        if g == 1 and self.tag == "d":
            return "ctx_kept", X(q, t)
        return "roped", X(q, t)


def program(nc, ctx, io, C, first, n_panels, stop):
    sem, up, at, known = C.sem, C.up, C.at, C.known

    def sb(name, shape, dt=F32, stack=ctx):
        return stack.enter_context(nc.sbuf_tensor("b_" + name, [P] + shape, dt))

    raw = sb("raw", [2, PANEL])
    whi = sb("whi", [2, PANEL], F32R)
    wlo = sb("wlo", [2, PANEL], F32R)
    x = sb("x", [KD, TT])
    hhi = sb("hhi", [KD, TT], F32R)
    hlo = sb("hlo", [KD, TT], F32R)
    par = sb("par", [NPAR])
    cst = sb("cst", [NCST])
    ones = sb("ones", [P])
    mods = sb("mods", [2 * (NM1 + 2 * NM2), 2])
    csil = sb("csil", [3, KD])
    vec = sb("vec", [2, 4, KD])
    rstd = sb("rstd", [TT])
    small = sb("small", [96])
    arena = ExitStack()
    with arena as s:
        y = sb("y", [KD, TT], F32, s)
        with ExitStack() as s2:
            tmp = sb("tmp", [2, TT], F32, s2)
            dhi = sb("dhi", [2, 2, TT], F32R, s2)
            dlo = sb("dlo", [2, 2, TT], F32R, s2)
            mraw = sb("mraw", [2, PANEL], F32, s2)
            macc = sb("macc", [4, 2, CW], F32, s2)
        with ExitStack() as s2:
            sq = sb("sq", [2, TT], F32, s2)
            tn = sb("tn", [4, TT], F32, s2)
            hf = sb("hf", [3, TT], F32, s2)
        with ExitStack() as s2:
            xpad = sb("xpad", [2, L + 4], F32, s2)
            xc = sb("xc", [2, L], F32, s2)
            ga = sb("ga", [2, L], F32, s2)
            gx = sb("gx", [2, L], F32, s2)
            gm = sb("gm", [2, L], F32, s2)
            gy = sb("gy", [2, L], F32, s2)
            hs = sb("hs", [2, L], F32, s2)
            wbd = sb("wbd", [2, KD, P], F32, s2)
        with ExitStack() as s2:
            qf = sb("qf", [4, L], F32, s2)
            kf = sb("kf", [4, L], F32, s2)
            pr = sb("pr", [2, 4, L], F32, s2)
            pt = sb("pt", [4, L], F32, s2)
            qm = sb("qm", [2, L], F32, s2)
            bias = sb("bias", [2, 2 * P], F32, s2)
        with ExitStack() as s2:
            bhi = sb("bhi", [KD, L], F32R, s2)
            blo = sb("blo", [KD, L], F32R, s2)
            gate = sb("gate", [4, L], F32, s2)
    with ExitStack() as s:
        dk = sb("dk", [4, TT], F32, s)
        dv = sb("dv", [6, 512], F32, s)
        with ExitStack() as s2:
            qm2 = sb("qm2", [2, L], F32, s2)
            pr2 = sb("pr2", [2, 2, TT], F32, s2)
            gv = sb("gv", [6, P], F32, s2)
            rope = sb("rope", [2, L], F32, s2)
        with ExitStack() as s2:
            ch = sb("ch", [4, TT], F32R, s2)
            cl = sb("cl", [4, TT], F32R, s2)
            with ExitStack() as s3:
                aq = sb("aq", [4, TT], F32, s3)
                pt2 = sb("pt2", [6, L], F32, s3)
                gk = sb("gk", [1, TT], F32, s3)
            with ExitStack() as s3:
                gate2 = sb("gate2", [4, TT], F32, s3)
                sg = sb("sg", [2, TT], F32, s3)
            with ExitStack() as s3:
                uf = sb("uf", [2, TT], F32, s3)
                fh = sb("fh", [2, TT], F32R, s3)
                fl = sb("fl", [2, TT], F32R, s3)
                vp = sb("vp", [3, TT + 60], F32, s3)
        with ExitStack() as s2:
            sb("ch_in_use", [3, TT], F32, s2)
            cv = sb("cv", [TT], F32, s2)
            sb("cl_in_use", [3, TT], F32, s2)
            spare = sb("spare", [TT], F32, s2)
        with ExitStack() as s2:
            mh = sb("mh", [KD, TT], F32R, s2)
            ml = sb("ml", [KD, TT], F32R, s2)
        uf_tile = [uf[:, 0, :], uf[:, 1, :], spare[:, :]]
        sg_tile = [sg[:, 0, :], sg[:, 1, :], spare[:, :]]

    ps = ctx.enter_context(nc.psum_tensor("ps", [P, 8, 512], F32))

    def const(name):
        return cst[:, CST[name]:CST[name] + dict(CST_SIZES)[name]]

    def pcol(name, j, n=1):
        return par[:, PAR[name] + j:PAR[name] + j + n]

    def spans(T):
        return [(0, L), (L, TT)][:1 if T <= L else 2]

    def wide(bank, T):
        return ps[:, bank:bank + len(spans(T)), :].rearrange("p a n -> p (a n)")[:, 0:T]

    def lin(a, b, i):
        return a if i is None else i * b + a

    raw_loaded = [sem("raw_loaded0"), sem("raw_loaded1")]
    mod_loaded = [sem("mod_loaded0"), sem("mod_loaded1")]
    hi_ready, lo_ready, panel_used = sem("hi_ready"), sem("lo_ready"), sem("panel_used")
    mod_read, mod_used = sem("mod_read"), sem("mod_used")
    setup = sem("setup")

    first = {**{n: 10 ** 6 for n in ("mix1", "ffn2", "mix2", "mlp1", "mix3", "mlp2")}, **first}
    MLPS = {"ffn1": Mlp("ffn1", True, L, first["ffn1"], 8, (4, 2, 5)),
            "ffn2": Mlp("ffn2", True, L, first["ffn2"], 32, (4, 2, 5)),
            "mlp1": Mlp("mlp1", False, TT, first["mlp1"], 56, (0, 2, 7)),
            "mlp2": Mlp("mlp2", False, L, first["mlp2"], 84, (0, 0, 7))}

    LAYER, TOKENS = {"mix2": 0, "mix3": 1}, {"mix2": TT, "mix3": L}
    BRANCHES = ("d", "g", "f", "c")
    DFT_PANELS = [(0, 1, 2), (0, 1)]
    DV_BANK, GV_BANK = [4, 5, 6, 7, 4, 5], [2, 3, 4, 5, 2, 3]
    GQ_BANK = [2, 4, 0, 2]
    ROWS = lambda st, tag: Rows(tag, TOKENS[st])
    LAST_UNIT = {(st, tag): len(ROWS(st, tag).units) - 1 for st in LAYER for tag in "dg"}
    ROW_COL = lambda r, j: 72 + 8 * (r % 2) + j

    l0, l1 = 2 * NM1, 2 * (NM1 + NM2)
    NORMS = {
        "n0": (None, (L, 0, 8, ("norm_pre", 0))),
        "n1": ((L, 16, 0.5, ("norm_post", 0)), (L, 24, 32, ("norm_pre", 8))),
        "n2": ((L, 40, 1.0, ("norm_post", 8)), (L, 48, 56, ("norm_pre", 16))),
        "n3": ((L, 64, 0.5, ("norm_post", 16)), (TT, l0, l0 + 8, ("g_pre_mix", 0))),
        "n4": ((TT, l0 + 16, 1.0, ("g_post_mix", 0)), (TT, l0 + 24, l0 + 32, ("g_pre_mlp", 0))),
        "n5": ((TT, l0 + 40, 1.0, ("g_post_mlp", 0)), (TT, l1, l1 + 8, ("g_pre_mix", 8))),
        "n6": ((L, l1 + 16, 1.0, ("g_post_mix", 8)), (L, l1 + 24, l1 + 32, ("g_pre_mlp", 8))),
        "n7": ((L, l1 + 40, 1.0, ("g_post_mlp", 8)), None),
    }
    SUM_BANK = {"post": 0, "pre": 2}
    MOD_NEED = {"n0": [(0, 16, 8)], "n1": [(16, 64, 32)], "n3": [(64, 72, 36), (72, 112, 56)], "n5": [(112, 168, 84)]}
    GROUPS = [(0, L), (L, TT)]

    def next_panel(norm):
        return first[NEXT[norm]]

    def groups(T):
        return [g for g in enumerate(GROUPS) if g[1][1] <= T]

    ORDER = ["n0", "ffn1", "n1", "mix1", "n2", "ffn2", "n3", "mix2", "n4", "mlp1", "n5", "mix3", "n6", "mlp2", "n7"][:stop]
    NEXT = {"n0": "ffn1", "n1": "mix1", "n2": "ffn2", "n3": "mix2", "n4": "mlp1", "n5": "mix3", "n6": "mlp2"}
    LAST_NORM = [s for s in ORDER if s in NORMS][-1]

    block = ctx.enter_context(nc.Block())

    @block.sync
    def _(sp):
        sp.dma_start(par[:, :], io["par"]).then_inc(setup, 16)
        sp.dma_start(x[:, :, 0:L], io["xT"].rearrange("(k p) t -> p k t", p=P)).then_inc(setup, 16)
        sp.dma_start(raw[:, 0, :], io["panels"][0]).then_inc(raw_loaded[0], 16)
        sp.dma_start(raw[:, 1, :], io["panels"][1]).then_inc(raw_loaded[1], 16)
        sp.dma_start(cst[:, :], io["cst"]).then_inc(setup, 16)
        with sp.Fori(1, n_panels // 2) as i:
            for s in range(2):
                sp.wait_ge(lo_ready, i * 2 + (s - 1))
                sp.dma_start(raw[:, s, :], io["panels"][i * 2 + s]).then_inc(raw_loaded[s], 16)
        for k in range(KD):
            sp.wait_ge(*at("x_new", (LAST_NORM, k)))
            sp.dma_start(io["outT"][k * P:(k + 1) * P, :], x[:, k, 0:L]).then_inc(sem("stored"), 16)
        sp.wait_ge(sem("stored"), 16 * KD)

    @block.gpsimd
    def _(pool):
        with pool.Fori(0, n_panels // 2) as i:
            for s in range(2):
                pool.wait_ge(hi_ready, i * 2 + (s + 1))
                pool.tensor_tensor(wlo[:, s, :], raw[:, s, :], whi[:, s, :].bitcast(F32), ALU.subtract).then_inc(lo_ready, 1)

    @block.scalar
    def _(act):
        already_split = set()

        def split(p, i=None, by=0):
            if p >= n_panels or (i is None and p in already_split):
                return
            already_split.add(p)
            act.wait_ge(raw_loaded[p % 2], lin(16 * (p // 2 + 1), 8 * by, i))
            if p >= 2:
                act.wait_ge(panel_used, lin(p - 1, by, i))
            act.activation(whi[:, p % 2, :], raw[:, p % 2, :], ACT.Copy).then_inc(hi_ready, 1)

        def mod_load(k, i=None, by=0):
            if k >= 2:
                act.wait_ge(mod_read, lin(k - 1, by, i))
            act.dma_start(mraw[:, k % 2, :], io["mod_panels"][lin(k, by, i)]).then_inc(mod_loaded[k % 2], 16)

        def squares(st, what, src, T):
            for k in range(KD):
                act.wait_ge(*at("src", (st, what, k)))
                if (st, what, k) == ("n3", "pre", 0):
                    act.wait_ge(*at("ctx_loaded", "all"))
                if k >= 2:
                    act.wait_ge(*at("sq_used", (st, what, k - 2)))
                act.activation(sq[:, k % 2, 0:T], src[:, k, 0:T], ACT.Square).then_inc(*up("sq", (st, what, k)))

        def root(st, what, T):
            act.wait_ge(*at("ms", (st, what)))
            act.activation(rstd[:, 0:T], rstd[:, 0:T], ACT.Sqrt).then_inc(*up("root", (st, what)))

        def norm(st):
            post, pre = NORMS[st]
            if post:
                squares(st, "post", y, post[0])
                if pre:
                    split(next_panel(st) + 1)
                root(st, "post", post[0])
            if pre:
                T = pre[0]
                if post:
                    squares(st, "pre", x, T)
                    root(st, "pre", T)
                v = vec[:, int(st[1]) % 2, :, :]
                for k in range(KD):
                    act.wait_ge(*at("normed", (st, k)))
                    if k >= 3:
                        act.wait_ge(*at("h_lo", (st, k - 3)))
                    for dst, kind in ((hhi[:, k, :], "h_hi"), (hf[:, k % 3, :], "hf")):
                        for g, (a, b) in groups(T):
                            act.activation(dst[:, a:b], tn[:, k % 4, a:b], ACT.Identity,
                                           bias=mods[:, pre[1] + k, g:g + 1],
                                           scale=v[:, 2 + g, k:k + 1]).then_inc(*up(kind, (st, k, g)))

        def mlp(m):
            st, T = m.name, m.T
            for kind in ("acted", "hid_hi"):
                C.start(kind, st)

            def units(c, p, i=None):
                for n in range(2):
                    if m.gated or n == 0:
                        split(p + n + 1, i, m.per_trip)
                    if m.gated or n == 1:
                        act.wait_ge(panel_used, lin(p + (n if m.gated else 0) + 1, m.per_trip, i))
                    else:
                        act.wait_ge(*at("up_first", ("start", st), lin(c + 1, 2, i)))
                    if c >= 1:
                        act.wait_ge(*at("hid_lo", ("start", st), lin(2 * (c - 1) + n + 1, 4, i)))
                    if m.gated:
                        act.activation(tmp[:, n, 0:T], ps[:, 2 * n, 0:T], ACT.Silu).then_inc(*up("acted"))
                    else:
                        act.activation(tmp[:, n, 0:T], wide(2 * n, T), ACT.Relu).then_inc(*up("acted"))
                    act.wait_ge(*at("hid", ("start", st), lin(2 * c + n + 1, 4, i)))
                    if c >= 2:
                        act.wait_ge(panel_used, lin(down_panel(m, c - 2) + 1, m.per_trip, i))
                    elif i is not None:
                        act.wait_ge(panel_used, lin(p, m.per_trip, i))
                    act.activation(dhi[:, c % 2, n, 0:T], tmp[:, n, 0:T], ACT.Copy).then_inc(*up("hid_hi"))

            k = m.mod0
            for v in range(m.before):
                mod_load(k + v)
            units(0, m.p0)
            k += m.before
            with C.loop(act, m.trips) as i:
                for u in range(2):
                    p = m.p0 + m.UP + u * (m.UP + 1)
                    for v in range(m.half):
                        mod_load(k + u * m.half + v, i, 2 * m.half)
                    units(1 + u, p, i)
                    split(p + m.UP + 1, i, m.per_trip)
            for c in m.rest:
                p = m.p0 + m.UP + (c - 1) * (m.UP + 1)
                units(c, p)
                split(p + m.UP + 1)
            split(m.p0 + m.UP * m.C + m.C)

        mod_load(0)
        mod_load(1)
        act.wait_ge(setup, 16 * 3)
        act.activation(csil[:, :, :].rearrange("p a k -> p (a k)"), pcol("cond", 0, 24), ACT.Silu).then_inc(*up("csil", "all"))
        squares("n0", "pre", x, L)
        mod_load(2)
        mod_load(3)
        split(0)
        split(1)
        root("n0", "pre", L)
        for k in range(4, 8):
            mod_load(k)

        def mix1():
            p0 = first["mix1"]
            act.wait_ge(*at("h_lo", ("n1", KD - 1)))
            act.dma_start(wbd[:, :, :, :].rearrange("p a k n -> p (a k n)"),
                          io["wbd"].rearrange("p a k n -> p (a k n)")).then_inc(*up("wbd", "all", 16))
            act.wait_ge(*at("lam", "abs"))
            act.activation(small[:, 24:32], small[:, 16:24], ACT.Exp, scale=-1.0).then_inc(*up("lam_exp", "all"))
            for r in range(4):
                p = p0 + 2 * r
                split(p + 1)
                for n in range(2):
                    act.wait_ge(*at("out", (p, n)))
                    if r == 0:
                        act.wait_ge(*at("xpad", n))
                    else:
                        act.wait_ge(*at("xc", (r - 1, n)))
                    act.activation(xpad[:, n, 3:3 + L], ps[:, n, :], ACT.Copy).then_inc(*up("xcopy", (r, n)))
                split(p + 2)
                for n in range(2):
                    act.wait_ge(*at("out", (p + 1, n)))
                    if r >= 1:
                        act.wait_ge(*at("rec", (r - 1, n)))
                    act.activation(gy[:, n, :], ps[:, 2 + n, :], ACT.Gelu_apprx_tanh).then_inc(*up("gelu", (r, n)))
                for n in range(2):
                    j = 2 * r + n
                    act.wait_ge(*at("gates", (r, n)))
                    act.activation(ga[:, n, :], ps[:, 4 + n, :], ACT.Sigmoid, bias=pcol("lru_ba", j)).then_inc(*up("ga", (r, n)))
                    act.activation(gx[:, n, :], ps[:, 6 + n, :], ACT.Sigmoid, bias=pcol("lru_bx", j)).then_inc(*up("gx", (r, n)))
                for n in range(2):
                    act.wait_ge(*at("exponent", (r, n)))
                    act.activation(gm[:, n, :], ga[:, n, :], ACT.Tanh).then_inc(*up("tanh", (r, n)))
                    act.wait_ge(*at("tanh", (r, n)))
                    act.activation(ga[:, n, :], ga[:, n, :], ACT.Exp, scale=-1.0).then_inc(*up("decay", (r, n)))
                for n in range(2):
                    act.wait_ge(*at("one_less_a2", (r, n)))
                    act.activation(gm[:, n, :], gm[:, n, :], ACT.Sqrt).then_inc(*up("mult", (r, n)))
            p = p0 + 8
            act.wait_ge(*at("rec", (3, 1)))
            for a in range(2):
                split(p + a + 1)
                for n in range(2):
                    act.wait_ge(*at("out", (p + a, n)))
                    act.activation(qf[:, 2 * a + n, :], ps[:, 2 * a + n, :], ACT.Copy).then_inc(*up("q", 2 * a + n))
            split(p + 3)
            split(p + 4)
            for a in range(2):
                split(p + 5 + a)
                for t in range(4):
                    act.wait_ge(*at("out", (p + 4 + a, t)))
                    act.activation(x[:, 2 * t + a, L:TT], ps[:, t + 4 * a, 0:CW], ACT.Copy).then_inc(*up("v", (a, t)))

            def load_bias(h):
                if h >= 2:
                    act.wait_ge(*at("biased", (h - 2, 3)))
                act.dma_start(bias[:, h % 2, :], io["bias_band"][h]).then_inc(*up(f"bias{h % 2}", h, 16))

            def exps(u):
                for i in range(4):
                    act.wait_ge(*at("max", (u, i)))
                    s = pr[:, u % 2, i, 0:(i + 1) * P]
                    act.activation(s, s, ACT.Exp, bias=small[:, 32 + 4 * (u % 2) + i:33 + 4 * (u % 2) + i],
                                   accum_out=small[:, 40 + 4 * (u % 2) + i:41 + 4 * (u % 2) + i]).then_inc(*up("exp", (u, i)))

            def keep_transposed(u):
                for j in range(4):
                    act.wait_ge(*at("tr", (u, j)))
                    if u >= 1:
                        act.wait_ge(*at("pv", u - 1))
                    act.activation(pt[:, j, j * P:L], ps[:, 4 * (u % 2) + j, j * P:L], ACT.Copy).then_inc(*up("pt", (u, j)))

            load_bias(0)
            load_bias(1)
            exps(0)
            exps(1)
            for u in range(HEADS):
                if u + 2 < HEADS:
                    load_bias(u + 2)
                keep_transposed(u)
                if u + 2 < HEADS:
                    exps(u + 2)
            act.wait_ge(*at("pv", HEADS - 1))
            act.dma_start(x[:, :, L:TT], io["ctxT"].rearrange("(k p) t -> p k t", p=P)).then_inc(*up("ctx_loaded", "all", 16))
            for k in range(KD):
                act.activation(bhi[:, k, :], y[:, k, 0:L], ACT.Copy).then_inc(*up("bhi", ("rec", k)))
            for j in range(2):
                p = p0 + 14 + 7 * j
                for b, q in (("a", p), ("r", p + 3)):
                    for a in range(2):
                        split(q + a + 1)
                        for n in range(2):
                            t = 2 * a + n
                            act.wait_ge(*at("out", (q + a, n)))
                            prev = ("a" if b == "r" else "r", j if b == "r" else j - 1)
                            if prev[1] >= 0:
                                act.wait_ge(*at("merged", (prev[1], prev[0], t)))
                            act.activation(gate[:, t, :], ps[:, t, :], ACT.Sigmoid).then_inc(*up("gate", (j, b, t)))
                    split(q + 3)
                    if b == "r":
                        split(q + 4)
            p = p0 + 28
            act.wait_ge(panel_used, p)
            for k in range(KD):
                act.wait_ge(*at("merged", (k // 4, "r", k % 4)))
                act.activation(bhi[:, k, :], y[:, k, 0:L], ACT.Copy).then_inc(*up("bhi", ("out", k)))
            for a in range(4):
                split(p + a + 1)
                for n in range(2):
                    k = 2 * a + n
                    act.wait_ge(*at("out", (p + a, n)))
                    act.activation(y[:, k, 0:L], ps[:, k % 4, :], ACT.Copy).then_inc(*up("src", ("n2", "post", k)))

        def mix2(st):
            X = lambda *k: (st,) + k
            l, T, p0 = LAYER[st], TOKENS[st], first[st]
            norm_before = "n3" if l == 0 else "n5"
            panel = [p0]

            def next_split():
                panel[0] += 1
                split(panel[0])

            def keep_hi(tag, nt, dst, src):
                for k in range(nt):
                    act.wait_ge(*at("ready", X(tag, k)))
                    act.activation(dst[:, k, 0:T], src(k), ACT.Copy).then_inc(*up("c_hi", X(tag, k)))

            def gates(tag, j):
                for a in range(2):
                    next_split()
                    for n in range(2):
                        t = 2 * a + n
                        act.wait_ge(*at("out", (panel[0] - 1, n)))
                        if (tag, j) != ("d", 0):
                            act.wait_ge(*at("gated", X(*((tag, 0) if j else (BRANCHES[BRANCHES.index(tag) - 1], 1)), t)))
                        if tag in "dg" and (j, t) == (0, 0):
                            act.wait_ge(*at("c_lo", X(tag, 3)))
                        act.activation(gate2[:, t, 0:T], wide(2 * t % 4, T), ACT.Sigmoid).then_inc(*up("gate", X(tag, j, t)))
                next_split()

            def keep_conv(n):
                act.wait_ge(*at("conv", X(n)))
                act.activation(vp[:, n, 0:T], cv[:, 0:T], ACT.Copy).then_inc(*up("conv_kept", X(n)))

            def row_exps(rows, r):
                u, i, js, k0, k1 = rows[r]
                for j in js:
                    c = ROW_COL(r, j)
                    act.wait_ge(*at("nmax", X(rows.tag, r, j)))
                    act.wait_ge(*at("scores", X(rows.tag, r, j)))
                    if r >= 2:
                        act.wait_ge(*at("tr", X(rows.tag, r - 2)))
                    b = rows.bank(r, j)
                    s = ps[:, b:b + 2, :].rearrange("p a n -> p (a n)")[:, k0:k1] if k0 == 0 else ps[:, b, 0:k1 - k0]
                    act.activation(pr2[:, r % 2, rows.slot(j), 0:k1 - k0], s, ACT.Exp, bias=small[:, c:c + 1], scale=SCALE,
                                   accum_out=small[:, c + 4:c + 5]).then_inc(*up("exp", X(rows.tag, r, j)))

            def keep_output(rows, r):
                uno = rows.unit_no(r)
                t, half, g = rows.unit(uno)
                o = slice(0, P) if half is None else slice(64 * half, 64 * half + 64)
                a, b = GROUPS[g]
                act.wait_ge(*at("pv", X(rows.tag, uno)))
                act.wait_ge(*at("qm", X(rows.tag, uno)))
                act.activation(aq[o, t, a:b], ps[o, 6 + uno % 2, 0:b - a], ACT.Copy).then_inc(*up("kept", X(rows.tag, uno)))

            def attention(rows):
                for r in range(rows.ahead):
                    row_exps(rows, r)
                for r in range(len(rows)):
                    if rows.ahead == 1 and r + 1 < len(rows):
                        row_exps(rows, r + 1)
                    if r >= 1 and rows.unit_end(r - 1):
                        keep_output(rows, r - 1)
                    u, i, js, k0, k1 = rows[r]
                    act.wait_ge(*at("tr", X(rows.tag, r)))
                    if rows.unit_start(r) and rows.unit_no(r) >= 1:
                        act.wait_ge(*at("pv", X(rows.tag, rows.unit_no(r) - 1)))
                    n = (k1 - k0) // P
                    q0 = (i % 4) * P
                    src = ps[:, 4:6, :].rearrange("p a n -> p (a n)")[:, 0:k1 - k0].rearrange("p (k q) -> p k q", q=P)
                    act.activation(pt2[:, 0:n, q0:q0 + P], src, ACT.Copy).then_inc(*up("pt", X(rows.tag, r)))
                    if rows.ahead == 2 and r + 2 < len(rows):
                        row_exps(rows, r + 2)
                keep_output(rows, len(rows) - 1)

            def head_norm(tag, src, T, source, free):
                head_squares(tag, src, T, source, free)
                head_root(tag, T)

            def head_squares(tag, src, T, source, free):
                act.wait_ge(*at(*source))
                act.wait_ge(*at(*free))
                act.activation(pr2[:, 0, 0, 0:T], src, ACT.Square).then_inc(*up("hsq", X(tag)))

            def head_root(tag, T):
                act.wait_ge(*at("hms", X(tag)))
                act.activation(rstd[:, 0:T], rstd[:, 0:T], ACT.Sqrt).then_inc(*up("hroot", X(tag)))

            act.wait_ge(*at("h_lo", (norm_before, KD - 1)))
            act.dma_start(rope[:, :, :], io["rope"]).then_inc(*up("rope", st, 16))
            act.dma_start(pr2[:, 0, 0, 0:256], io["lv"][:, l, :]).then_inc(*up("lv", st, 16))
            act.wait_ge(*at("lv_sums", st))
            act.activation(small[:, 66:68], small[:, 64:66], ACT.Exp).then_inc(*up("lv_exp", st))
            for a in range(2):
                next_split()
                for n in range(2):
                    act.wait_ge(*at("out", (panel[0] - 1, n)))
                    act.wait_ge(*at("roped", X("dk", 2 * a + n)))
                    act.activation(dk[:, 2 * a + n, L:TT], ps[:, 2 * (2 * a + n) % 4 + 1, 0:LC], ACT.Copy)\
                       .then_inc(*up("ctx_kept", X("dk", 2 * a + n)))
            for a in range(2):
                next_split()
                for t in range(6):
                    act.wait_ge(*at("out", (panel[0] - 1, t)))
                    act.activation(dv[:, t, a * CW:(a + 1) * CW], ps[:, DV_BANK[t], 0:CW], ACT.Copy).then_inc(*up("dv", X(a, t)))
            for a in range(2):
                next_split()
                for n in range(2 if T > L else 0):
                    act.wait_ge(*at("roped", X("dq", 2 * a + n)))
                    act.activation(aq[:, 2 * a + n, L:TT], ps[:, 2 * (2 * a + n) % 4 + 1, 0:LC], ACT.Copy)\
                       .then_inc(*up("ctx_kept", X("dq", 2 * a + n)))
            rows = ROWS(st, "d")
            attention(rows)
            for t in range(4):
                head_norm(("sub", t), aq[:, t, 0:T], T, ("kept", X("d", rows.last_unit_of(t))),
                          ("hsum", X(("sub", t - 1))) if t else ("tr", X("d", len(rows) - 1)))
            keep_hi("d", 4, ch, lambda k: aq[:, k, 0:T])
            gates("d", 0)
            gates("d", 1)
            act.wait_ge(*at("out", (p0 + 11, 3)))
            act.dma_start(rope[:, :, :], io["rope"]).then_inc(*up("rope2", st, 16))
            next_split()
            head_squares(("gk", 0), wide(0, TT), TT, ("out", (panel[0] - 1, 0)), ("out", (p0 + 11, 3)))
            for t in range(6):
                act.wait_ge(*at("out", (panel[0] - 1, 1 + t)))
                act.activation(gv[:, t, :], ps[:, GV_BANK[t], 0:P], ACT.Copy).then_inc(*up("gv", X(t)))
            head_root(("gk", 0), TT)
            for a in range(2):
                next_split()
                for n in range(2):
                    t = 2 * a + n
                    head_norm(("gq", t), wide(GQ_BANK[t], T), T, ("out", (panel[0] - 1, n)),
                              ("hsum", X(("gq", t - 1) if t else ("gk", 0))))
            rows = ROWS(st, "g")
            attention(rows)
            for t in range(4):
                C.name("ready", X("g", t), *C.labels[("kept", X("g", rows.last_unit_of(t)))])
            keep_hi("g", 4, ch, lambda k: aq[:, k, 0:T])
            gates("g", 0)
            gates("g", 1)
            for n in range(3):
                next_split()
                act.wait_ge(*at("out", (panel[0] - 1, 1)))
                act.activation(sg_tile[n][:, 0:T], wide(4 * (n % 2) + 2, T), ACT.Sigmoid).then_inc(*up("sg", X(n)))
            for a in range(2):
                next_split()
                for n in range(2 - a):
                    t = 2 * a + n
                    act.wait_ge(*at("out", (panel[0] - 1, n)))
                    if t == 0:
                        act.wait_ge(*at("gated", X("g", 1, 3)))
                    if t == 2:
                        act.wait_ge(*at("vp", X(2)))
                    act.activation(uf_tile[t][:, 0:T], wide(2 * t % 4, T), ACT.Copy).then_inc(*up("uf", X(t)))
            keep_conv(0)
            for g, (a, b) in groups(T):
                for t in range(a // P, b // P):
                    if (t - a // P) % 2 == 1:
                        next_split()
                    act.wait_ge(*at("grouped", X(t)))
                    if t >= 2:
                        act.wait_ge(*at("slot_read", X(t - 2)))
                    act.activation(fh[:, t % 2, :], wide(2 * (t % 2), TT), ACT.Copy).then_inc(*up("fh", X(t)))
                for f in range(3):
                    act.wait_ge(*at("mixed", X(g, f)))
                    act.activation(ch[:, f, a:b], ps[:, 4 + f, 0:b - a], ACT.Copy).then_inc(*up("yf_hi", X(g, f)))
            keep_conv(1)
            gates("f", 0)
            keep_conv(2)
            for n in range(3):
                act.wait_ge(*at("centred", X(n)))
                act.activation(sg_tile[n][:, 0:T], vp[:, n, 0:T], ACT.Square).then_inc(*up("csq", X(n)))
            gates("f", 1)
            act.wait_ge(*at("cvar", X()))
            act.activation(rstd[:, 0:T], rstd[:, 0:T], ACT.Sqrt).then_inc(*up("croot", X()))
            for n in range(3):
                act.wait_ge(*at("cnormed", X(n)))
                act.activation(vp[:, n, 0:T], vp[:, n, 0:T], ACT.Silu, bias=pcol("ln_b", 3 * l + n),
                               scale=pcol("ln_g", 3 * l + n)).then_inc(*up("ready", X("c", n)))
            act.wait_ge(panel_used, panel[0])
            keep_hi("c", 3, ch, lambda k: vp[:, k, 0:T])
            gates("c", 0)
            gates("c", 1)
            act.wait_ge(panel_used, panel[0])
            for k in range(KD):
                act.wait_ge(*at("gated", X("c", k // 4, k % 4)))
                act.activation(mh[:, k, 0:T], y[:, k, 0:T], ACT.Copy).then_inc(*up("c_hi", X("out", k)))
            nxt = "n4" if l == 0 else "n6"
            for a in range(4):
                next_split()
                for n in range(2):
                    k = 2 * a + n
                    act.wait_ge(*at("out", (panel[0] - 1, n)))
                    act.activation(y[:, k, 0:T], wide(2 * k % 4, T), ACT.Copy).then_inc(*up("src", (nxt, "post", k)))

        def mix_act(st):
            if st == "mix1":
                mix1()
            else:
                mix2(st)

        for st in ORDER:
            if st in NORMS:
                norm(st)
            elif st in MLPS:
                mlp(MLPS[st])
            else:
                mix_act(st)

    @block.vector
    def _(dve):
        def chain(ins):
            ins.then_inc(*up("chain", ("n", C.count.get("chain", 0))))
            dve.wait_ge(sem("chain"), C.count["chain"])

        def mean_square(st, what, T):
            dve.wait_ge(*at("sq_used", (st, what, KD - 1)))
            dve.tensor_scalar(rstd[:, 0:T], wide(SUM_BANK[what], T), 1.0 / D, EPS, ALU.mult, ALU.add)\
               .then_inc(*up("ms", (st, what)))
            dve.wait_ge(*at("root", (st, what)))
            dve.reciprocal(rstd[:, 0:T], rstd[:, 0:T]).then_inc(*up("rstd", (st, what)))
            dve.wait_ge(*at("rstd", (st, what)))

        def mod(k, i=None, by=0):
            dve.wait_ge(mod_loaded[k % 2], lin(16 * (k // 2 + 1), 8 * by, i))
            if k >= 4:
                dve.wait_ge(mod_used, lin(k - 3, by, i))
            conds = (0,) if k < NM1 else (1, 2)
            C.start("mod_part", (k,))
            n = 0
            for j in range(KD):
                for c, cond in enumerate(conds):
                    w, s = mraw[:, k % 2, j * CW:(j + 1) * CW], csil[:, cond, j:j + 1]
                    acc = macc[:, k % 4, c, :]
                    if j == 0:
                        ins = dve.tensor_scalar(acc, w, s, None, ALU.mult)
                    else:
                        dve.wait_ge(*at("mod_part", ("start", (k,)), lin(n - len(conds) + 1, by * (KD * len(conds) - 1), i)))
                        ins = dve.scalar_tensor_tensor(acc, w, s, acc, ALU.mult, ALU.add)
                    n += 1
                    if n < KD * len(conds):
                        ins.then_inc(*up("mod_part"))
            ins.then_inc(mod_read, 1)

        def norm(st):
            post, pre = NORMS[st]
            v = vec[:, int(st[1]) % 2, :, :]
            for t0, t1, n in MOD_NEED.get(st, ()):
                dve.wait_ge(mod_used, n)
                name, b0 = ("b_ada", t0) if t0 < 72 else ("b_mod", t0 - 72)
                for c in range(1 if t0 < 72 else 2):
                    chain(dve.tensor_tensor(mods[:, t0:t1, c], ps[:, 7, 2 * t0 + c:2 * t1 + c:2],
                                            pcol(name, b0, t1 - t0), ALU.add))
            if post:
                T, tg, factor, (gain, j) = post
                for g, _ in groups(T):
                    chain(dve.scalar_tensor_tensor(v[:, g, :], mods[:, tg:tg + KD, g], factor,
                                                   pcol(gain, j, KD), ALU.mult, ALU.mult))
            if pre:
                T, _, tsc, (gain, j) = pre
                for g, _ in groups(T):
                    chain(dve.scalar_tensor_tensor(v[:, 2 + g, :], mods[:, tsc:tsc + KD, g], 1.0,
                                                   pcol(gain, j, KD), ALU.add, ALU.mult))
            if post:
                T = post[0]
                mean_square(st, "post", T)
                for k in range(KD + 1):
                    if k < KD:
                        dve.tensor_tensor(y[:, k, 0:T], y[:, k, 0:T], rstd[:, 0:T], ALU.mult)\
                           .then_inc(*up("ynormed", (st, k)))
                    if k >= 1:
                        dve.wait_ge(*at("ynormed", (st, k - 1)))
                        gs = groups(T)
                        for g, (a, b) in gs:
                            ins = dve.scalar_tensor_tensor(x[:, k - 1, a:b], y[:, k - 1, a:b],
                                                           v[:, g, k - 1:k], x[:, k - 1, a:b], ALU.mult, ALU.add)
                            ins.then_inc(*up("x_new", (st, k - 1, g)))
                        C.name("x_new", (st, k - 1), *C.labels[("x_new", (st, k - 1, gs[-1][0]))])
                        C.name("src", (st, "pre", k - 1), *C.labels[("x_new", (st, k - 1))])
            if pre:
                T = pre[0]
                if post:
                    mean_square(st, "pre", T)
                for k in range(KD + 2):
                    if k < KD:
                        dve.tensor_tensor(tn[:, k % 4, 0:T], x[:, k, 0:T], rstd[:, 0:T], ALU.mult)\
                           .then_inc(*up("normed", (st, k)))
                    if k >= 2:
                        dve.wait_ge(*at("hf", (st, k - 2, groups(T)[-1][0])))
                        dve.tensor_tensor(hlo[:, k - 2, 0:T], hf[:, (k - 2) % 3, 0:T],
                                          hhi[:, k - 2, 0:T].bitcast(F32), ALU.subtract).then_inc(*up("h_lo", (st, k - 2)))

        def mlp(m):
            st, T, O = m.name, m.T, m.O
            for kind in ("hid", "hid_lo", "added"):
                C.start(kind, st)
            for k in range(KD):
                for a, b in spans(T):
                    dve.memset(y[:, k, a:b], 0.0).then_inc(*up("added"))

            def units(c, i=None):
                for n in range(2):
                    e = lin(2 * c + n + 1, 4, i)
                    dve.wait_ge(*at("acted", ("start", st), e))
                    if m.gated:
                        dve.tensor_tensor(tmp[:, n, 0:T], tmp[:, n, 0:T], ps[:, 2 * n + 1, 0:T], ALU.mult)\
                           .then_inc(*up("hid"))
                    else:
                        dve.tensor_tensor(tmp[:, n, 0:T], tmp[:, n, 0:T], wide(2 * n, T), ALU.mult)\
                           .then_inc(*up("hid"))
                    dve.wait_ge(*at("hid_hi", ("start", st), e))
                    dve.tensor_tensor(dlo[:, c % 2, n, 0:T], tmp[:, n, 0:T],
                                      dhi[:, c % 2, n, 0:T].bitcast(F32), ALU.subtract).then_inc(*up("hid_lo"))

            def add(c, i=None):
                for o in range(O):
                    if o < O - 1:
                        dve.wait_ge(*at("down", ("start", st), lin((O - 1) * c + o + 1, 2 * (O - 1), i)))
                    else:
                        dve.wait_ge(panel_used, lin(down_panel(m, c) + 1, m.per_trip, i))
                    dve.wait_ge(*at("added", ("start", st), lin(O * c + o + 1, 2 * O, i)))
                    a, b = spans(T)[o % m.H]
                    dst = y[:, o // m.H, a:b]
                    dve.tensor_tensor(dst, ps[:, 4 + o % 3, 0:b - a], dst, ALU.add).then_inc(*up("added"))

            k = m.mod0
            for v in range(m.before):
                mod(k + v)
            units(0)
            k += m.before
            with C.loop(dve, m.trips) as i:
                for u in range(2):
                    for v in range(m.half):
                        mod(k + u * m.half + v, i, 2 * m.half)
                    units(1 + u, i)
                    add(u, i)
            for c in m.rest:
                units(c)
                add(c - 1)
            add(m.C - 1)
            nxt = ORDER[ORDER.index(st) + 1] if ORDER.index(st) + 1 < len(ORDER) else None
            for k in range(KD):
                C.name("src", (nxt, "post", k), "added", C.count["added"] - O + (k + 1) * m.H)

        dve.memset(ones[:, :], 1.0).then_inc(*up("ones", "all"))
        for k in range(KD):
            C.name("src", ("n0", "pre", k), "setup", 16 * 3)
        dve.wait_ge(*at("csil", "all"))
        mod(0)
        mod(1)
        mean_square("n0", "pre", L)
        for k in range(2, 8):
            mod(k)

        def softplus_of_minus_lambda():
            lam = pcol("lru_lambda", 0, KD)
            s8, neg, ab, e, s, s2, q = [small[:, KD * i:KD * (i + 1)] for i in range(7)]
            chain(dve.tensor_scalar(neg, lam, -1.0, None, ALU.mult))
            dve.tensor_tensor(ab, lam, neg, ALU.max).then_inc(*up("lam", "abs"))
            dve.wait_ge(*at("lam_exp", "all"))
            chain(dve.tensor_scalar(s, e, 2.0, None, ALU.add))
            chain(dve.reciprocal(s, s))
            chain(dve.tensor_tensor(s, s, e, ALU.mult))
            chain(dve.tensor_tensor(s2, s, s, ALU.mult))
            chain(dve.tensor_scalar(q, s2, 1.0 / 17, None, ALU.mult))
            for n in (15, 13, 11, 9, 7, 5, 3):
                chain(dve.scalar_tensor_tensor(q, q, 1.0 / n, s2, ALU.add, ALU.mult))
            chain(dve.scalar_tensor_tensor(q, q, 1.0, s, ALU.add, ALU.mult))
            chain(dve.tensor_scalar(neg, neg, 0.0, 8.0, ALU.max, ALU.mult))
            chain(dve.scalar_tensor_tensor(s8, q, 16.0, neg, ALU.mult, ALU.add))

        def mix1():
            softplus_of_minus_lambda()
            for n in range(2):
                dve.memset(xpad[:, n, 0:4], 0.0).then_inc(*up("xpad", n))
            for r in range(4):
                for n in range(2):
                    j = 2 * r + n
                    dve.wait_ge(*at("xcopy", (r, n)))
                    if r >= 1:
                        dve.wait_ge(*at("gates", (r - 1, n)))
                        dve.wait_ge(*at("gated_in", (r - 1, n)))
                    chain(dve.tensor_scalar(xc[:, n, :], xpad[:, n, 0:L], pcol("conv_w", j), pcol("conv_b", j),
                                            ALU.mult, ALU.add))
                    for t in range(1, 4):
                        ins = dve.scalar_tensor_tensor(xc[:, n, :], xpad[:, n, t:t + L], pcol("conv_w", KD * t + j),
                                                       xc[:, n, :], ALU.mult, ALU.add)
                        if t < 3:
                            chain(ins)
                    ins.then_inc(*up("xc", (r, n)))
                for n in range(2):
                    j = 2 * r + n
                    dve.wait_ge(*at("ga", (r, n)))
                    dve.tensor_scalar(ga[:, n, :], ga[:, n, :], small[:, j:j + 1], None, ALU.mult)\
                       .then_inc(*up("exponent", (r, n)))
                    dve.wait_ge(*at("gx", (r, n)))
                    dve.wait_ge(*at("xc", (r, n)))
                    dve.tensor_tensor(gx[:, n, :], gx[:, n, :], xc[:, n, :], ALU.mult).then_inc(*up("gated_in", (r, n)))
                for n in range(2):
                    dve.wait_ge(*at("decay", (r, n)))
                    chain(dve.tensor_tensor(hs[:, n, :], ga[:, n, :], ga[:, n, :], ALU.mult))
                    dve.scalar_tensor_tensor(gm[:, n, :], hs[:, n, :], 1.0, gm[:, n, :], ALU.add, ALU.mult)\
                       .then_inc(*up("one_less_a2", (r, n)))
                for n in range(2):
                    j = 2 * r + n
                    dve.wait_ge(*at("mult", (r, n)))
                    dve.wait_ge(*at("gated_in", (r, n)))
                    chain(dve.tensor_tensor(gm[:, n, :], gm[:, n, :], gx[:, n, :], ALU.mult))
                    chain(dve.tensor_tensor_scan(hs[:, n, :], ga[:, n, :], gm[:, n, :], 0.0, ALU.mult, ALU.add))
                    dve.wait_ge(*at("gelu", (r, n)))
                    dve.tensor_tensor(y[:, j, 0:L], hs[:, n, :], gy[:, n, :], ALU.mult).then_inc(*up("rec", (r, n)))
            p = first["mix1"] + 8
            dve.wait_ge(*at("rec", (3, 1)))
            for half in range(2):
                o = 64 * (1 - half)
                chain(dve.memset(qm[o:o + 64, half, :], 0.0))
            for t in range(4):
                dve.wait_ge(*at("out", (p + 2 + t // 2, t % 2)))
                dve.tensor_copy(kf[:, t, :], ps[:, 4 + t, :]).then_inc(*up("k", t))

            def one_head(u):
                if u >= 2:
                    dve.wait_ge(*at("scores", (u - 2, 3)))
                dve.wait_ge(*at("q", u // 2))
                o = 64 * (u % 2)
                dve.tensor_copy(qm[o:o + 64, u % 2, :], qf[o:o + 64, u // 2, :]).then_inc(*up("qm", u))

            def biased_max(u):
                dve.wait_ge(*at(f"bias{u % 2}", u))
                chain(dve.memset(bias[0:64, u % 2, 192:256], float(np.finfo(np.float32).min)))
                for i in range(4):
                    dve.wait_ge(*at("scores", (u, i)))
                    if u >= 2:
                        dve.wait_ge(*at("tr", (u - 2, 3)))
                    near = max(0, i - 1) * P
                    end = (i + 1) * P
                    b = 4 * (u % 2) + i
                    ins = dve.scalar_tensor_tensor(pr[:, u % 2, i, near:end], ps[:, b, near:end], SCALE,
                                                   bias[:, u % 2, 2 * P - (end - near):2 * P], ALU.mult, ALU.add)
                    if near:
                        chain(ins)
                        ins = dve.tensor_scalar(pr[:, u % 2, i, 0:near], ps[:, b, 0:near], SCALE, pcol("rb_far", u),
                                                ALU.mult, ALU.add)
                    ins.then_inc(*up("biased", (u, i)))
                    dve.wait_ge(*at("biased", (u, i)))
                    dve.tensor_reduce(small[:, 32 + 4 * (u % 2) + i:33 + 4 * (u % 2) + i], pr[:, u % 2, i, 0:end],
                                      AX.X, ALU.max, negate=True).then_inc(*up("max", (u, i)))

            def normalise(u):
                s = slice(40 + 4 * (u % 2), 44 + 4 * (u % 2))
                dve.wait_ge(*at("exp", (u, 3)))
                chain(dve.reciprocal(small[:, s], small[:, s]))
                for i in range(4):
                    a = pr[:, u % 2, i, 0:(i + 1) * P]
                    dve.tensor_scalar(a, a, small[:, s.start + i:s.start + i + 1], None, ALU.mult).then_inc(*up("probs", (u, i)))

            def keep(u):
                o, t = 64 * (u % 2), u // 2
                dve.wait_ge(*at("pv", u))
                src = ps[o:o + 64, 4 * (u % 2), :].rearrange("p (a n) -> p a n", a=2)
                hi, lo = hhi[o:o + 64, 2 * t:2 * t + 2, L:TT], hlo[o:o + 64, 2 * t:2 * t + 2, L:TT]
                chain(dve.tensor_copy(hi, src))
                dve.tensor_tensor(lo, src, hi.bitcast(F32), ALU.subtract).then_inc(*up("att", u))

            for u in range(2):
                one_head(u)
                biased_max(u)
            normalise(0)
            normalise(1)
            for u in range(HEADS):
                if u + 2 < HEADS:
                    one_head(u + 2)
                keep(u)
                if u + 2 < HEADS:
                    biased_max(u + 2)
                    normalise(u + 2)
            for k in range(KD):
                dve.wait_ge(*at("bhi", ("rec", k)))
                dve.tensor_tensor(blo[:, k, :], y[:, k, 0:L], bhi[:, k, :].bitcast(F32), ALU.subtract).then_inc(*up("blo", ("rec", k)))
            for j in range(2):
                p = first["mix1"] + 14 + 7 * j
                for t in range(4):
                    dve.wait_ge(*at("out", (p + 2, t)))
                    dve.wait_ge(*at("gate", (j, "a", t)))
                    dve.wait_ge(*at("blo", ("rec", 4 * j + t)))
                    dve.tensor_tensor(y[:, 4 * j + t, 0:L], ps[:, 4 + t, :], gate[:, t, :], ALU.mult).then_inc(*up("merged", (j, "a", t)))
                for t in range(4):
                    dve.wait_ge(*at("out", (p + 5 + t // 2, t % 2)))
                    dve.wait_ge(*at("gate", (j, "r", t)))
                    dve.tensor_tensor(gate[:, t, :], ps[:, 4 + t, :], gate[:, t, :], ALU.mult).then_inc(*up("rgated", (j, t)))
                    dve.wait_ge(*at("rgated", (j, t)))
                    dve.tensor_tensor(y[:, 4 * j + t, 0:L], y[:, 4 * j + t, 0:L], gate[:, t, :], ALU.add).then_inc(*up("merged", (j, "r", t)))
            for k in range(KD):
                dve.wait_ge(*at("bhi", ("out", k)))
                dve.tensor_tensor(blo[:, k, :], y[:, k, 0:L], bhi[:, k, :].bitcast(F32), ALU.subtract).then_inc(*up("blo", ("out", k)))

        def mix2(st):
            X = lambda *k: (st,) + k
            l, T, p0 = LAYER[st], TOKENS[st], first[st]
            lam_init = 0.8 - 0.6 * math.exp(-0.3 * l)
            swap = [(i + 16) % 32 for i in range(32)]

            def turn(tag, t, src, dst, scratch, rope_event):
                dve.wait_ge(*at(rope_event, st))
                chain(dve.stream_shuffle(scratch, src, swap))
                chain(dve.tensor_tensor(scratch, scratch, rope[:, 1, :], ALU.mult))
                chain(dve.tensor_tensor(dst, src, rope[:, 0, :], ALU.mult))
                dve.tensor_tensor(dst, dst, scratch, ALU.add).then_inc(*up("roped", X(tag, t)))

            def head_norm(tag, T, size, src, gain, dst, bank, out_event, before):
                if before:
                    dve.wait_ge(*at(out_event, X(before)))
                dve.wait_ge(*at("hsum", X(tag)))
                dve.tensor_scalar(rstd[:, 0:T], wide(bank, T), 1.0 / size, EPS, ALU.mult, ALU.add)\
                   .then_inc(*up("hms", X(tag)))
                dve.wait_ge(*at("hroot", X(tag)))
                chain(dve.reciprocal(rstd[:, 0:T], rstd[:, 0:T]))
                dve.scalar_tensor_tensor(dst, src, gain, rstd[:, 0:T], ALU.mult, ALU.mult).then_inc(*up(out_event, X(tag)))

            def keep_lo(tag, nt, dst, hi, src):
                for k in range(nt):
                    dve.wait_ge(*at("c_hi", X(tag, k)))
                    dve.tensor_tensor(dst[:, k, 0:T], src(k), hi[:, k, 0:T].bitcast(F32), ALU.subtract)\
                       .then_inc(*up("c_lo", X(tag, k)))

            def merge(tag, j, p):
                for t in range(4):
                    k = 4 * j + t
                    dve.wait_ge(*at("out", (p + 3 * j, t)))
                    dve.wait_ge(*at("gate", X(tag, j, t)))
                    b = 4 + 2 * (t % 2)
                    if tag == BRANCHES[0]:
                        if k == 0:
                            dve.wait_ge(*at("pv", X("d", LAST_UNIT[st, "d"])))
                        dve.tensor_tensor(y[:, k, 0:T], wide(b, T), gate2[:, t, 0:T], ALU.mult).then_inc(*up("gated", X(tag, j, t)))
                    else:
                        dve.tensor_tensor(gate2[:, t, 0:T], wide(b, T), gate2[:, t, 0:T], ALU.mult).then_inc(*up("bank_read", X(tag, j, t)))
                        dve.wait_ge(*at("bank_read", X(tag, j, t)))
                        dve.tensor_tensor(y[:, k, 0:T], y[:, k, 0:T], gate2[:, t, 0:T], ALU.add).then_inc(*up("gated", X(tag, j, t)))

            def masked_query(rows, uno):
                u = rows.unit(uno)
                t, half, g = u
                a, b = GROUPS[g]
                for j in ((0, 1) if half is None else (half,)):
                    prev = rows.last_row_with(uno, j)
                    if prev is not None:
                        dve.wait_ge(*at("scores", X(rows.tag, prev, j)))
                    dve.wait_ge(*at(*rows.query_event(X, t, g)))
                    o = slice(64 * j, 64 * j + 64)
                    ins = dve.tensor_copy(qm2[o, j, 0:b - a], aq[o, t, a:b])
                    if half is None and j == 0:
                        chain(ins)
                ins.then_inc(*up("qm", X(rows.tag, uno)))

            def row_max(rows, r):
                u, i, js, k0, k1 = rows[r]
                for j in js:
                    c = ROW_COL(r, j)
                    dve.wait_ge(*at("scores", X(rows.tag, r, j)))
                    if r >= 2:
                        dve.wait_ge(*at("exp", X(rows.tag, r - 2, rows[r - 2][2][-1])))
                    b = rows.bank(r, j)
                    s = ps[:, b:b + 2, :].rearrange("p a n -> p (a n)")[:, k0:k1] if k0 == 0 else ps[:, b, 0:k1 - k0]
                    chain(dve.tensor_reduce(small[:, c:c + 1], s, AX.X, ALU.max, negate=True))
                    dve.tensor_scalar(small[:, c:c + 1], small[:, c:c + 1], SCALE, None, ALU.mult)\
                       .then_inc(*up("nmax", X(rows.tag, r, j)))

            def row_probs(rows, r):
                u, i, js, k0, k1 = rows[r]
                n = k1 - k0
                c = ROW_COL(r, js[0]) + 4
                dve.wait_ge(*at("exp", X(rows.tag, r, js[-1])))
                chain(dve.reciprocal(small[:, c:c + len(js)], small[:, c:c + len(js)]))
                if len(js) == 2:
                    chain(dve.tensor_scalar(pr2[:, r % 2, 1, 0:n], pr2[:, r % 2, 1, 0:n], small[:, c + 1:c + 2],
                                            small[:, 48:49], ALU.mult, ALU.mult))
                    dve.scalar_tensor_tensor(pr2[:, r % 2, 0, 0:n], pr2[:, r % 2, 0, 0:n], small[:, c:c + 1],
                                             pr2[:, r % 2, 1, 0:n], ALU.mult, ALU.add).then_inc(*up("probs", X(rows.tag, r)))
                else:
                    dve.tensor_scalar(pr2[:, r % 2, 0, 0:n], pr2[:, r % 2, 0, 0:n], small[:, c:c + 1], None, ALU.mult)\
                       .then_inc(*up("probs", X(rows.tag, r)))

            def attention(rows):
                for half in range(2):
                    o = 64 * (1 - half)
                    chain(dve.memset(qm2[o:o + 64, half, :], 0.0))
                masked_query(rows, 0)
                for r in range(rows.ahead):
                    row_max(rows, r)
                for r in range(len(rows)):
                    if r + rows.ahead < len(rows) and rows.unit_start(r + rows.ahead):
                        masked_query(rows, rows.unit_no(r + rows.ahead))
                    row_probs(rows, r)
                    if r + rows.ahead < len(rows):
                        row_max(rows, r + rows.ahead)

            dve.wait_ge(*at("lv", st))
            v = pr2[:, 0, 0, 0:256].rearrange("p (a b d) -> p a b d", a=2, b=2)
            chain(dve.tensor_tensor(v[:, :, 0, :], v[:, :, 0, :], v[:, :, 1, :], ALU.mult))
            dve.tensor_reduce(small[:, 64:66], v[:, :, 0, :], AX.X, ALU.add).then_inc(*up("lv_sums", st))
            dve.wait_ge(*at("lv_exp", st))
            chain(dve.tensor_tensor(small[:, 48:49], small[:, 67:68], small[:, 66:67], ALU.subtract))
            chain(dve.tensor_scalar(small[:, 48:49], small[:, 48:49], -lam_init, None, ALU.add))
            chain(dve.tensor_scalar(small[:, 49:50], pcol("subln", l), 1.0 - lam_init, None, ALU.mult))
            for t in range(4):
                dve.wait_ge(*at("out", (p0 + t // 2, t % 2)))
                turn("dk", t, ps[:, 2 * t % 4, :], dk[:, t, 0:L], pr2[:, 1, t % 2, 0:L], "rope")
            for t in range(4):
                dve.wait_ge(*at("out", (p0 + 4 + t // 2, t % 2)))
                turn("dq", t, ps[:, 2 * t % 4, :], aq[:, t, 0:L], pr2[:, 1, t % 2, 0:L], "rope")
            for t in range(4):
                dve.wait_ge(*at("roped", X("dq", t)))
            attention(ROWS(st, "d"))
            for t in range(4):
                head_norm(("sub", t), T, P, aq[:, t, 0:T], small[:, 49:50], aq[:, t, 0:T], 2 * (t % 2), "subbed",
                          ("sub", t - 1) if t else None)
                C.name("ready", X("d", t), *C.labels[("subbed", X(("sub", t)))])
            keep_lo("d", 4, cl, ch, lambda k: aq[:, k, 0:T])
            merge("d", 0, p0 + 8)
            merge("d", 1, p0 + 8)
            pg = p0 + 12

            def normed_and_turned(tag, t, bank, sum_bank, T, gain, dst):
                dve.wait_ge(*at("out", (pg if tag == "gk" else pg + 1 + t // 2, t % 2 if tag == "gq" else 0)))
                before = {("gk", 0): None, ("gq", 0): ("gk", 0)}.get((tag, t), ("gq", t - 1))
                head_norm((tag, t), T, 64, wide(bank, T), gain, dst, sum_bank, "hnormed", before)
                dve.wait_ge(*at("hnormed", X((tag, t))))
                turn(tag, t, dst[:, 0:L], dst[:, 0:L], pr2[:, 1, t % 2, 0:L], "rope2")

            normed_and_turned("gk", 0, 0, 6, TT, pcol("k_norm", l), gk[:, 0, :])
            for t in range(4):
                normed_and_turned("gq", t, GQ_BANK[t], 6, T, pcol("q_norm", l), aq[:, t, 0:T])
            for t in range(4):
                dve.wait_ge(*at("roped", X("gq", t)))
            attention(ROWS(st, "g"))
            keep_lo("g", 4, cl, ch, lambda k: aq[:, k, 0:T])
            merge("g", 0, pg + 5)
            merge("g", 1, pg + 5)
            pc = pg + 9
            segs = [(a, b, a + 15 + 30 * g) for g, (a, b) in groups(T)]

            def conv_input(n):
                dve.wait_ge(*at("sg", X(n)))
                for g, (a, b, s) in enumerate(segs):
                    ins = dve.tensor_tensor(vp[:, n, s:s + b - a], ps[:, 4 * (n % 2) + g, 0:b - a], sg_tile[n][:, a:b], ALU.mult)
                    if g + 1 < len(segs):
                        chain(ins)
                ins.then_inc(*up("vp", X(n)))

            def taps(n, t0, t1):
                for t in range(t0, t1):
                    if t == 0:
                        dve.wait_ge(*at("vp", X(n)))
                        if n >= 1:
                            dve.wait_ge(*at("conv_kept", X(n - 1)))
                    else:
                        dve.wait_ge(*at("tap", X(n, t - 1)))
                    w = pcol("conv_dw", 93 * l + 3 * t + n)
                    for g, (a, b, s) in enumerate(segs):
                        tap = vp[:, n, s - 15 + t:s - 15 + t + b - a]
                        if t == 0:
                            ins = dve.tensor_scalar(cv[:, a:b], tap, w, pcol("conv_dw_b", 3 * l + n), ALU.mult, ALU.add)
                        else:
                            ins = dve.scalar_tensor_tensor(cv[:, a:b], tap, w, cv[:, a:b], ALU.mult, ALU.add)
                        if g + 1 < len(segs):
                            ins.then_inc(*up("tap"))
                    ins.then_inc(*up(*(("tap", X(n, t)) if t < 30 else ("conv", X(n)))))

            dve.wait_ge(*at("gated", X("g", 1, 3)))
            for n in range(3):
                chain(dve.memset(vp[:, n, :], 0.0))
            conv_input(0)
            taps(0, 0, 14)
            conv_input(1)
            taps(0, 14, 28)
            conv_input(2)
            taps(0, 28, 31)
            taps(1, 0, 4)
            pf = pc + 3
            for g, (a, b) in groups(T):
                for t in range(a // P, b // P):
                    dve.wait_ge(*at("fh", X(t)))
                    dve.tensor_tensor(fl[:, t % 2, :], wide(2 * (t % 2), TT), fh[:, t % 2, :].bitcast(F32), ALU.subtract)\
                       .then_inc(*up("fl", X(t)))
                    taps(1, 4 + 27 * t // (T // P), 4 + 27 * (t + 1) // (T // P))
                for f in range(3):
                    dve.wait_ge(*at("yf_hi", X(g, f)))
                    dve.tensor_tensor(cl[:, f, a:b], ps[:, 4 + f, 0:b - a], ch[:, f, a:b].bitcast(F32), ALU.subtract)\
                       .then_inc(*up("yf_lo", X(g, f)))
            for f in range(3):
                C.name("c_lo", X("f", f), *C.labels[("yf_lo", X(groups(T)[-1][0], f))])
            pm = pf + 2 + len(DFT_PANELS[l])
            taps(2, 0, 31)
            dve.wait_ge(*at("mean_sum", X(2)))
            chain(dve.tensor_scalar(cv[:, 0:T], wide(0, T), 1.0 / 384, None, ALU.mult))
            for n in range(3):
                dve.tensor_tensor(vp[:, n, 0:T], vp[:, n, 0:T], cv[:, 0:T], ALU.subtract).then_inc(*up("centred", X(n)))
            merge("f", 0, pm + 2)
            dve.wait_ge(*at("var_sum", X(2)))
            dve.tensor_scalar(rstd[:, 0:T], wide(2, T), 1.0 / 384, EPS, ALU.mult, ALU.add).then_inc(*up("cvar", X()))
            dve.wait_ge(*at("croot", X()))
            chain(dve.reciprocal(rstd[:, 0:T], rstd[:, 0:T]))
            for n in range(3):
                dve.tensor_tensor(vp[:, n, 0:T], vp[:, n, 0:T], rstd[:, 0:T], ALU.mult).then_inc(*up("cnormed", X(n)))
            merge("f", 1, pm + 2)
            keep_lo("c", 3, cl, ch, lambda k: vp[:, k, 0:T])
            merge("c", 0, pm + 8)
            merge("c", 1, pm + 8)
            dve.wait_ge(*at("gated", X("c", 1, 3)))
            for k in range(KD):
                dve.wait_ge(*at("c_hi", X("out", k)))
                dve.tensor_tensor(ml[:, k, 0:T], y[:, k, 0:T], mh[:, k, 0:T].bitcast(F32), ALU.subtract)\
                   .then_inc(*up("c_lo", X("out", k)))

        def mix_dve(st):
            if st == "mix1":
                mix1()
            else:
                mix2(st)

        for st in ORDER:
            if st in NORMS:
                norm(st)
            elif st in MLPS:
                mlp(MLPS[st])
            else:
                mix_dve(st)

    @block.tensor
    def _(pe):
        def tri(out, a, b, first, last):
            pe.matmul(out, a[0], b[0], start=first, stop=False)
            pe.matmul(out, a[0], b[1], start=False, stop=False)
            return pe.matmul(out, a[1], b[0], start=False, stop=last)

        def wtile(p, kt, cw, k, c0, n=P):
            s = k * cw + c0
            return whi[:, p % 2, s:s + n], wlo[:, p % 2, s:s + n]

        def mod(k, i=None, by=0):
            pe.wait_ge(mod_read, lin(k + 1, by, i))
            for n in range(2):
                for c in range(1 if k < NM1 else 2):
                    ins = pe.matmul(ps[:, 7, bass.ds(lin(4 * k + 2 * n + c, 4 * by, i), 1)],
                                    macc[:, k % 4, c, n * P:(n + 1) * P], ones[:, 0:1], start=True, stop=True)
            ins.then_inc(mod_used, 1)

        def sums(st, what, T):
            for k in range(KD):
                pe.wait_ge(*at("sq", (st, what, k)))
                for h, (a, b) in enumerate(spans(T)):
                    ins = pe.matmul(ps[:, SUM_BANK[what] + h, 0:b - a], ones[:, :], sq[:, k % 2, a:b],
                                    start=(k == 0), stop=(k == KD - 1))
                ins.then_inc(*up("sq_used", (st, what, k)))

        def norm(st):
            post, pre = NORMS[st]
            if post:
                sums(st, "post", post[0])
            if pre and post:
                sums(st, "pre", pre[0])

        def mlp(m):
            st, T, H, O = m.name, m.T, m.H, m.O
            for kind in ("up_first", "down"):
                C.start(kind, st)
            pre = ORDER[ORDER.index(st) - 1]

            def up_product(p, n, h, k):
                mv = slice(*spans(T)[0 if m.gated else h])
                return tri(ps[:, 2 * n + h, 0:mv.stop - mv.start],
                           wtile(p + n if m.gated else p, KD, CW, k, h * P if m.gated else n * P),
                           (hhi[:, k, mv], hlo[:, k, mv]), k == 0, k == KD - 1)

            def first_ups():
                pe.wait_ge(lo_ready, m.p0 + m.UP)
                for k in range(KD):
                    pe.wait_ge(*at("h_lo", (pre, k)))
                    for n in range(2):
                        for h in range(2 if m.gated else H):
                            ins = up_product(m.p0, n, h, k)
                        if k == KD - 1:
                            if m.gated or n == 1:
                                ins.then_inc(panel_used, 1)
                            else:
                                ins.then_inc(*up("up_first"))

            def ups(c, p, i=None):
                for n in range(2):
                    pn = p + n if m.gated else p
                    if m.gated or n == 0:
                        pe.wait_ge(lo_ready, lin(pn + 1, m.per_trip, i))
                    pe.wait_ge(*at("hid", ("start", st), lin(2 * (c - 1) + n + 1, 4, i)))
                    for h in range(2 if m.gated else H):
                        for k in range(KD):
                            ins = up_product(p, n, h, k)
                    if m.gated or n == 1:
                        ins.then_inc(panel_used, 1)
                    else:
                        ins.then_inc(*up("up_first"))

            def down(c, p, i=None):
                pe.wait_ge(lo_ready, lin(p + 1, m.per_trip, i))
                pe.wait_ge(*at("hid_lo", ("start", st), lin(2 * c + 2, 4, i)))
                for o in range(O):
                    j, h = o // H, o % H
                    prior = O * (c + 1) + o - 3 if o >= 3 else O * c + max(q for q in range(O) if q % 3 == o)
                    pe.wait_ge(*at("added", ("start", st), lin(prior + 1, 2 * O, i)))
                    for k in range(2):
                        mv = slice(*spans(T)[h])
                        ins = tri(ps[:, 4 + o % 3, 0:mv.stop - mv.start], wtile(p, 2, D, k, j * P),
                                  (dhi[:, c % 2, k, mv], dlo[:, c % 2, k, mv]), k == 0, k == 1)
                    if o < O - 1:
                        ins.then_inc(*up("down"))
                ins.then_inc(panel_used, 1)

            first_ups()
            k = m.mod0
            for v in range(m.before):
                mod(k + v)
            k += m.before
            with C.loop(pe, m.trips) as i:
                for u in range(2):
                    p = m.p0 + m.UP + u * (m.UP + 1)
                    ups(1 + u, p, i)
                    for v in range(m.half):
                        mod(k + u * m.half + v, i, 2 * m.half)
                    down(u, p + m.UP, i)
            for c in m.rest:
                p = m.p0 + m.UP + (c - 1) * (m.UP + 1)
                ups(c, p)
                down(c - 1, p + m.UP)
            down(m.C - 1, m.p0 + (m.UP + 1) * m.C - 1)

        pe.wait_ge(*at("ones", "all"))
        sums("n0", "pre", L)
        for k in range(8):
            mod(k)

        free = {}

        def claim(banks, event):
            for b in banks:
                if b in free:
                    pe.wait_ge(*at(*free[b]))
                free[b] = event

        def ended(ins, p, n, last):
            if last:
                ins.then_inc(panel_used, 1)
                C.name("out", (p, n), "panel_used", p + 1)
            else:
                ins.then_inc(*up("out", (p, n)))

        def project(p, kt, cw, src, T, banks, events, ready=None, whole=True):
            pe.wait_ge(lo_ready, p + 1)
            if ready and len(set(banks)) == len(banks):
                for n, bank in enumerate(banks):
                    claim(range(bank, bank + len(spans(T))), events[n])
                for k in range(kt):
                    pe.wait_ge(*at(*ready(k)))
                    for n, bank in enumerate(banks):
                        for h, (a, b) in enumerate(spans(T)):
                            ins = tri(ps[:, bank + h, 0:b - a], wtile(p, kt, cw, k, n * P), src(k, a, b), k == 0, k == kt - 1)
                        if k == kt - 1:
                            ended(ins, p, n, whole and n == len(banks) - 1)
                return
            for n in range(cw // P):
                if n >= len(banks):
                    break
                claim(range(banks[n], banks[n] + len(spans(T))), events[n])
                for h, (a, b) in enumerate(spans(T)):
                    for k in range(kt):
                        if ready and n == 0 and h == 0:
                            pe.wait_ge(*at(*ready(k)))
                        hi, lo = src(k, a, b)
                        ins = tri(ps[:, banks[n] + h, 0:b - a], wtile(p, kt, cw, k, n * P), (hi, lo), k == 0, k == kt - 1)
                ended(ins, p, n, whole and n == len(banks) - 1)

        def by_token(p, cw, c0, c1, T, banks, events, n0=0):
            pe.wait_ge(lo_ready, p + 1)
            for t in range(T // P):
                claim([banks[t]], events[t])
                for k in range(KD):
                    a = (hhi[:, k, t * P:(t + 1) * P], hlo[:, k, t * P:(t + 1) * P])
                    b = wtile(p, KD, cw, k, c0, c1 - c0)
                    ins = tri(ps[:, banks[t], 0:c1 - c0], a, b, k == 0, k == KD - 1)
                ended(ins, p, n0 + t, t == T // P - 1)

        def from_h(k, a, b):
            return hhi[:, k, a:b], hlo[:, k, a:b]

        def mix1():
            p0 = first["mix1"]
            free.clear()
            for r in range(4):
                p = p0 + 2 * r
                project(p, KD, CW, from_h, L, (0, 1), [("xcopy", (r, n)) for n in range(2)],
                        (lambda k: ("h_lo", ("n1", k))) if r == 0 else None)
                project(p + 1, KD, CW, from_h, L, (2, 3), [("gelu", (r, n)) for n in range(2)])
                if r == 0:
                    pe.wait_ge(*at("wbd", "all"))
                for n in range(2):
                    pe.wait_ge(*at("xc", (r, n)))
                    claim([4 + n], ("ga", (r, n)))
                    claim([6 + n], ("gx", (r, n)))
                    pe.matmul(ps[:, 4 + n, :], wbd[:, 0, 2 * r + n, :], xc[:, n, :], start=True, stop=True)
                    pe.matmul(ps[:, 6 + n, :], wbd[:, 1, 2 * r + n, :], xc[:, n, :], start=True, stop=True)\
                      .then_inc(*up("gates", (r, n)))
            p = p0 + 8
            for a in range(2):
                project(p + a, KD, CW, from_h, L, (2 * a, 2 * a + 1), [("q", 2 * a + n) for n in range(2)])
            for a in range(2):
                project(p + 2 + a, KD, CW, from_h, L, (4 + 2 * a, 5 + 2 * a), [("k", 2 * a + n) for n in range(2)])
            for a in range(2):
                by_token(p + 4 + a, CW, 0, CW, L, [4 * a + t for t in range(4)], [("v", (a, t)) for t in range(4)])

            def scores(u):
                pe.wait_ge(*at("qm", u))
                pe.wait_ge(*at("k", u // 2))
                for i in range(4):
                    b = 4 * (u % 2) + i
                    claim([b], ("biased", (u, i)))
                    pe.matmul(ps[:, b, 0:(i + 1) * P], qm[:, u % 2, i * P:(i + 1) * P], kf[:, u // 2, 0:(i + 1) * P],
                              start=True, stop=True).then_inc(*up("scores", (u, i)))

            def turn(u):
                pe.wait_ge(*at("probs", (u, 3)))
                for j in range(4):
                    b = 4 * (u % 2) + j
                    claim([b], ("pt", (u, j)))
                    for i in range(j, 4):
                        ins = pe.transpose(ps[:, b, i * P:(i + 1) * P], pr[:, u % 2, i, j * P:(j + 1) * P], const("ident"))
                    ins.then_inc(*up("tr", (u, j)))

            def weigh(u):
                b, t = 4 * (u % 2), u // 2
                claim([b], ("att", u))
                for j in range(4):
                    pe.wait_ge(*at("pt", (u, j)))
                    v = x[:, 2 * j + t // 2, L + (t % 2) * P:L + (t % 2 + 1) * P]
                    ins = pe.matmul(ps[:, b, j * P:L], v, pt[:, j, j * P:L], start=(j == 0), stop=(j == 3))
                ins.then_inc(*up("pv", u))

            scores(0)
            scores(1)
            for u in range(HEADS):
                turn(u)
                weigh(u)
                if u + 2 < HEADS:
                    scores(u + 2)

            def from_att(k, a, b):
                return hhi[:, 2 * k:2 * k + 2, L:TT], hlo[:, 2 * k:2 * k + 2, L:TT]

            def from_b(k, a, b):
                return bhi[:, k, a:b], blo[:, k, a:b]

            for j in range(2):
                p = p0 + 14 + 7 * j
                for a in range(2):
                    project(p + a, KD, CW, from_h, L, (2 * a, 2 * a + 1), [("gate", (j, "a", 2 * a + n)) for n in range(2)])
                pe.wait_ge(*at("att", HEADS - 1))
                project(p + 2, 4, 512, from_att, L, (4, 5, 6, 7), [("merged", (j, "a", t)) for t in range(4)])
                for a in range(2):
                    project(p + 3 + a, KD, CW, from_h, L, (2 * a, 2 * a + 1), [("gate", (j, "r", 2 * a + n)) for n in range(2)])
                for a in range(2):
                    project(p + 5 + a, KD, CW, from_b, L, (4 + 2 * a, 5 + 2 * a), [("rgated", (j, 2 * a + n)) for n in range(2)],
                            (lambda k: ("blo", ("rec", k))) if j == 0 and a == 0 else None)
            p = p0 + 28
            for a in range(4):
                b = 2 * (a % 2)
                project(p + a, KD, CW, from_b, L, (b, b + 1), [("src", ("n2", "post", 2 * a + n)) for n in range(2)],
                        (lambda k: ("blo", ("out", k))) if a == 0 else None)

        def mix2(st):
            X = lambda *k: (st,) + k
            l, T, p = LAYER[st], TOKENS[st], first[st]
            norm_before = "n3" if l == 0 else "n5"
            free.clear()

            def from_c(k, a, b):
                return ch[:, k, a:b], cl[:, k, a:b]

            def gates(tag, j, p):
                for a in range(2):
                    project(p + a, KD, CW, from_h, T, (0, 2), [("gate", X(tag, j, 2 * a + n)) for n in range(2)])
                return p + 2

            def branch(tag, kt, j, p):
                kind = "gated" if tag == BRANCHES[0] else "bank_read"
                project(p, kt, 512, from_c, T, (4, 6, 4, 6), [(kind, X(tag, j, t)) for t in range(4)],
                        (lambda k: ("c_lo", X(tag, k))) if j == 0 else None)
                return p + 1

            def merge(tag, kt, p):
                for j in range(2):
                    p = branch(tag, kt, j, gates(tag, j, p))
                return p

            def head_sum(tag, T, bank, weights):
                pe.wait_ge(*at("hsq", X(tag)))
                claim(range(bank, bank + len(spans(T))), ("hms", X(tag)))
                for h, (a, b) in enumerate(spans(T)):
                    ins = pe.matmul(ps[:, bank + h, 0:b - a], weights, pr2[:, 0, 0, a:b], start=True, stop=True)
                ins.then_inc(*up("hsum", X(tag)))

            def row_scores(rows, r, keys):
                u, i, js, k0, k1 = rows[r]
                if rows.unit_start(r):
                    pe.wait_ge(*at("qm", X(rows.tag, rows.unit_no(r))))
                for j in js:
                    b = rows.bank(r, j)
                    claim([b, b + 1] if k1 - k0 > L else [b], ("exp", X(rows.tag, r, j)))
                    q = qm2[:, j, (i % 4) * P:(i % 4 + 1) * P]
                    if k0 == 0:
                        pe.matmul(ps[:, b, :], q, keys(u)[:, 0:L], start=True, stop=True)
                        ins = pe.matmul(ps[:, b + 1, 0:LC], q, keys(u)[:, L:TT], start=True, stop=True)
                    else:
                        ins = pe.matmul(ps[:, b, 0:LC], q, keys(u)[:, L:TT], start=True, stop=True)
                    ins.then_inc(*up("scores", X(rows.tag, r, j)))

            def weigh(rows, r, values):
                u, i, js, k0, k1 = rows[r]
                uno, (a, b), n = rows.unit_no(r), GROUPS[u[2]], (k1 - k0) // P
                pe.wait_ge(*at("pt", X(rows.tag, r)))
                claim([6 + uno % 2], ("kept", X(rows.tag, uno)))
                for k in range(n):
                    ins = pe.matmul(ps[:, 6 + uno % 2, 0:b - a], values(u, k0 // P + k), pt2[:, k, 0:b - a],
                                    start=(k == 0), stop=(k == n - 1))
                ins.then_inc(*up("pv", X(rows.tag, uno)))

            def attention(rows, keys, values):
                for r in range(rows.ahead):
                    row_scores(rows, r, keys)
                for r in range(len(rows)):
                    if r + rows.ahead < len(rows):
                        row_scores(rows, r + rows.ahead, keys)
                    if r >= 1 and rows.unit_end(r - 1):
                        weigh(rows, r - 1, values)
                    u, i, js, k0, k1 = rows[r]
                    pe.wait_ge(*at("probs", X(rows.tag, r)))
                    claim([4, 5], ("pt", X(rows.tag, r)))
                    for k in range((k1 - k0) // P):
                        ins = pe.transpose(ps[:, 4 + k // 4, (k % 4) * P:(k % 4 + 1) * P],
                                           pr2[:, r % 2, 0, k * P:(k + 1) * P], const("ident"))
                    ins.then_inc(*up("tr", X(rows.tag, r)))
                weigh(rows, len(rows) - 1, values)

            for a in range(2):
                project(p + a, KD, CW, from_h, TT, (0, 2), [("ctx_kept", X("dk", 2 * a + n)) for n in range(2)],
                        (lambda k: ("h_lo", (norm_before, k))) if a == 0 else None)
            for a in range(2):
                by_token(p + 2 + a, CW, 0, CW, TT, DV_BANK, [("dv", X(a, t)) for t in range(6)])
            for a in range(2):
                kind = "ctx_kept" if T > L else "roped"
                project(p + 4 + a, KD, CW, from_h, T, (0, 2), [(kind, X("dq", 2 * a + n)) for n in range(2)])
            pe.wait_ge(*at("ctx_kept", X("dk", 3)))
            pe.wait_ge(*at("roped", X("dk", 3)))
            pe.wait_ge(*at("dv", X(1, 5)))
            attention(ROWS(st, "d"), lambda u: dk[:, u[0], :], lambda u, k: dv[:, k, u[0] * P:(u[0] + 1) * P])
            for t in range(4):
                head_sum(("sub", t), T, 2 * (t % 2), ones[:, :])
            p = merge("d", 4, p + 6)
            project(p, KD, CW, from_h, TT, (0,), [("hnormed", X(("gk", 0)))], whole=False)
            by_token(p, CW, P, CW, TT, GV_BANK, [("gv", X(t)) for t in range(6)], n0=1)
            head_sum(("gk", 0), TT, 6, const("block"))
            for a in range(2):
                project(p + 1 + a, KD, CW, from_h, T, tuple(GQ_BANK[2 * a:2 * a + 2]),
                        [("hnormed", X(("gq", 2 * a + n))) for n in range(2)])
                for n in range(2):
                    head_sum(("gq", 2 * a + n), T, 6, const("block"))
            pe.wait_ge(*at("roped", X("gk", 0)))
            pe.wait_ge(*at("gv", X(5)))
            attention(ROWS(st, "g"), lambda u: gk[:, 0, :], lambda u, k: gv[:, k, :])
            p = merge("g", 4, p + 3)
            for n in range(3):
                b = 4 * (n % 2)
                project(p, KD, CW, from_h, T, (b, b + 2), [("vp", X(n)), ("sg", X(n))])
                p += 1

            def layer_sums(event, bank, ready, src, reader):
                claim(range(bank, bank + len(spans(T))), reader)
                for n in range(3):
                    pe.wait_ge(*at(ready, X(n)))
                    for h, (a, b) in enumerate(spans(T)):
                        ins = pe.matmul(ps[:, bank + h, 0:b - a], ones[:, :], src(n, a, b), start=(n == 0), stop=(n == 2))
                    ins.then_inc(*up(event, X(n)))

            project(p, KD, CW, from_h, T, (0, 2), [("uf", X(n)) for n in range(2)])
            project(p + 1, KD, P, from_h, T, (0,), [("uf", X(2))])
            p += 2
            pe.wait_ge(*at("uf", X(2)))

            def over_group(t):
                b = 2 * (t % 2)
                claim([b, b + 1], ("fl", X(t)))
                for f in range(3):
                    ins = pe.matmul(ps[:, b + f // 2, (f % 2) * CW:(f % 2 + 1) * CW], uf_tile[f][:, t * P:(t + 1) * P],
                                    const("dft64"), start=True, stop=True)
                ins.then_inc(*up("grouped", X(t)))

            for g, (a, b) in groups(T):
                t0, t1, n = a // P, b // P, b - a
                over_group(t0)
                for t in range(t0, t1):
                    if t + 1 < t1:
                        over_group(t + 1)
                    if (t - t0) % 2 == 0:
                        pe.wait_ge(lo_ready, p + 1)
                    pe.wait_ge(*at("fl", X(t)))
                    for f in range(3):
                        if t == t0:
                            claim([4 + f], ("yf_lo", X(g, f)))
                        for part in range(2):
                            c = f * CW + part * P
                            ins = tri(ps[:, 4 + f, 0:n], (fh[:, t % 2, c:c + P], fl[:, t % 2, c:c + P]),
                                      wtile(p, 2, 2 * n, (t - t0) % 2, part * n, n), t == t0 and part == 0, t == t1 - 1 and part == 1)
                        if t == t1 - 1 and f < 2:
                            ins.then_inc(*up("mixed", X(g, f)))
                    if (t - t0) % 2 == 1:
                        ins.then_inc(panel_used, 1)
                        p += 1
                        C.name("slot_read", X(t), "panel_used", p)
                        if t == t1 - 1:
                            C.name("mixed", X(g, 2), "panel_used", p)
                    else:
                        ins.then_inc(*up("slot_read", X(t)))
            p = gates("f", 0, p)
            layer_sums("mean_sum", 0, "conv_kept", lambda n, a, b: vp[:, n, a:b], ("centred", X(2)))
            p = gates("f", 1, branch("f", 3, 0, p))
            layer_sums("var_sum", 2, "csq", lambda n, a, b: sg_tile[n][:, a:b], ("cvar", X()))
            p = branch("f", 3, 1, p)
            p = merge("c", 3, p)
            nxt = "n4" if l == 0 else "n6"
            for a in range(4):
                project(p + a, KD, CW, lambda k, a, b: (mh[:, k, a:b], ml[:, k, a:b]), T, (0, 2),
                        [("src", (nxt, "post", 2 * a + n)) for n in range(2)],
                        (lambda k: ("c_lo", X("out", k))) if a == 0 else None)

        def mix_pe(st):
            if st == "mix1":
                mix1()
            else:
                mix2(st)

        for st in ORDER:
            if st in NORMS:
                norm(st)
            elif st in MLPS:
                mlp(MLPS[st])
            else:
                mix_pe(st)


def down_panel(m, c):
    return m.p0 + m.UP * min(c + 2, m.C) + c


def lay_out(v):
    v = {k: np.asarray(a) for k, a in v.items()}
    first, panels = {}, []

    def stage(name, ps):
        first[name] = len(panels)
        panels.extend(ps)

    stage("ffn1", ffn_panels(v["ffn1_w_gu"][0], v["ffn1_w_down"][0]))
    w = v["w_in"][0]
    ps = []
    for r in range(4):
        ps += cols_panels(w, 1536 + r * CW, 1536 + (r + 1) * CW) + cols_panels(w, 2560 + r * CW, 2560 + (r + 1) * CW)
    ps += cols_panels(w, 0, 1536)
    for j in range(2):
        ps += cols_panels(w, 3584 + 512 * j, 4096 + 512 * j)
        ps += rows_panels(v["w_att_o"][0], 512 * j, 512 * (j + 1))
        ps += cols_panels(w, 4608 + 512 * j, 5120 + 512 * j)
        ps += cols_panels(v["w_rec_o"][0], 512 * j, 512 * (j + 1))
    stage("mix1", ps + cols_panels(v["w_out"][0], 0, D))

    stage("ffn2", ffn_panels(v["ffn2_w_gu"][0], v["ffn2_w_down"][0]))
    stage("mix2", mix2_panels(v, 0))

    stage("mlp1", mlp_panels(v["w_ff1_2"][0], v["w_ff2_2"][0]))
    stage("mix3", mix2_panels(v, 1))

    stage("mlp2", mlp_panels(v["w_ff1_2"][1], v["w_ff2_2"][1]))
    if len(panels) % 2:
        panels.append(np.zeros((P, PANEL), np.float32))

    mod_panels = []
    for w in (v["w_ada"][0], v["w_mod_2"][0], v["w_mod_2"][1]):
        mod_panels += cols_panels(w, 0, w.shape[1])

    par = {
        "b_ada": columns(v["b_ada"]), "b_mod": columns(v["b_mod_2"]), "norm_pre": columns(v["norm_pre"]),
        "norm_post": columns(v["norm_post"]), "conv_w": columns(v["conv_w"]), "conv_b": columns(v["conv_b"]),
        "lru_ba": columns(v["lru_ba"]), "lru_bx": columns(v["lru_bx"]), "lru_lambda": columns(v["lru_lambda"]),
        "g_pre_mix": columns(v["g_pre_mix_2"]), "g_post_mix": columns(v["g_post_mix_2"]),
        "g_pre_mlp": columns(v["g_pre_mlp_2"]), "g_post_mlp": columns(v["g_post_mlp_2"]),
        "q_norm": np.tile(v["q_norm_2"], (1, 2)).T, "k_norm": np.tile(v["k_norm_2"], (1, 2)).T,
        "subln": v["diff_subln_2"].T, "conv_dw": columns(v["conv_dw_2"]), "conv_dw_b": columns(v["conv_dw_bias_2"]),
        "ln_g": columns(v["conv_ln_g_2"]), "ln_b": columns(v["conv_ln_b_2"]),
        "rb_far": np.tile(v["rel_bias"][0][:, -1], (P, 1)),
        "cond": columns(np.concatenate([v["c"][0], v["c_2"][0], v["c_ctx_2"]])),
    }
    par = np.concatenate([par[n] for n, _ in PAR_SIZES], axis=1)

    half = np.kron(np.eye(2), np.ones((64, 64)))
    w64 = 2 * np.pi * np.outer(np.arange(64), np.arange(64)) / 64
    dft = np.concatenate([np.kron(np.eye(2), np.cos(w64)), np.kron(np.eye(2), np.sin(w64))], axis=1)
    cst = np.concatenate([np.eye(P), half, dft], axis=1)
    arrays = {
        "panels": np.stack(panels), "mod_panels": np.stack(mod_panels), "par": par, "cst": cst,
        "xT": v["x"][0].T,
        "wbd": np.stack([block_diagonal(v["lru_wa"][0]), block_diagonal(v["lru_wx"][0])], axis=1),
        "bias_band": v["rel_bias"][0][:, BAND],
        "ctxT": v["ctx_2"][0].T,
        "rope": rope_tables(),
        "lv": np.tile(v["diff_lambda_2"].reshape(1, 2, 256), (P, 1, 1)),

    }
    return {k: np.ascontiguousarray(a, dtype=np.float32) for k, a in arrays.items()}, first


def build(nc, shapes, first, stop=99, known=None):
    io = {k: nc.dram_tensor(k, shape, F32, kind="ExternalInput").ap() for k, shape in shapes.items()}
    io["outT"] = nc.dram_tensor("outT", (D, L), F32, kind="ExternalOutput").ap()
    with ExitStack() as ctx:
        C = Counts(nc, ctx, known)
        program(nc, ctx, io, C, first, shapes["panels"][0], stop)
    return C.labels


def kernel(**inputs):
    import concourse.bacc as bacc
    from concourse.bass_utils import run_bass_kernel_spmd

    arrays, first = lay_out(inputs)
    shapes = {k: a.shape for k, a in arrays.items()}
    counts = build(bacc.Bacc("TRN2", target_bir_lowering=False, num_devices=1), shapes, first)
    nc = bacc.Bacc("TRN2", target_bir_lowering=False, num_devices=1)
    build(nc, shapes, first, known=counts)
    r = run_bass_kernel_spmd(nc, [arrays], core_ids=[0])
    return np.ascontiguousarray(r.results[0]["outT"].T)[None]
```
